# Optimizing a Trainium2 kernel written in Bass

```python
import jax, jax.numpy as jnp
from jax import lax
import numpy as np

D_MODEL = 1024
BATCH = 1
SEQ = 2048
DEPTH = 1

D_MIX = D_MODEL
DN_HEADS = 6
DN_DK = 64
DN_DV = 64
DN_CONV = 4
DN_CHUNK = 64
CF_CH = 256
CF_KERNEL = 31
NSA_HEADS = 6
NSA_KV = 2
NSA_HPG = NSA_HEADS // NSA_KV
NSA_DH = 64
CMP_LEN = 32
CMP_STRIDE = 16
CMP_HID = 2 * NSA_DH
SEL_BLOCK = 64
N_SEL = 8
WINDOW = 512
Q_BLOCK = 64
D_FF = -(-8 * D_MODEL // (3 * 256)) * 256

EPS = 1e-6
NEG = -1e30
SEL_BIG = 1e4

DN_QKV = 2 * DN_HEADS * DN_DK + DN_HEADS * DN_DV
IN_SPLITS = (DN_QKV, DN_HEADS * DN_DV, DN_HEADS, DN_HEADS, 2 * CF_CH,
             NSA_HEADS * NSA_DH,
             NSA_KV * NSA_DH, NSA_KV * NSA_DH, NSA_KV * NSA_DH,
             NSA_KV * NSA_DH, NSA_KV * NSA_DH, NSA_KV * NSA_DH,
             3 * NSA_HEADS)
N_IN = DN_QKV + DN_HEADS * DN_DV + 2 * DN_HEADS + 2 * CF_CH + NSA_HEADS * NSA_DH + 6 * NSA_KV * NSA_DH + 3 * NSA_HEADS

kernel_name = "hybrid_deltanet_conformer_nsa_block"

def rms_norm(x, w):
    xf = x.astype(jnp.float32)
    y = xf * lax.rsqrt(jnp.mean(xf * xf, axis=-1, keepdims=True) + EPS)
    return (y * w.astype(jnp.float32)).astype(x.dtype)

def layer_norm(x, w, b):
    xf = x.astype(jnp.float32)
    mu = jnp.mean(xf, axis=-1, keepdims=True)
    var = jnp.mean(jnp.square(xf - mu), axis=-1, keepdims=True)
    y = (xf - mu) * lax.rsqrt(var + EPS) * w.astype(jnp.float32) + b.astype(jnp.float32)
    return y.astype(x.dtype)

def l2norm(t):
    return t * lax.rsqrt(jnp.sum(t * t, axis=-1, keepdims=True) + EPS)

def masked_softmax(s, mask):
    return jax.nn.softmax(jnp.where(mask, s.astype(jnp.float32), NEG), axis=-1)

def split_cols(t, sizes):
    out, start = [], 0
    for s in sizes:
        out.append(t[..., start:start + s])
        start += s
    return out

def causal_depthwise_conv(x, w):
    k, c = w.shape
    return lax.conv_general_dilated(
        x, w[:, None, :].astype(x.dtype), window_strides=(1,), padding=[(k - 1, 0)],
        dimension_numbers=("NWC", "WIO", "NWC"), feature_group_count=c)

def chunked_gated_delta(q, k, v, g, beta):
    bsz, nh, s, dk = q.shape
    dv = v.shape[-1]
    c = DN_CHUNK
    n = s // c
    f32 = jnp.float32
    q = q.reshape(bsz, nh, n, c, dk)
    k = k.reshape(bsz, nh, n, c, dk)
    v = v.reshape(bsz, nh, n, c, dv)
    g = g.reshape(bsz, nh, n, c)
    beta = beta.reshape(bsz, nh, n, c)
    gam = jnp.cumsum(g, axis=-1)
    idx = jnp.arange(c)
    causal = idx[:, None] >= idx[None, :]
    strict = idx[:, None] > idx[None, :]
    decay = jnp.exp(jnp.where(causal, gam[..., :, None] - gam[..., None, :], NEG))
    kk = jnp.einsum("bhnid,bhnjd->bhnij", k, k)
    a_mat = jnp.where(strict, kk * beta[..., :, None] * decay, 0.0) + jnp.eye(c, dtype=f32)
    u = lax.linalg.triangular_solve(a_mat, v * beta[..., None], left_side=True, lower=True, unit_diagonal=True)
    w = lax.linalg.triangular_solve(a_mat, k * (beta * jnp.exp(gam))[..., None], left_side=True, lower=True, unit_diagonal=True)
    qk = jnp.einsum("bhnid,bhnjd->bhnij", q, k) * decay
    q_dec = q * jnp.exp(gam)[..., None]
    k_dec = k * jnp.exp(gam[..., -1:] - gam)[..., None]
    g_tot = jnp.exp(gam[..., -1])
    xs = tuple(jnp.moveaxis(t, 2, 0) for t in (u, w, qk, q_dec, k_dec, g_tot))

    def step(state, inp):
        u_c, w_c, qk_c, qd_c, kd_c, gt_c = inp
        v_new = u_c - jnp.einsum("bhck,bhkv->bhcv", w_c, state)
        o_c = jnp.einsum("bhck,bhkv->bhcv", qd_c, state) + jnp.einsum("bhcs,bhsv->bhcv", qk_c, v_new)
        state = state * gt_c[..., None, None] + jnp.einsum("bhck,bhcv->bhkv", kd_c, v_new)
        return state, o_c

    s0 = jnp.zeros((bsz, nh, dk, dv), f32)
    _, o = lax.scan(step, s0, xs)
    return jnp.moveaxis(o, 0, 2).reshape(bsz, nh, s, dv)

def gated_deltanet(qkv, z, b_raw, a_raw, conv_w, a_log, dt_bias, norm_w):
    bsz, s, _ = qkv.shape
    f32 = jnp.float32
    qkv_c = jax.nn.silu(causal_depthwise_conv(qkv, conv_w))
    q, k, v = split_cols(qkv_c, (DN_HEADS * DN_DK, DN_HEADS * DN_DK, DN_HEADS * DN_DV))

    def heads(t, d):
        return t.reshape(bsz, s, DN_HEADS, d).transpose(0, 2, 1, 3).astype(f32)

    q = l2norm(heads(q, DN_DK)) * DN_DK ** -0.5
    k = l2norm(heads(k, DN_DK))
    v = heads(v, DN_DV)
    beta = jax.nn.sigmoid(b_raw.astype(f32)).transpose(0, 2, 1)
    g = (-jnp.exp(a_log.astype(f32)) * jax.nn.softplus(a_raw.astype(f32) + dt_bias.astype(f32))).transpose(0, 2, 1)
    o = chunked_gated_delta(q, k, v, g, beta).transpose(0, 2, 1, 3)
    o = o * lax.rsqrt(jnp.mean(o * o, axis=-1, keepdims=True) + EPS) * norm_w.astype(f32)
    o = o * jax.nn.silu(z.reshape(bsz, s, DN_HEADS, DN_DV).astype(f32))
    return o.reshape(bsz, s, DN_HEADS * DN_DV).astype(qkv.dtype)

def conformer_conv(u, dw_w, dw_b, ln_w, ln_b):
    val, gate = jnp.split(u, 2, axis=-1)
    h = val * jax.nn.sigmoid(gate)
    h = causal_depthwise_conv(h, dw_w) + dw_b
    h = layer_norm(h, ln_w, ln_b)
    return jax.nn.silu(h)

def nsa_mixer(q, k_cmp, v_cmp, k_slc, v_slc, k_win, v_win, gate_raw,
              k_pos, v_pos, k_w1, k_w2, v_w1, v_w2):
    bsz, s, _ = q.shape
    dt = q.dtype

    def kv_heads(t):
        return t.reshape(bsz, s, NSA_KV, NSA_DH).transpose(0, 2, 1, 3)

    qh = q.reshape(bsz, s, NSA_KV, NSA_HPG, NSA_DH).transpose(0, 2, 3, 1, 4) * NSA_DH ** -0.5
    gates = jax.nn.sigmoid(gate_raw.astype(jnp.float32)).astype(dt)
    gates = gates.reshape(bsz, s, 3, NSA_KV, NSA_HPG).transpose(2, 0, 3, 4, 1)

    n_cmp = (s - CMP_LEN) // CMP_STRIDE + 1
    win_idx = np.arange(n_cmp)[:, None] * CMP_STRIDE + np.arange(CMP_LEN)[None, :]

    def compress(t, pos, w1, w2):
        blocks = kv_heads(t)[:, :, win_idx] + pos
        blocks = blocks.reshape(bsz, NSA_KV, n_cmp, CMP_LEN * NSA_DH)
        return jax.nn.silu(blocks @ w1) @ w2

    kc = compress(k_cmp, k_pos, k_w1, k_w2)
    vc = compress(v_cmp, v_pos, v_w1, v_w2)
    cmp_start = np.arange(n_cmp) * CMP_STRIDE
    cmp_end = jnp.asarray(cmp_start + CMP_LEN - 1)

    n_blk = s // SEL_BLOCK
    n_sel = min(N_SEL, n_blk)
    blk_start = np.arange(n_blk) * SEL_BLOCK
    overlap = jnp.asarray(((cmp_start[:, None] < blk_start[None, :] + SEL_BLOCK)
                           & (cmp_start[:, None] + CMP_LEN > blk_start[None, :])).astype(np.float32))
    ks = kv_heads(k_slc).reshape(bsz, NSA_KV, n_blk, SEL_BLOCK, NSA_DH)
    vs = kv_heads(v_slc).reshape(bsz, NSA_KV, n_blk, SEL_BLOCK, NSA_DH)

    kw = jnp.pad(kv_heads(k_win), ((0, 0), (0, 0), (WINDOW, 0), (0, 0)))
    vw = jnp.pad(kv_heads(v_win), ((0, 0), (0, 0), (WINDOW, 0), (0, 0)))

    bi = jnp.arange(bsz)[:, None, None, None]
    gi = jnp.arange(NSA_KV)[None, :, None, None]
    blk_ids = jnp.arange(n_blk)

    def block_fn(c):
        start = c * Q_BLOCK
        t = start + jnp.arange(Q_BLOCK)
        qc = lax.dynamic_slice_in_dim(qh, start, Q_BLOCK, axis=3)
        gc = lax.dynamic_slice_in_dim(gates, start, Q_BLOCK, axis=4)
        m_c = cmp_end[None, :] <= t[:, None]
        p_c = masked_softmax(jnp.einsum("bghqd,bgnd->bghqn", qc, kc), m_c) * m_c
        o_c = jnp.einsum("bghqn,bgnd->bghqd", p_c.astype(dt), vc)
        imp = jnp.einsum("bghqn,nj->bgqj", p_c, overlap)
        cur = t[:, None] // SEL_BLOCK
        elig = blk_ids[None, :] <= cur
        forced = (blk_ids[None, :] == 0) | (blk_ids[None, :] == cur) | (blk_ids[None, :] == cur - 1)
        score = jnp.where(elig, imp + jnp.where(forced, SEL_BIG, 0.0), -SEL_BIG)
        _, sel = lax.top_k(score, n_sel)
        k_sel = ks[bi, gi, sel]
        v_sel = vs[bi, gi, sel].reshape(bsz, NSA_KV, Q_BLOCK, n_sel * SEL_BLOCK, NSA_DH)
        kpos = (sel[..., None] * SEL_BLOCK + jnp.arange(SEL_BLOCK)).reshape(bsz, NSA_KV, 1, Q_BLOCK, n_sel * SEL_BLOCK)
        m_s = kpos <= t[:, None]
        s_s = jnp.einsum("bghqd,bgqnld->bghqnl", qc, k_sel).reshape(bsz, NSA_KV, NSA_HPG, Q_BLOCK, n_sel * SEL_BLOCK)
        p_s = masked_softmax(s_s, m_s)
        o_s = jnp.einsum("bghqk,bgqkd->bghqd", p_s.astype(dt), v_sel)
        kwc = lax.dynamic_slice_in_dim(kw, start, WINDOW + Q_BLOCK, axis=2)
        vwc = lax.dynamic_slice_in_dim(vw, start, WINDOW + Q_BLOCK, axis=2)
        kpos_w = start - WINDOW + jnp.arange(WINDOW + Q_BLOCK)
        m_w = (kpos_w[None, :] <= t[:, None]) & (kpos_w[None, :] > t[:, None] - WINDOW) & (kpos_w[None, :] >= 0)
        p_w = masked_softmax(jnp.einsum("bghqd,bgkd->bghqk", qc, kwc), m_w)
        o_w = jnp.einsum("bghqk,bgkd->bghqd", p_w.astype(dt), vwc)
        return gc[0][..., None] * o_c + gc[1][..., None] * o_s + gc[2][..., None] * o_w

    out = lax.map(block_fn, jnp.arange(s // Q_BLOCK))
    return out.transpose(1, 0, 4, 2, 3, 5).reshape(bsz, s, NSA_HEADS * NSA_DH)

def setup_inputs(seed: int = 0) -> dict:
    key = jax.random.key(seed)
    ks = jax.random.split(key, 24)
    f32 = jnp.float32
    nrm = lambda k, shape, scale: scale * jax.random.normal(k, shape, f32)
    dt_init = jnp.exp(jax.random.uniform(ks[5], (DEPTH, DN_HEADS), f32, np.log(1e-3), np.log(1e-1)))
    return {
        "x": nrm(ks[0], (BATCH, SEQ, D_MODEL), 1.0),
        "norm_w": 1.0 + nrm(ks[1], (DEPTH, 4, D_MODEL), 0.05),
        "w_in": nrm(ks[2], (DEPTH, D_MODEL, N_IN), D_MODEL ** -0.5),
        "dn_conv_w": nrm(ks[3], (DEPTH, DN_CONV, DN_QKV), DN_CONV ** -0.5),
        "dn_a_log": jnp.log(jax.random.uniform(ks[4], (DEPTH, DN_HEADS), f32, 1.0, 16.0)),
        "dn_dt_bias": dt_init + jnp.log(-jnp.expm1(-dt_init)),
        "dn_norm_w": 1.0 + nrm(ks[6], (DEPTH, DN_DV), 0.05),
        "cf_dw_w": nrm(ks[7], (DEPTH, CF_KERNEL, CF_CH), CF_KERNEL ** -0.5),
        "cf_dw_b": nrm(ks[8], (DEPTH, CF_CH), 0.02),
        "cf_ln_w": 1.0 + nrm(ks[9], (DEPTH, CF_CH), 0.05),
        "cf_ln_b": nrm(ks[10], (DEPTH, CF_CH), 0.02),
        "nsa_k_pos": nrm(ks[11], (DEPTH, CMP_LEN, NSA_DH), 0.1),
        "nsa_v_pos": nrm(ks[12], (DEPTH, CMP_LEN, NSA_DH), 0.1),
        "nsa_k_w1": nrm(ks[13], (DEPTH, CMP_LEN * NSA_DH, CMP_HID), (CMP_LEN * NSA_DH) ** -0.5),
        "nsa_k_w2": nrm(ks[14], (DEPTH, CMP_HID, NSA_DH), CMP_HID ** -0.5),
        "nsa_v_w1": nrm(ks[15], (DEPTH, CMP_LEN * NSA_DH, CMP_HID), (CMP_LEN * NSA_DH) ** -0.5),
        "nsa_v_w2": nrm(ks[16], (DEPTH, CMP_HID, NSA_DH), CMP_HID ** -0.5),
        "w_out": nrm(ks[17], (DEPTH, D_MIX, D_MODEL), D_MIX ** -0.5),
        "ffn_w_gate": nrm(ks[18], (DEPTH, D_MODEL, D_FF), D_MODEL ** -0.5),
        "ffn_w_up": nrm(ks[19], (DEPTH, D_MODEL, D_FF), D_MODEL ** -0.5),
        "ffn_w_down": nrm(ks[20], (DEPTH, D_FF, D_MODEL), D_FF ** -0.5),
    }

def reference(x, norm_w, w_in, dn_conv_w, dn_a_log, dn_dt_bias, dn_norm_w,
              cf_dw_w, cf_dw_b, cf_ln_w, cf_ln_b,
              nsa_k_pos, nsa_v_pos, nsa_k_w1, nsa_k_w2, nsa_v_w1, nsa_v_w2,
              w_out, ffn_w_gate, ffn_w_up, ffn_w_down):
    for l in range(DEPTH):
        h = rms_norm(x, norm_w[l, 0])
        proj = h @ w_in[l]
        (dn_qkv, dn_z, dn_b, dn_a, cf_u, n_q, n_kc, n_vc, n_ks, n_vs,
         n_kw, n_vw, n_gate) = split_cols(proj, IN_SPLITS)
        o_dn = gated_deltanet(dn_qkv, dn_z, dn_b, dn_a, dn_conv_w[l], dn_a_log[l], dn_dt_bias[l], dn_norm_w[l])
        o_cf = conformer_conv(cf_u, cf_dw_w[l], cf_dw_b[l], cf_ln_w[l], cf_ln_b[l])
        o_nsa = nsa_mixer(n_q, n_kc, n_vc, n_ks, n_vs, n_kw, n_vw, n_gate,
                          nsa_k_pos[l], nsa_v_pos[l], nsa_k_w1[l], nsa_k_w2[l], nsa_v_w1[l], nsa_v_w2[l])
        mix = jnp.concatenate([o_dn, o_cf, o_nsa], axis=-1) @ w_out[l]
        x = x + rms_norm(mix, norm_w[l, 1])
        h = rms_norm(x, norm_w[l, 2])
        f = (jax.nn.silu(h @ ffn_w_gate[l]) * (h @ ffn_w_up[l])) @ ffn_w_down[l]
        x = x + rms_norm(f, norm_w[l, 3])
    return x


_drawn_inputs = setup_inputs


def setup_inputs(seed=0):
    import zlib

    import numpy as np

    out = dict(_drawn_inputs(seed))
    spreads = {}
    factors = {'cf_dw_b': 2.868, 'cf_ln_b': 5.111, 'nsa_k_pos': 7.684}
    for name, (base, spread) in spreads.items():
        noise = np.random.default_rng([zlib.crc32(name.encode()), seed]).standard_normal(out[name].shape)
        drawn = base * np.exp(spread * noise) if base else spread * noise
        out[name] = __import__('jax').numpy.asarray(drawn.astype(out[name].dtype))
    for name, factor in factors.items():
        out[name] = (out[name] * factor).astype(out[name].dtype)
    return out
```

```python
from contextlib import ExitStack

import numpy as np
import concourse.bass as bass
from concourse import mybir

F32 = mybir.dt.float32
F32R = mybir.dt.float32r
ALU = mybir.AluOpType
ACT = mybir.ActivationFunctionType
AX = mybir.AxisListType

LOG_EXP = "natural_log_exp_and_others"

P = 128
D_MODEL = 1024
SEQ = 2048
KT = D_MODEL // P
NT = SEQ // P
NB = 512
TB = SEQ // NB
EPS = 1e-6
NEG = -1e30
SEL_BIG = 1e4

DN_HEADS = 6
DH = 64
DN_PAIRS = DN_HEADS // 2
DN_TAPS = 4
CF_CH = 256
CF_TAPS = 31
HPG = 3
CMP_LEN = 32
CMP_STRIDE = 16
N_CMP = (SEQ - CMP_LEN) // CMP_STRIDE + 1
SEL_BLOCK = 64
N_BLK = SEQ // SEL_BLOCK
WINDOW = 512
D_FF = 2816
FT = D_FF // P

T_CF = 0
T_NQ = 4
T_KC, T_VC, T_KS, T_VS, T_KW, T_VW, T_SM = 7, 8, 9, 10, 11, 12, 13
T_DZ, T_DQ, T_DK, T_DV = 14, 17, 20, 23
MT = 26
PAD = 32
N_SMALL = 2 * DN_HEADS + 3 * 2 * HPG


def mm3(pe, out, w_hi, w_lo, a_hi, a_lo, start, stop):
    pe.matmul(out, w_hi, a_hi, start=start, stop=False)
    pe.matmul(out, w_hi, a_lo, start=False, stop=False)
    return pe.matmul(out, w_lo, a_hi, start=False, stop=stop)


def alone(eng, stood):
    eng.sem_inc(stood, 1)


class Scope:

    def __init__(self, nc, ctx, tag):
        self.nc, self.ctx, self.tag = nc, ctx, tag

    def sb(self, name, shape, dt=F32):
        return self.ctx.enter_context(self.nc.sbuf_tensor(f"{self.tag}_{name}", shape, dt))

    def ps(self, name, shape, dt=F32):
        return self.ctx.enter_context(self.nc.psum_tensor(f"{self.tag}_{name}", shape, dt))

    def sem(self, name):
        return self.nc.alloc_semaphore(f"{self.tag}_{name}")


def build_constants(nc, ident):
    with ExitStack() as ctx:
        sc = Scope(nc, ctx, "const")
        made = sc.sem("made")
        block = ctx.enter_context(nc.Block())

        @block.gpsimd
        def _(pool):
            pool.memset(ident[:, :], 0.0).then_inc(made, 1)
            pool.wait_ge(made, 1)
            pool.affine_select(out=ident[:, :], in_=ident[:, :], compare_op=ALU.not_equal, fill=1.0, base=0,
                               pattern=[[-1, P]], channel_multiplier=1).then_inc(made, 1)
            pool.wait_ge(made, 2)


def norm_and_turn(nc, x, w_pre, ident, h_hi, h_lo):
    with ExitStack() as ctx:
        sc = Scope(nc, ctx, "turn")
        xt = sc.sb("xt", [P, 2, D_MODEL])
        xn = sc.sb("xn", [P, 2, D_MODEL])
        sq = sc.sb("sq", [P, D_MODEL])
        wb = sc.sb("wb", [P, D_MODEL])
        eps = sc.sb("eps", [P, 1])
        ssq = sc.sb("ssq", [P, NT])
        rms = sc.sb("rms", [P, NT])
        rstd = sc.sb("rstd", [P, NT])
        turned = [[sc.ps(f"turned{b}{g}", [P, NB]) for g in range(2)] for b in range(2)]
        x_in = [sc.sem(f"x_in{b}") for b in range(2)]
        w_in, eps_set, squared, rooted, inverted, normed = (
            sc.sem(n) for n in ("w_in", "eps_set", "squared", "rooted", "inverted", "normed"))
        turn_done, hi_done, lo_done = sc.sem("turn_done"), sc.sem("hi_done"), sc.sem("lo_done")
        block = ctx.enter_context(nc.Block())

        @block.sync
        def _(sp):
            sp.dma_start(wb[:, :], w_pre.partition_broadcast(P)).then_inc(w_in, 16)
            for b in range(2):
                sp.dma_start(xt[:, b, :], x[b * P:(b + 1) * P, :]).then_inc(x_in[b], 16)
            with sp.Fori(1, NT // 2) as i:
                for b in range(2):
                    sp.wait_ge(normed, i * 2 + (b - 1))
                    sp.dma_start(xt[:, b, :], x[bass.ds((i * 2 + b) * P, P), :]).then_inc(x_in[b], 16)

        @block.scalar
        def _(act):
            act.wait_ge(eps_set, 1)
            with act.Fori(0, NT // 2) as i:
                for b in range(2):
                    act.wait_ge(x_in[b], i * 16 + 16)
                    act.wait_ge(rooted, i * 2 + b) if b else None
                    act.activation(sq[:, :], xt[:, b, :], ACT.Square,
                                   accum_out=ssq[:, bass.ds(i * 2 + b, 1)]).then_inc(squared, 1)
                    act.wait_ge(squared, i * 2 + b + 1)
                    act.activation(rms[:, bass.ds(i * 2 + b, 1)], ssq[:, bass.ds(i * 2 + b, 1)], ACT.Sqrt,
                                   bias=eps[:, :], scale=1.0 / D_MODEL).then_inc(rooted, 1)
                for b in range(2):
                    for g in range(2):
                        act.wait_ge(turn_done, i * 4 + 2 * b + g + 1)
                        act.activation(h_hi[:, 4 * g:4 * g + 4, bass.ds((i * 2 + b) * P, P)],
                                       turned[b][g][:, :].rearrange("p (k t) -> p k t", k=4),
                                       ACT.Copy).then_inc(hi_done, 1)

        @block.vector
        def _(dve):
            dve.memset(eps[:, :], EPS).then_inc(eps_set, 1)
            dve.wait_ge(w_in, 16)
            with dve.Fori(0, NT // 2) as i:
                for b in range(2):
                    dve.wait_ge(rooted, i * 2 + b + 1)
                    dve.reciprocal(rstd[:, bass.ds(i * 2 + b, 1)], rms[:, bass.ds(i * 2 + b, 1)]).then_inc(inverted, 1)
                    dve.wait_ge(inverted, i * 2 + b + 1)
                    dve.scalar_tensor_tensor(xn[:, b, :], xt[:, b, :], rstd[:, bass.ds(i * 2 + b, 1)], wb[:, :],
                                             ALU.mult, ALU.mult).then_inc(normed, 1)
                for b in range(2):
                    for g in range(2):
                        dve.wait_ge(hi_done, i * 4 + 2 * b + g + 1)
                        part = (slice(None), slice(4 * g, 4 * g + 4), bass.ds((i * 2 + b) * P, P))
                        dve.tensor_tensor(h_lo[part], turned[b][g][:, :].rearrange("p (k t) -> p k t", k=4),
                                          h_hi[part].bitcast(F32), ALU.subtract).then_inc(lo_done, 1)

        @block.tensor
        def _(pe):
            def tile(i, b, first):
                pe.wait_ge(normed, i * 2 + b + 1)
                for g in range(2):
                    if not first:
                        pe.wait_ge(lo_done, i * 4 + (2 * b + g - 3))
                    for k in range(4):
                        last = pe.transpose(turned[b][g][:, k * P:(k + 1) * P],
                                            xn[:, b, (4 * g + k) * P:(4 * g + k + 1) * P], ident[:, :])
                    last.then_inc(turn_done, 1)

            for b in range(2):
                tile(0, b, True)
            with pe.Fori(1, NT // 2) as i:
                for b in range(2):
                    tile(i, b, False)


def project_in(nc, w_cols, cf_w, cf_b, dn_w, h_hi, h_lo, cf_conv, proj):
    with ExitStack() as ctx:
        sc = Scope(nc, ctx, "proj")
        w_raw = sc.sb("w_raw", [P, 2, D_MODEL])
        w_hi = sc.sb("w_hi", [P, 2, D_MODEL], F32R)
        w_lo = sc.sb("w_lo", [P, 2, D_MODEL], F32R)
        row = sc.sb("row", [P, 2, PAD + SEQ])
        work = sc.sb("work", [P, 2, PAD + SEQ])
        taps_cf = sc.sb("taps_cf", [P, 2, CF_TAPS])
        bias_cf = sc.sb("bias_cf", [P, 2])
        taps_dn = sc.sb("taps_dn", [P, 9, DN_TAPS])
        acc = [sc.ps(f"acc{n}", [P, NB]) for n in range(8)]
        raw_in = [sc.sem(f"raw_in{b}") for b in range(2)]
        row_sent = [sc.sem(f"row_sent{b}") for b in range(2)]
        conv_sent = [sc.sem(f"conv_sent{b}") for b in range(2)]
        taps_in, zeroed, hi_done, lo_done, summed, taken = (
            sc.sem(n) for n in ("taps_in", "zeroed", "hi_done", "lo_done", "summed", "taken"))
        gated, cf_step, dn_step, silu_done = (sc.sem(n) for n in ("gated", "cf_step", "dn_step", "silu_done"))
        block = ctx.enter_context(nc.Block())
        PLAIN, CONV = T_NQ, T_DQ
        tok = slice(PAD, PAD + SEQ)

        @block.sync
        def _(sp):
            for b in range(2):
                sp.dma_start(w_raw[:, b, :], w_cols[b]).then_inc(raw_in[b], 16)
            sp.dma_start(taps_cf[:, :, :], cf_w).then_inc(taps_in, 16)
            sp.dma_start(bias_cf[:, :], cf_b).then_inc(taps_in, 16)
            sp.dma_start(taps_dn[:, :, :], dn_w).then_inc(taps_in, 16)
            with sp.Fori(1, MT // 2) as i:
                for b in range(2):
                    sp.wait_ge(lo_done, i * 2 + (b - 1))
                    sp.dma_start(w_raw[:, b, :], w_cols[i * 2 + b]).then_inc(raw_in[b], 16)

        @block.gpsimd
        def _(pool):
            pool.memset(row[:, :, 0:PAD], 0.0).then_inc(zeroed, 1)
            pool.memset(work[:, :, 0:PAD], 0.0).then_inc(zeroed, 1)
            with pool.Fori(0, MT // 2) as i:
                for b in range(2):
                    pool.wait_ge(hi_done, i * 2 + b + 1)
                    if b == 0:
                        pool.wait_ge(lo_done, i * 2)
                    pool.tensor_tensor(w_lo[:, b, :], w_raw[:, b, :], w_hi[:, b, :].bitcast(F32),
                                       ALU.subtract).then_inc(lo_done, 1)

        @block.scalar
        def _(act):
            def split(r, b, first=False):
                act.wait_ge(raw_in[b], (r - b) * 8 + 16)
                if not first:
                    act.wait_ge(summed, r * 4 - 4)
                act.activation(w_hi[:, b, :], w_raw[:, b, :], ACT.Copy).then_inc(hi_done, 1)

            def evacuate(r, b, dst, func=ACT.Copy):
                for t in range(4):
                    act.wait_ge(summed, r * 4 + (t + 1))
                    act.activation(dst[:, b, PAD + t * NB:PAD + (t + 1) * NB], acc[4 * b + t][:, :],
                                   func).then_inc(taken, 1)

            def send_row(r, b):
                act.wait_ge(taken, r * 4 + 4)
                act.dma_start(proj[r], row[:, b, tok]).then_inc(row_sent[b], 16)

            def silu_row(n, b):
                act.wait_ge(dn_step, n * DN_TAPS + DN_TAPS)
                act.activation(work[:, b, tok], work[:, b, tok], ACT.Silu).then_inc(silu_done, 1)
                act.wait_ge(silu_done, n + 1)
                act.dma_start(proj[n + CONV], work[:, b, tok]).then_inc(conv_sent[b], 16)

            split(0, 0, True)
            split(1, 1, True)
            for c in range(2):
                for t in range(4):
                    act.wait_ge(summed, 8 * c + t + 1)
                    act.activation(work[:, c, PAD + t * NB:PAD + (t + 1) * NB], acc[t][:, :],
                                   ACT.Sigmoid).then_inc(taken, 1)
                split(2 * c + 2, 0)
                if c:
                    act.wait_ge(gated, 1)
                evacuate(2 * c + 1, 1, row)
                split(2 * c + 3, 1)
            def plain(r, b, sent, func=ACT.Copy):
                if sent is not None:
                    act.wait_ge(row_sent[b], sent)
                evacuate(r, b, row, func)
                send_row(r, b)
                split(r + 2, b)

            plain(PLAIN, 0, None)
            act.wait_ge(gated, 2)
            plain(PLAIN + 1, 1, None)
            with act.Fori(1, 5) as i:
                for b in range(2):
                    plain(i * 2 + (PLAIN + b), b, i * 16)
            for r in range(T_DZ, T_DQ):
                plain(r, r % 2, (r - PLAIN) // 2 * 16, ACT.Silu)

            def convolved(r, b, n, first):
                if first:
                    act.wait_ge(row_sent[b], (7 - b) * 16)
                else:
                    act.wait_ge(dn_step, n * DN_TAPS - DN_TAPS)
                evacuate(r, b, row)

            convolved(CONV, 1, 0, True)
            split(CONV + 2, 1)
            convolved(CONV + 1, 0, 1, True)
            split(CONV + 3, 0)
            silu_row(0, 0)
            with act.Fori(1, 3) as i:
                convolved(i * 2 + CONV, 1, i * 2, False)
                split(i * 2 + (CONV + 2), 1)
                silu_row(i * 2 - 1, 1)
                convolved(i * 2 + (CONV + 1), 0, i * 2 + 1, False)
                split(i * 2 + (CONV + 3), 0)
                silu_row(i * 2, 0)
            convolved(CONV + 6, 1, 6, False)
            split(CONV + 8, 1)
            silu_row(5, 1)
            convolved(CONV + 7, 0, 7, False)
            silu_row(6, 0)
            convolved(CONV + 8, 1, 8, False)
            silu_row(7, 1)
            silu_row(8, 0)
            for b in range(2):
                act.wait_ge(row_sent[b], (7 - b) * 16)
                act.wait_ge(conv_sent[b], (5 - b) * 16)

        @block.vector
        def _(dve):
            dve.wait_ge(taps_in, 48)
            dve.wait_ge(zeroed, 2)
            n = 0
            for c in range(2):
                dve.wait_ge(taken, 8 * c + 8)
                dve.tensor_tensor(work[:, c, tok], work[:, c, tok], row[:, 1, tok], ALU.mult).then_inc(gated, 1)
                dve.wait_ge(gated, c + 1)
                for k in range(CF_TAPS):
                    at = work[:, c, PAD - CF_TAPS + 1 + k:PAD - CF_TAPS + 1 + k + SEQ]
                    if k == 0:
                        dve.tensor_scalar(cf_conv[:, c, :], at, taps_cf[:, c, k:k + 1], bias_cf[:, c:c + 1],
                                          ALU.mult, ALU.add).then_inc(cf_step, 1)
                    else:
                        dve.wait_ge(cf_step, n)
                        dve.scalar_tensor_tensor(cf_conv[:, c, :], at, taps_cf[:, c, k:k + 1], cf_conv[:, c, :],
                                                 ALU.mult, ALU.add).then_inc(cf_step, 1)
                    n += 1

            def convolve(n, b, sent):
                dve.wait_ge(taken, n * 4 + (CONV * 4 + 4))
                if sent is not None:
                    dve.wait_ge(conv_sent[b], sent)
                for k in range(DN_TAPS):
                    at = row[:, 1 - b, PAD - DN_TAPS + 1 + k:PAD - DN_TAPS + 1 + k + SEQ]
                    tap = taps_dn[:, bass.ds(n, 1), k]
                    if k == 0:
                        dve.wait_ge(cf_step, 2 * CF_TAPS)
                        dve.tensor_scalar(work[:, b, tok], at, tap, None, ALU.mult).then_inc(dn_step, 1)
                    else:
                        dve.wait_ge(dn_step, n * DN_TAPS + k)
                        dve.scalar_tensor_tensor(work[:, b, tok], at, tap, work[:, b, tok],
                                                 ALU.mult, ALU.add).then_inc(dn_step, 1)

            convolve(0, 0, None)
            convolve(1, 1, None)
            with dve.Fori(1, 4) as i:
                convolve(i * 2, 0, i * 16)
                convolve(i * 2 + 1, 1, i * 16)
            convolve(8, 0, 4 * 16)

        @block.tensor
        def _(pe):
            def project(r, b, first):
                pe.wait_ge(lo_done, r + 1)
                for t in range(4):
                    if not first:
                        pe.wait_ge(taken, r * 4 + (t - 7))
                    for k in range(KT):
                        last = mm3(pe, acc[4 * b + t][:, :], w_hi[:, b, k * P:(k + 1) * P],
                                   w_lo[:, b, k * P:(k + 1) * P], h_hi[:, k, t * NB:(t + 1) * NB],
                                   h_lo[:, k, t * NB:(t + 1) * NB], k == 0, k == KT - 1)
                    last.then_inc(summed, 1)

            for b in range(2):
                project(b, b, True)
            with pe.Fori(1, MT // 2) as i:
                for b in range(2):
                    project(i * 2 + b, b, False)


def shape_constants():
    f = np.float32
    i, j = np.arange(P)[:, None], np.arange(P)[None, :]
    c = {"ident": (i == j), "upper": (i <= j), "halves": (i // DH == j // DH),
         "mean_cf": np.full((P, P), 1.0 / CF_CH)}
    steps = [2 ** n for n in range(7)]
    c["joins"] = np.concatenate([(i // (2 * s) == j // (2 * s)) & (j // s % 2 == 1) & (i // s % 2 == 0)
                                 for s in steps], axis=1)
    m = np.arange(2 * P - 8)[None, :] - (P - 8)
    seen = CMP_STRIDE * m + CMP_LEN - 1 <= i
    c["cmp_seen"], c["cmp_bias"] = seen, np.where(seen, 0.0, NEG)
    m = np.arange(2 * N_BLK - 2)[None, :] - (N_BLK - 2)
    cur = i // SEL_BLOCK
    elig = m <= cur
    c["blk_elig"] = elig
    c["blk_add"] = np.where(elig, np.where(m >= cur - 1, SEL_BIG, 0.0), -SEL_BIG)
    c["causal"] = np.where(j <= i, 0.0, NEG)
    k = np.arange(WINDOW + P)[None, :]
    c["band"] = np.where((k > i) & (k <= i + WINDOW), 0.0, NEG)
    k = np.arange(WINDOW + SEQ)[None, :]
    c["before_start"] = np.where((k < WINDOW) & (i >= 0), NEG, 0.0)
    return {n: np.ascontiguousarray(np.broadcast_to(a, (P, a.shape[1])).astype(f)) for n, a in c.items()}


def prepare(nc, consts, prm, cf_conv, proj, mixed, rows, gates, kc, vc, vs, ks, vw, kw):
    with ExitStack() as ctx:
        sc = Scope(nc, ctx, "prep")
        ident, upper, mean_w = sc.sb("ident", [P, P]), sc.sb("upper", [P, P]), sc.sb("mean_w", [P, P])
        ones = sc.sb("ones", [P, P])
        total = sc.sb("total", [P, NT * DN_HEADS])
        to_last = sc.sb("to_last", [P, NT * DN_HEADS])
        ln_w, ln_b = sc.sb("ln_w", [P, 2]), sc.sb("ln_b", [P, 2])
        eps = sc.sb("eps", [P, 1])
        dt_b, a_log = sc.sb("dt_b", [P, DN_HEADS]), sc.sb("a_log", [P, DN_HEADS])
        small = sc.sb("small", [N_SMALL, SEQ])
        tok_small = sc.sb("tok_small", [P, NT, 32])
        sp_t = [sc.sb(f"sp{n}", [P, NT * DN_HEADS]) for n in range(4)]
        neg_rate = sc.sb("neg_rate", [P, DN_HEADS])
        row_sb = sc.sb("row_sb", [NT * DN_HEADS, 2, P])
        sq = sc.sb("sq", [P, 2, SEQ])
        std = sc.sb("std", [P, SEQ])
        feat = {n: sc.sb(f"f_{n}", [P, SEQ]) for n in ("kc", "vc", "vs", "vw")}
        w1 = {n: sc.sb(f"w1_{n}", [P, CMP_LEN, P]) for n in "kv"}
        w2 = {n: sc.sb(f"w2_{n}", [P, DH]) for n in "kv"}
        pos = {n: sc.sb(f"pos_{n}", [DH, CMP_LEN]) for n in "kv"}
        pos_b = sc.sb("pos_b", [P, 2])
        hid = sc.sb("hid", [P, 4, P])
        bank = [sc.ps(f"bank{n}", [P, NB]) for n in range(8)]
        names = ("c_in c_small in_v in_w in_k in_small zeroed m_sum m_sub sq_done v_sum v_std v_inv v_mul cf_done cf_sent "
                 "sm_turn sm_copy sg step pe_gam gam_copy pe_rows rows_copy rows_sent pe_pos pos_copy pe_hid hid_done pe_cmp "
                 "cmp_copy pe_v v_copy")
        (c_in, c_small, in_v, in_w, in_k, in_small, zeroed, m_sum, m_sub, sq_done, v_sum, v_std, v_inv, v_mul, cf_done, cf_sent,
         sm_turn, sm_copy, sg, step, pe_gam, gam_copy, pe_rows, rows_copy, rows_sent, pe_pos, pos_copy, pe_hid, hid_done, pe_cmp,
         cmp_copy, pe_v, v_copy) = (sc.sem(n) for n in names.split())
        block = ctx.enter_context(nc.Block())
        NH = NT * DN_HEADS
        hid_bank = [bank[7], bank[0]]
        beta, gam, nsa_gate = gates[:, :, 0:6], gates[:, :, 6:12], gates[:, :, 12:30]

        @block.sync
        def _(sp):
            sp.dma_start(mean_w[:, :], consts["mean_cf"]).then_inc(c_in, 16)
            sp.dma_start(ident[:, :], consts["ident"]).then_inc(c_in, 16)
            sp.dma_start(upper[:, :], consts["upper"]).then_inc(c_in, 16)
            sp.dma_start(small[:, :], proj[T_SM][0:N_SMALL, :]).then_inc(in_small, 16)
            sp.dma_start(ln_w[:, :], prm["cf_ln_w"]).then_inc(c_small, 16)
            sp.dma_start(ln_b[:, :], prm["cf_ln_b"]).then_inc(c_small, 16)
            sp.dma_start(dt_b[:, :], prm["dn_dt_bias"].partition_broadcast(P)).then_inc(c_small, 16)
            sp.dma_start(a_log[:, :], prm["dn_a_log"].partition_broadcast(P)).then_inc(c_small, 16)
            for n, t in (("vs", T_VS), ("vw", T_VW)):
                sp.dma_start(feat[n][:, :], proj[t]).then_inc(in_v, 16)
            for n in "kv":
                for h in range(2):
                    sp.dma_start(w1[n][h * DH:(h + 1) * DH, :, :], prm[f"nsa_{n}_w1"]).then_inc(in_w, 16)
                sp.dma_start(w2[n][:, :], prm[f"nsa_{n}_w2"]).then_inc(in_w, 16)
                sp.dma_start(pos[n][:, :], prm[f"nsa_{n}_pos"]).then_inc(in_w, 16)
            for n, t in (("kc", T_KC), ("vc", T_VC)):
                sp.dma_start(feat[n][:, :], proj[t]).then_inc(in_w, 16)
            sp.dma_start(ks[:, :], proj[T_KS]).then_inc(in_k, 16)
            sp.dma_start(kw[:, WINDOW:WINDOW + SEQ], proj[T_KW]).then_inc(in_k, 16)
            for c in range(2):
                sp.wait_ge(cf_done, c + 1)
                sp.dma_start(mixed[:, 3 + c, :], sq[:, c, :]).then_inc(cf_sent, 16)
            sp.wait_ge(rows_copy, 2)
            sp.dma_start(rows.rearrange("r (h t) -> h r t", t=P), row_sb[:, :, :]).then_inc(rows_sent, 16)
            sp.wait_ge(in_k, 32)
            sp.wait_ge(cf_sent, 32)
            sp.wait_ge(rows_sent, 16)

        @block.gpsimd
        def _(pool):
            pool.memset(vw[:, 0:4, :], 0.0).then_inc(zeroed, 1)
            pool.memset(kw[:, 0:WINDOW], 0.0).then_inc(zeroed, 1)
            pool.memset(kc[:, :], 0.0).then_inc(zeroed, 1)
            pool.memset(vc[:, :], 0.0).then_inc(zeroed, 1)
            pool.memset(eps[:, :], EPS).then_inc(zeroed, 1)
            pool.memset(ones[:, :], 1.0).then_inc(zeroed, 1)
            pool.wait_ge(zeroed, 6)

        @block.tensor
        def _(pe):
            pe.wait_ge(c_in, 48)
            for t in range(TB):
                for c in range(2):
                    last = pe.matmul(bank[t][:, :], mean_w[:, :], cf_conv[:, c, t * NB:(t + 1) * NB],
                                     start=c == 0, stop=c == 1)
                last.then_inc(m_sum, 1)
            pe.wait_ge(in_small, 16)
            for t in range(NT):
                last = pe.transpose(bank[4][:, t * 32:t * 32 + N_SMALL], small[:, t * P:(t + 1) * P],
                                    ident[0:N_SMALL, 0:N_SMALL])
            last.then_inc(sm_turn, 1)
            pe.wait_ge(in_w, 16 * 10)
            for n, x in enumerate("kv"):
                for l in range(CMP_LEN):
                    last = pe.matmul(bank[6][:, n:n + 1], w1[x][0:DH, l, :], pos[x][:, l:l + 1],
                                     start=l == 0, stop=l == CMP_LEN - 1)
            last.then_inc(pe_pos, 1)
            for t in range(TB):
                pe.wait_ge(sq_done, 2 * t + 2)
                for c in range(2):
                    last = pe.matmul(bank[t][:, :], mean_w[:, :], sq[:, c, t * NB:(t + 1) * NB],
                                     start=c == 0, stop=c == 1)
                last.then_inc(v_sum, 1)
            pe.wait_ge(v_std, 1)
            for n, x in enumerate("kv"):
                src = feat[x + "c"]
                for l in range(CMP_LEN):
                    for g in range(2):
                        at = slice(g * DH, (g + 1) * DH)
                        last = pe.matmul(hid_bank[g][:, n * P:n * P + N_CMP], w1[x][at, l, :],
                                         src[at, l:l + CMP_STRIDE * (N_CMP - 1) + 1:CMP_STRIDE],
                                         start=l == 0, stop=l == CMP_LEN - 1)
                        if l == CMP_LEN - 1 and n:
                            last.then_inc(pe_hid, 1)
            pe.wait_ge(gam_copy, 1)
            pe.matmul(bank[5][:, 0:NH], upper[:, :], sp_t[3][:, :], start=True, stop=True)
            pe.wait_ge(zeroed, 6)
            pe.matmul(bank[5][:, 3 * P:3 * P + NH], ones[:, :], sp_t[3][:, :], start=True, stop=True).then_inc(pe_gam, 1)
            pe.wait_ge(in_v, 32)
            n = 0
            for x, dst in (("vs", vs), ("vw", vw)):
                for q in range(4):
                    b = bank[6] if n % 2 else bank[4]
                    if n == 0:
                        pe.wait_ge(sm_copy, 1)
                    elif n == 1:
                        pe.wait_ge(pos_copy, 1)
                    else:
                        pe.wait_ge(v_copy, n - 1)
                    for k in range(4):
                        last = pe.transpose(b[:, k * P:(k + 1) * P], feat[x][:, (4 * q + k) * P:(4 * q + k + 1) * P],
                                            ident[:, :])
                    last.then_inc(pe_v, 1)
                    n += 1
            pe.wait_ge(gam_copy, 2)
            pe.transpose(bank[5][0:NH, P:2 * P], sp_t[0][:, :], ident[:, :]).then_inc(pe_rows, 1)
            pe.transpose(bank[5][0:NH, 2 * P:3 * P], sp_t[1][:, :], ident[:, :]).then_inc(pe_rows, 1)
            pe.wait_ge(hid_done, 4)
            pe.wait_ge(v_copy, 8)
            for g in range(2):
                pe.matmul(bank[6][g * DH:(g + 1) * DH, 0:N_CMP], w2["k"][:, :], hid[:, g, 0:N_CMP],
                          start=True, stop=True)
            for g in range(2):
                last = pe.matmul(bank[6][0:N_CMP, P + g * DH:P + (g + 1) * DH], hid[:, 2 + g, 0:N_CMP], w2["v"][:, :],
                                 start=True, stop=True)
            last.then_inc(pe_cmp, 1)

        @block.scalar
        def _(act):
            for t in range(TB):
                for c in range(2):
                    act.wait_ge(m_sub, 2 * t + c + 1)
                    act.activation(sq[:, c, t * NB:(t + 1) * NB], cf_conv[:, c, t * NB:(t + 1) * NB],
                                   ACT.Square).then_inc(sq_done, 1)
            act.wait_ge(zeroed, 6)
            act.wait_ge(sm_copy, 1)
            act.activation(beta, tok_small[:, :, 0:6], ACT.Sigmoid).then_inc(sg, 1)
            act.activation(nsa_gate, tok_small[:, :, 12:30], ACT.Sigmoid).then_inc(sg, 1)
            for t in range(TB):
                act.wait_ge(v_sum, t + 1)
                act.activation(std[:, t * NB:(t + 1) * NB], bank[t][:, :], ACT.Sqrt, bias=eps[:, :]).then_inc(v_std, 1)
            act.wait_ge(step, 2)
            act.activation(sp_t[1][:, :], sp_t[0][:, :], ACT.Abs).then_inc(sg, 1)
            act.wait_ge(sg, 3)
            act.activation(sp_t[2][:, :], sp_t[1][:, :], ACT.Exp, scale=-1.0).then_inc(sg, 1)
            act.wait_ge(c_small, 64)
            act.activation(neg_rate[:, :], a_log[:, :], ACT.Exp).then_inc(sg, 1)
            act.wait_ge(sg, 4)
            act.activation(sp_t[1][:, :], sp_t[2][:, :], ACT.Ln, bias=1.0).then_inc(sg, 1)
            act.wait_ge(step, 7)
            for at, src in ((30, sp_t[0]), (42, to_last)):
                act.activation(gates[:, :, at:at + 6], src[:, :].rearrange("p (t h) -> p t h", h=DN_HEADS),
                               ACT.Exp).then_inc(sg, 1)
            for r in range(2):
                part = slice(r * DH, (r + 1) * DH)
                act.activation(gates[part, :, 48:51],
                               total[part, :].rearrange("p (t h) -> p t h", h=DN_HEADS)[:, :, 3 * r:3 * r + 3],
                               ACT.Exp).then_inc(sg, 1)
            for n in range(4):
                act.wait_ge(pe_hid, 2)
                act.wait_ge(pos_copy, 1)
                act.activation(hid[:, n, 0:N_CMP], hid_bank[n % 2][:, (n // 2) * P:(n // 2) * P + N_CMP], ACT.Silu,
                               bias=pos_b[:, n // 2:n // 2 + 1]).then_inc(hid_done, 1)
            for c in range(2):
                act.wait_ge(v_mul, c + 1)
                act.activation(sq[:, c, :], cf_conv[:, c, :], ACT.Silu, scale=ln_w[:, c:c + 1],
                               bias=ln_b[:, c:c + 1]).then_inc(cf_done, 1)

        @block.vector
        def _(dve):
            for t in range(TB):
                dve.wait_ge(m_sum, t + 1)
                for c in range(2):
                    part = cf_conv[:, c, t * NB:(t + 1) * NB]
                    dve.tensor_tensor(part, part, bank[t][:, :], ALU.subtract).then_inc(m_sub, 1)
            dve.wait_ge(sm_turn, 1)
            dve.tensor_copy(tok_small[:, :, 0:N_SMALL],
                            bank[4][:, :].rearrange("p (t n) -> p t n", n=32)[:, :, 0:N_SMALL]).then_inc(sm_copy, 1)
            dve.wait_ge(pe_pos, 1)
            dve.tensor_copy(pos_b[:, :], bank[6][:, 0:2]).then_inc(pos_copy, 1)
            dve.wait_ge(sm_copy, 1)
            dve.wait_ge(c_small, 64)
            heads = [P, NT, DN_HEADS]
            x0 = sp_t[0][:, :].rearrange("p (t h) -> p t h", h=DN_HEADS)
            dve.tensor_tensor(x0, tok_small[:, :, 6:12], dt_b[:, None, :].to_broadcast(heads), ALU.add).then_inc(step, 1)
            dve.wait_ge(step, 1)
            dve.tensor_scalar(sp_t[3][:, :], sp_t[0][:, :], 0.0, None, ALU.max).then_inc(step, 1)
            dve.wait_ge(sg, 6)
            dve.wait_ge(step, 2)
            dve.tensor_tensor(sp_t[3][:, :], sp_t[3][:, :], sp_t[1][:, :], ALU.add).then_inc(step, 1)
            dve.wait_ge(step, 3)
            x3 = sp_t[3][:, :].rearrange("p (t h) -> p t h", h=DN_HEADS)
            dve.scalar_tensor_tensor(x3, x3, -1.0, neg_rate[:, None, :].to_broadcast(heads),
                                     ALU.mult, ALU.mult).then_inc(gam_copy, 1)
            dve.tensor_copy(sp_t[1][:, :].rearrange("p (t h) -> p t h", h=DN_HEADS), beta).then_inc(step, 1)
            dve.wait_ge(pe_gam, 1)
            dve.tensor_copy(gam, bank[5][:, 0:NH].rearrange("p (t h) -> p t h", h=DN_HEADS)).then_inc(step, 1)
            dve.wait_ge(step, 4)
            dve.tensor_copy(sp_t[0][:, :], bank[5][:, 0:NH]).then_inc(gam_copy, 1)
            dve.tensor_copy(total[:, :], bank[5][:, 3 * P:3 * P + NH]).then_inc(step, 1)
            dve.wait_ge(step, 6)
            dve.wait_ge(gam_copy, 2)
            dve.tensor_tensor(to_last[:, :], total[:, :], sp_t[0][:, :], ALU.subtract).then_inc(step, 1)
            dve.wait_ge(sg, 10)
            dve.tensor_tensor(gates[:, :, 36:42], beta, gates[:, :, 30:36], ALU.mult).then_inc(step, 1)
            for n in range(8):
                dve.wait_ge(pe_v, n + 1)
                dst = vs[:, 4 * n:4 * n + 4, :] if n < 4 else vw[:, 4 * (n - 3):4 * (n - 3) + 4, :]
                b = bank[6] if n % 2 else bank[4]
                dve.tensor_copy(dst, b[:, :].rearrange("p (k t) -> p k t", k=4)).then_inc(v_copy, 1)
            dve.wait_ge(pe_rows, 2)
            for r in range(2):
                dve.tensor_copy(row_sb[:, r, :], bank[5][0:NH, (1 + r) * P:(2 + r) * P]).then_inc(rows_copy, 1)
            dve.wait_ge(zeroed, 6)
            dve.wait_ge(pe_cmp, 1)
            dve.tensor_copy(kc[:, 0:N_CMP], bank[6][:, 0:N_CMP]).then_inc(cmp_copy, 1)
            dve.tensor_copy(vc[0:N_CMP, :], bank[6][0:N_CMP, P:2 * P]).then_inc(cmp_copy, 1)
            for t in range(TB):
                dve.wait_ge(v_std, t + 1)
                part = std[:, t * NB:(t + 1) * NB]
                dve.reciprocal(part, part).then_inc(v_inv, 1)
            dve.wait_ge(v_inv, TB)
            dve.wait_ge(sq_done, 2 * TB)
            for c in range(2):
                dve.tensor_tensor(cf_conv[:, c, :], cf_conv[:, c, :], std[:, :], ALU.mult).then_inc(v_mul, 1)
            dve.wait_ge(cmp_copy, 2)


LEVELS = [2, 4, 8, 16, 32, 64]
HX = [0, 2, 4, 1, 3, 5]


class Steps:

    def __init__(self, sem, names):
        self.sem, self.names, self.at = sem, names.split(), 0
        self.count = len(self.names)

    def step(self, name):
        assert self.names[self.at] == name, (self.names[self.at], name)
        self.at = (self.at + 1) % self.count
        return self.sem

    def after(self, name, t):
        return t * self.count + (self.count + self.names.index(name) + 1)

    def before(self, name, t):
        return t * self.count + (self.names.index(name) + 1)


class DeltaNet:

    RING = 3
    PLACES = 28

    def __init__(self, sc, banks, consts, prm, proj, rows, gates, mixed, ident):
        self.proj, self.rows, self.gates, self.mixed, self.ident, self.prm, self.consts = (
            proj, rows, gates, mixed, ident, prm, consts)
        self.bank = banks
        sb = sc.sb
        self.qkv = sb("qkv", [P, 9, P])
        self.z = sb("z", [P, 3, P])
        self.bc = sb("bc", [P, 2, DN_HEADS, P])
        self.sq = sb("sq", [P, 2, 3 * P])
        self.rs = sb("rs", [P, 2, 3 * P])
        self.qn, self.kn = sb("qn", [P, 3, P]), sb("kn", [P, 3, P])
        self.E, self.EB = sb("E", [P, DN_HEADS, P]), sb("EB", [P, DN_HEADS, P])
        self.AT, self.QK = sb("AT", [P, DN_HEADS, P]), sb("QK", [P, DN_HEADS, P])
        self.L = sb("L", [P, 7, DN_HEADS, P])
        self.X, self.XT, self.Y = sb("X", [P, DN_HEADS, P]), sb("XT", [P, DN_HEADS, P]), sb("Y", [P, DN_HEADS, P])
        self.bv, self.kb, self.kd = sb("bv", [P, 3, P]), sb("kb", [P, 3, P]), sb("kd", [P, 3, P])
        self.U, self.WT, self.vn, self.o = sb("U", [P, 3, P]), sb("WT", [P, 3, P]), sb("vn", [P, 3, P]), sb("o", [P, 3, P])
        self.S, self.Sg = sb("S", [P, 3, P]), sb("Sg", [P, 3, P])
        self.osq, self.ssq, self.ors = sb("osq", [P, 3, P]), sb("ssq", [P, DN_HEADS]), sb("ors", [P, DN_HEADS])
        self.mix = sb("mix", [P, 3, P])
        self.halves, self.upper, self.joins = sb("halves", [P, P]), sb("upper", [P, P]), sb("joins", [P, 7, P])
        self.nw, self.eps = sb("nw", [P, 1]), sb("eps", [P, 1])
        self.c_in, self.ready, self.stood = sc.sem("c_in"), sc.sem("ready"), sc.sem("stood")
        self.qkv_in, self.z_in, self.bc_in, self.sent = (sc.sem(n) for n in ("qkv_in", "z_in", "bc_in", "sent"))
        lev = " ".join(f"y{s}A y{s}B x{s}A t{s}A x{s}B t{s}B" if s < 64 else f"y{s}A y{s}B t{s}A t{s}B" for s in LEVELS)
        self.pe = Steps(sc.sem("pe"), f"l2q l2k kt vt kkA kkB qkA qkB x1A x1B {lev} u wt ws o1 o2 sn ot")
        lev = " ".join(f"x{s}A t{s}A x{s}B t{s}B" if s < 64 else f"t{s}A t{s}B" for s in LEVELS)
        self.v = Steps(sc.sem("dve"), f"qn kn diff kb kd bv atA atB qkA qkB t1 {lev} vn o1 o2 sn ssq mix")
        lev = " ".join(f"y{s}A y{s}B" for s in LEVELS)
        self.a = Steps(sc.sem("act"), f"lnq rsq lnk rsk e x1A x1B {lev} u wt lno rso")
        self.p = Steps(sc.sem("pool"), "sq em eb l1 l2 l4 l8 l16 l32 l64 sg osq on")
        self.taker = {n: (self.v, n) for n in self.pe.names if n in self.v.names}
        self.taker |= {n: (self.a, n) for n in self.pe.names if n in self.a.names}
        self.taker |= {"l2q": (self.a, "lnq"), "l2k": (self.a, "lnk"), "kt": (self.v, "kd"), "vt": (self.v, "bv"),
                       "kkA": (self.v, "atA"), "kkB": (self.v, "atB"), "ws": (self.v, "vn"), "ot": (self.v, "mix")}
        assert set(self.taker) == set(self.pe.names)

    def bank_of(self, name):
        return self.bank[self.pe.names.index(name) % self.RING]

    def wait_bank(self, pe, name, t):
        n = self.pe.names.index(name)
        if n >= self.RING:
            who, what = self.taker[self.pe.names[n - self.RING]]
            pe.wait_ge(who.sem, who.after(what, t))
        else:
            last = max(m for m in range(self.pe.count) if m % self.RING == n % self.RING)
            who, what = self.taker[self.pe.names[last]]
            pe.wait_ge(who.sem, who.before(what, t))

    def start(self, sp, pool):
        if sp is not None:
            sp.dma_start(self.halves[:, :], self.consts["halves"]).then_inc(self.c_in, 16)
            sp.dma_start(self.upper[:, :], self.consts["upper"]).then_inc(self.c_in, 16)
            sp.dma_start(self.joins[:, :, :], self.consts["joins"].rearrange("p (s t) -> p s t", s=7)).then_inc(self.c_in, 16)
            sp.dma_start(self.nw[:, :], self.prm["dn_norm_w"]).then_inc(self.c_in, 16)
        if pool is not None:
            pool.memset(self.eps[:, :], EPS).then_inc(self.ready, 1)
            pool.memset(self.S[:, :, :], 0.0).then_inc(self.ready, 1)
            pool.wait_ge(self.ready, 2)
            for who in (self.pe, self.v, self.a, self.p):
                pool.sem_inc(who.sem, who.count)

    def sync(self, sp, t):
        at = bass.ds(t * P, P)
        sp.wait_ge(self.v.sem, self.v.before("kn", t))
        sp.wait_ge(self.pe.sem, self.pe.before("vt", t))
        sp.dma_start(self.qkv[:, :, :], self.proj[T_DQ:T_DQ + 9, :, at].rearrange("m p t -> p m t")).then_inc(self.qkv_in, 16)
        sp.wait_ge(self.v.sem, self.v.before("diff", t))
        sp.wait_ge(self.p.sem, self.p.before("eb", t))
        alone(sp, self.stood)
        sp.dma_start(self.bc[:, :, :, :], self.rows[:, bass.ds(t * (DN_HEADS * P), DN_HEADS * P)]
                     .rearrange("r (h t) -> r h t", t=P).partition_broadcast(P)).then_inc(self.bc_in, 16)
        sp.wait_ge(self.v.sem, self.v.before("mix", t))
        alone(sp, self.stood)
        sp.dma_start(self.z[:, :, :], self.proj[T_DZ:T_DZ + 3, :, at].rearrange("m p t -> p m t")).then_inc(self.z_in, 16)

    def send(self, sp, t):
        sp.wait_ge(self.v.sem, self.v.after("mix", t))
        alone(sp, self.stood)
        sp.dma_start(self.mixed[:, 0:3, bass.ds(t * P, P)], self.mix[:, :, :]).then_inc(self.sent, 16)

    def tensor(self, pe, t):
        v, a, p = self.v, self.a, self.p
        me = self.pe
        q, k, val = self.qkv[:, 0:3, :], self.qkv[:, 3:6, :], self.qkv[:, 6:9, :]
        flat = "p m t -> p (m t)"

        def heads(group):
            return range(3 * group, 3 * group + 3)

        yield 0
        pe.wait_ge(p.sem, p.after("sq", t))
        for n, name in enumerate(("l2q", "l2k")):
            self.wait_bank(pe, name, t)
            pe.matmul(self.bank_of(name)[:, 0:3 * P], self.halves[:, :], self.sq[:, n, :],
                      start=True, stop=True).then_inc(me.step(name), 1)
        yield 1
        pe.wait_ge(v.sem, v.after("kn", t))
        self.wait_bank(pe, "kt", t)
        for m in range(3):
            last = pe.transpose(self.bank_of("kt")[:, m * P:(m + 1) * P], self.kn[:, m, :], self.ident[:, :])
        last.then_inc(me.step("kt"), 1)
        self.wait_bank(pe, "vt", t)
        for m in range(3):
            last = pe.transpose(self.bank_of("vt")[:, m * P:(m + 1) * P], val[:, m, :], self.ident[:, :])
        last.then_inc(me.step("vt"), 1)
        yield 2
        for what, other in (("kk", self.kn), ("qk", self.qn)):
            for g, name in enumerate((what + "A", what + "B")):
                self.wait_bank(pe, name, t)
                rows = slice(g * DH, (g + 1) * DH)
                for m in range(3):
                    last = pe.matmul(self.bank_of(name)[:, m * P:(m + 1) * P], self.kn[rows, m, :], other[rows, m, :],
                                     start=True, stop=True)
                last.then_inc(me.step(name), 1)
            yield 3 if what == 'kk' else 4
        pe.wait_ge(v.sem, v.after("t1", t))
        for g, name in enumerate(("x1A", "x1B")):
            self.wait_bank(pe, name, t)
            for m, h in enumerate(heads(g)):
                last = pe.transpose(self.bank_of(name)[:, m * P:(m + 1) * P], self.XT[:, h, :], self.ident[:, :])
            last.then_inc(me.step(name), 1)
        yield 5
        prev = 1
        for n, s in enumerate(LEVELS):
            pe.wait_ge(p.sem, p.after(f"l{s}", t))
            for g, G in enumerate("AB"):
                name = f"y{s}{G}"
                self.wait_bank(pe, name, t)
                if prev == 1:
                    pe.wait_ge(a.sem, a.after(f"x1{G}", t))
                else:
                    pe.wait_ge(v.sem, v.after(f"x{prev}{G}", t))
                for m, h in enumerate(heads(g)):
                    last = pe.matmul(self.bank_of(name)[:, m * P:(m + 1) * P], self.L[:, n + 1, h, :], self.X[:, h, :],
                                     start=True, stop=True)
                last.then_inc(me.step(name), 1)
            yield 6 + 3 * n
            for g, G in enumerate("AB"):
                if prev > 1:
                    pe.wait_ge(v.sem, v.after(f"t{prev}{G}", t))
                pe.wait_ge(a.sem, a.after(f"y{s}{G}", t))
                for kind in ("x", "t") if s < 64 else ("t",):
                    name = f"{kind}{s}{G}"
                    self.wait_bank(pe, name, t)
                    for m, h in enumerate(heads(g)):
                        lhs, rhs = (self.XT, self.Y) if kind == "x" else (self.Y, self.XT)
                        last = pe.matmul(self.bank_of(name)[:, m * P:(m + 1) * P], lhs[:, h, :], rhs[:, h, :],
                                         start=True, stop=True)
                    last.then_inc(me.step(name), 1)
                yield 7 + 3 * n + g
            prev = s
        pe.wait_ge(v.sem, v.after("t64B", t))
        self.wait_bank(pe, "u", t)
        for h in range(DN_HEADS):
            at = slice(h * DH, (h + 1) * DH)
            last = pe.matmul(self.bank_of("u")[:, at], self.XT[:, HX.index(h), :],
                             self.bv[:, :, :].rearrange(flat)[:, at], start=True, stop=True)
        last.then_inc(me.step("u"), 1)
        yield 24
        self.wait_bank(pe, "wt", t)
        for h in range(DN_HEADS):
            r = h % 2
            last = pe.matmul(self.bank_of("wt")[r * DH:(r + 1) * DH, (h // 2) * P:(h // 2 + 1) * P],
                             self.kb[:, h // 2, r * DH:(r + 1) * DH], self.XT[:, HX.index(h), :], start=True, stop=True)
        last.then_inc(me.step("wt"), 1)
        yield 25
        pe.wait_ge(v.sem, v.before("sn", t))
        pe.wait_ge(a.sem, a.after("wt", t))
        for name, lhs in (("ws", self.WT), ("o1", self.qn)):
            self.wait_bank(pe, name, t)
            for m in range(3):
                last = pe.matmul(self.bank_of(name)[:, m * P:(m + 1) * P], lhs[:, m, :], self.S[:, m, :],
                                 start=True, stop=True)
            last.then_inc(me.step(name), 1)
        yield 26
        pe.wait_ge(v.sem, v.after("vn", t))
        self.wait_bank(pe, "o2", t)
        for h in range(DN_HEADS):
            at = slice(h * DH, (h + 1) * DH)
            last = pe.matmul(self.bank_of("o2")[:, at], self.QK[:, HX.index(h), :],
                             self.vn[:, :, :].rearrange(flat)[:, at], start=True, stop=True)
        last.then_inc(me.step("o2"), 1)
        self.wait_bank(pe, "sn", t)
        for m in range(3):
            last = pe.matmul(self.bank_of("sn")[:, m * P:(m + 1) * P], self.kd[:, m, :], self.vn[:, m, :],
                             start=True, stop=True)
        last.then_inc(me.step("sn"), 1)
        yield 27
        pe.wait_ge(p.sem, p.after("on", t))
        self.wait_bank(pe, "ot", t)
        for m in range(3):
            last = pe.transpose(self.bank_of("ot")[:, m * P:(m + 1) * P], self.o[:, m, :], self.ident[:, :])
        last.then_inc(me.step("ot"), 1)

    def scalar(self, act, t):
        me, pe, v, p = self.a, self.pe, self.v, self.p
        yield 0.3
        for n, x in enumerate("qk"):
            act.wait_ge(pe.sem, pe.after("l2" + x, t))
            act.wait_ge(v.sem, v.before(x + "n", t))
            act.activation(self.rs[:, n, :], self.bank_of("l2" + x)[:, 0:3 * P], ACT.Ln,
                           bias=self.eps[:, :]).then_inc(me.step("ln" + x), 1)
            act.wait_ge(me.sem, me.after("ln" + x, t))
            act.activation(self.rs[:, n, :], self.rs[:, n, :], ACT.Exp, scale=-0.5).then_inc(me.step("rs" + x), 1)
        yield 0.7
        act.wait_ge(v.sem, v.after("diff", t))
        act.activation(self.E[:, :, :], self.E[:, :, :], ACT.Exp).then_inc(me.step("e"), 1)
        yield 4.5
        for g, G in enumerate("AB"):
            name = "x1" + G
            act.wait_ge(pe.sem, pe.after(name, t))
            act.activation(self.X[:, 3 * g:3 * g + 3, :], self.bank_of(name)[:, 0:3 * P].rearrange("p (h t) -> p h t", h=3),
                           ACT.Copy).then_inc(me.step(name), 1)
        yield 5.3
        for n, s in enumerate(LEVELS):
            for g, G in enumerate("AB"):
                name = f"y{s}{G}"
                act.wait_ge(pe.sem, pe.after(name, t))
                act.activation(self.Y[:, 3 * g:3 * g + 3, :],
                               self.bank_of(name)[:, 0:3 * P].rearrange("p (h t) -> p h t", h=3),
                               ACT.Copy).then_inc(me.step(name), 1)
            yield 8.3 + 3 * n if s < 64 else 24.3
        for name, dst in (("u", self.U), ("wt", self.WT)):
            act.wait_ge(pe.sem, pe.after(name, t))
            act.activation(dst[:, :, :], self.bank_of(name)[:, 0:3 * P].rearrange("p (h t) -> p h t", h=3),
                           ACT.Copy).then_inc(me.step(name), 1)
        yield 26.85
        act.wait_ge(v.sem, v.after("ssq", t))
        act.activation(self.ors[:, :], self.ssq[:, :], ACT.Ln, bias=self.eps[:, :], scale=1.0 / DH).then_inc(me.step("lno"), 1)
        act.wait_ge(me.sem, me.after("lno", t))
        act.activation(self.ors[:, :], self.ors[:, :], ACT.Exp, scale=-0.5).then_inc(me.step("rso"), 1)

    def gpsimd(self, pool, t):
        me, pe, v, a = self.p, self.pe, self.v, self.a
        yield 0
        pool.wait_ge(self.qkv_in, t * 16 + 16)
        pool.wait_ge(pe.sem, pe.before("l2k", t))
        pool.tensor_tensor(self.sq[:, :, :], self.qkv[:, 0:6, :].rearrange("p (a m) t -> p a (m t)", a=2),
                           self.qkv[:, 0:6, :].rearrange("p (a m) t -> p a (m t)", a=2), ALU.mult).then_inc(me.step("sq"), 1)
        yield 0.8
        pool.wait_ge(a.sem, a.after("e", t))
        pool.tensor_tensor(self.E[:, :, :], self.E[:, :, :], self.upper[:, None, :].to_broadcast([P, DN_HEADS, P]),
                           ALU.mult).then_inc(me.step("em"), 1)
        pool.wait_ge(me.sem, me.after("em", t))
        pool.wait_ge(v.sem, v.before("atB", t))
        pool.tensor_tensor(self.EB[:, :, :], self.E[:, :, :], self.bc[:, 1, :, :], ALU.mult).then_inc(me.step("eb"), 1)
        yield 2.7
        pool.wait_ge(v.sem, v.after("atB", t))
        for n in range(7):
            if n:
                pool.wait_ge(pe.sem, pe.before(f"y{2 ** n}B", t))
            pool.tensor_tensor(self.L[:, n, :, :], self.AT[:, :, :],
                               self.joins[:, n:n + 1, :].to_broadcast([P, DN_HEADS, P]),
                               ALU.mult).then_inc(me.step(f"l{2 ** n}"), 1)
        yield 20
        pool.wait_ge(v.sem, v.before("sn", t))
        pool.tensor_tensor(self.Sg[:, :, :], self.S[:, :, :],
                           self.gates[:, bass.ds(t, 1), 48:51].rearrange("p a h -> p (a h)")[:, :, None]
                           .to_broadcast([P, 3, P]), ALU.mult).then_inc(me.step("sg"), 1)
        yield 26.7
        pool.wait_ge(v.sem, v.after("o2", t))
        pool.tensor_tensor(self.osq[:, :, :], self.o[:, :, :], self.o[:, :, :], ALU.mult).then_inc(me.step("osq"), 1)
        yield 26.9
        pool.wait_ge(a.sem, a.after("rso", t))
        o = self.o[:, :, :].rearrange("p m (r d) -> p (m r) d", r=2)
        pool.tensor_tensor(o, o, self.ors[:, :, None].to_broadcast([P, DN_HEADS, DH]), ALU.mult).then_inc(me.step("on"), 1)

    def by_head(self, t, at):
        return (self.gates[:, bass.ds(t, 1), at:at + 6].rearrange("p a (r m) -> p (a m) r", r=2)[:, :, :, None]
                .to_broadcast([P, 3, 2, DH]))

    def vector(self, dve, t):
        me, pe, a, p = self.v, self.pe, self.a, self.p
        four = "p (m r d) -> p m r d"
        q, k = self.qkv[:, 0:3, :], self.qkv[:, 3:6, :]
        rs = [self.rs[:, n, :].rearrange("p (m t) -> p m t", m=3) for n in range(2)]
        yield 0.5
        dve.wait_ge(a.sem, a.after("rsq", t))
        dve.wait_ge(pe.sem, pe.before("o1", t))
        dve.scalar_tensor_tensor(self.qn[:, :, :], q, DH ** -0.5, rs[0], ALU.mult, ALU.mult).then_inc(me.step("qn"), 1)
        dve.wait_ge(a.sem, a.after("rsk", t))
        dve.tensor_tensor(self.kn[:, :, :], k, rs[1], ALU.mult).then_inc(me.step("kn"), 1)
        dve.wait_ge(self.bc_in, t * 16 + 16)
        dve.wait_ge(p.sem, p.before("eb", t))
        for h in range(DN_HEADS):
            last = dve.tensor_scalar(self.E[:, h, :], self.bc[:, 0, h, :],
                                     self.gates[:, bass.ds(t, 1), 6 + h], 0.0, ALU.subtract, ALU.min)
        last.then_inc(me.step("diff"), 1)
        yield 1.5
        dve.wait_ge(pe.sem, pe.after("kt", t))
        kt = self.bank_of("kt")[:, 0:3 * P].rearrange(four, m=3, r=2)
        dve.tensor_tensor(self.kb[:, :, :].rearrange("p m (r d) -> p m r d", r=2), kt, self.by_head(t, 36),
                          ALU.mult).then_inc(me.step("kb"), 1)
        dve.tensor_tensor(self.kd[:, :, :].rearrange("p m (r d) -> p m r d", r=2), kt, self.by_head(t, 42),
                          ALU.mult).then_inc(me.step("kd"), 1)
        dve.wait_ge(pe.sem, pe.after("vt", t))
        dve.tensor_tensor(self.bv[:, :, :].rearrange("p m (r d) -> p m r d", r=2),
                          self.bank_of("vt")[:, 0:3 * P].rearrange(four, m=3, r=2), self.by_head(t, 0),
                          ALU.mult).then_inc(me.step("bv"), 1)
        yield 2.5
        dve.wait_ge(p.sem, p.after("eb", t))
        for name, src, dec, dst in (("at", "kk", self.EB, self.AT), ("qk", "qk", self.E, self.QK)):
            for g, G in enumerate("AB"):
                dve.wait_ge(pe.sem, pe.after(src + G, t))
                at = slice(3 * g, 3 * g + 3)
                dve.tensor_tensor(dst[:, at, :], self.bank_of(src + G)[:, 0:3 * P].rearrange("p (h t) -> p h t", h=3),
                                  dec[:, at, :], ALU.mult).then_inc(me.step(name + G), 1)
            yield 3.5 if name == "at" else 3.7
        dve.wait_ge(p.sem, p.after("l1", t))
        dve.tensor_tensor(self.XT[:, :, :], self.ident[:, None, :].to_broadcast([P, DN_HEADS, P]), self.L[:, 0, :, :],
                          ALU.subtract).then_inc(me.step("t1"), 1)
        yield 6.5
        for n, s in enumerate(LEVELS):
            for g, G in enumerate("AB"):
                at = slice(3 * g, 3 * g + 3)
                for kind in ("x", "t") if s < 64 else ("t",):
                    name = f"{kind}{s}{G}"
                    X = self.X if kind == "x" else self.XT
                    dve.wait_ge(pe.sem, pe.after(name, t))
                    dve.tensor_tensor(X[:, at, :], X[:, at, :],
                                      self.bank_of(name)[:, 0:3 * P].rearrange("p (h t) -> p h t", h=3),
                                      ALU.subtract).then_inc(me.step(name), 1)
                yield 25.5 if name == "t64B" else 7.5 + 3 * n + 2 * g
        m3 = "p (m t) -> p m t"
        dve.wait_ge(pe.sem, pe.after("ws", t))
        dve.wait_ge(a.sem, a.after("u", t))
        dve.tensor_tensor(self.vn[:, :, :], self.U[:, :, :], self.bank_of("ws")[:, 0:3 * P].rearrange(m3, m=3),
                          ALU.subtract).then_inc(me.step("vn"), 1)
        dve.wait_ge(pe.sem, pe.after("o1", t))
        dve.tensor_tensor(self.o[:, :, :].rearrange("p m (r d) -> p m r d", r=2),
                          self.bank_of("o1")[:, 0:3 * P].rearrange(four, m=3, r=2), self.by_head(t, 30),
                          ALU.mult).then_inc(me.step("o1"), 1)
        yield 26.5
        dve.wait_ge(pe.sem, pe.after("o2", t))
        dve.wait_ge(me.sem, me.after("o1", t))
        dve.tensor_tensor(self.o[:, :, :], self.o[:, :, :], self.bank_of("o2")[:, 0:3 * P].rearrange(m3, m=3),
                          ALU.add).then_inc(me.step("o2"), 1)
        dve.wait_ge(pe.sem, pe.after("sn", t))
        dve.wait_ge(p.sem, p.after("sg", t))
        for r in range(2):
            at = slice(r * DH, (r + 1) * DH)
            last = dve.tensor_tensor(self.S[at, :, at], self.Sg[at, :, at],
                                     self.bank_of("sn")[at, 0:3 * P].rearrange(m3, m=3)[:, :, at], ALU.add)
        last.then_inc(me.step("sn"), 1)
        yield 26.8
        dve.wait_ge(p.sem, p.after("osq", t))
        dve.tensor_reduce(self.ssq[:, :], self.osq[:, :, :].rearrange("p m (r d) -> p (m r) d", r=2), AX.X,
                          ALU.add).then_inc(me.step("ssq"), 1)
        yield 27.5
        dve.wait_ge(pe.sem, pe.after("ot", t))
        dve.wait_ge(self.z_in, t * 16 + 16)
        if not isinstance(t, int) or t:
            dve.wait_ge(self.sent, t * 16)
        dve.scalar_tensor_tensor(self.mix[:, :, :], self.bank_of("ot")[:, 0:3 * P].rearrange(m3, m=3), self.nw[:, :],
                                 self.z[:, :, :], ALU.mult, ALU.mult).then_inc(me.step("mix"), 1)


HEADS = [(hh, g) for hh in range(HPG) for g in range(2)]
WK = (WINDOW + P) // P
LOW = -3.0e38


class Nsa:

    RING = 3
    PT_RING = 3

    def __init__(self, sc, banks, outs, consts, proj, gates, kc, vc, vs, ks, vw, kw, mixed, ident):
        self.consts, self.proj, self.gates, self.mixed, self.ident = consts, proj, gates, mixed, ident
        self.kc, self.vc, self.vs, self.ks, self.vw, self.kw = kc, vc, vs, ks, vw, kw
        self.bank, self.out_bank = banks, outs
        sb = sc.sb
        self.q_raw, self.q = sb("q_raw", [P, HPG, P]), sb("q", [P, 6, P])
        self.cp = sb("cp", [P, 6, P])
        self.psum_heads = sb("psum_heads", [P, 2, P + 4])
        self.imp, self.score, self.left, self.selb = (sb(n, [P, 2, N_BLK]) for n in ("imp", "score", "left", "selb"))
        self.top = sb("top", [P, 2, 8])
        self.last_mask = sb("last_mask", [P, 2, NB])
        self.win_mask = sb("win_mask", [P, WINDOW + P])
        self.sx = sb("sx", [P, 2, SEQ])
        self.mx = sb("mx", [P, 2, 4])
        self.nm = sb("nm", [P, 2])
        self.cmx = sb("cmx", [P, 6])
        self.rsum, self.coef = sb("rsum", [P, 3, 6]), sb("coef", [P, 3, 6])
        self.pt = sb("pt", [P, self.PT_RING, NB])
        self.acc, self.part = sb("acc", [P, 6, DH]), sb("part", [P, 6, DH])
        self.mix = sb("mix", [P, 3, P])
        self.seen, self.cbias = sb("seen", [P, 2 * P - 8]), sb("cbias", [P, 2 * P - 8])
        self.elig, self.add = sb("elig", [P, 2 * N_BLK - 2]), sb("add", [P, 2 * N_BLK - 2])
        self.causal, self.band = sb("causal", [P, P]), sb("band", [P, WINDOW + P])
        self.before_start = sb("before_start", [P, WINDOW + SEQ])
        self.c_in, self.q_in, self.sent, self.zeroed = (sc.sem(n) for n in ("c_in", "q_in", "sent", "zeroed"))
        self.stood = sc.sem("stood")
        self.sems = {n: sc.sem(n) for n in ("pe", "dve", "act", "pool")}
        self.spans = []
        base = None
        for s in range(4):
            lists = self.names(s)
            if base is None:
                self.credit = {n: max(len(self.names(z)[n].split()) for z in range(4)) for n in lists}
                base = dict(self.credit)
            span = {n: SpanSteps(self.sems[n], lists[n], base[n]) for n in lists}
            self.spans.append(span)
            base = {n: base[n] + 4 * span[n].count for n in lists}

    def items(self, s):
        win = [(f"w{n}", [4, 1]) for n in range(6)]
        return win + [(f"s{n}", [4] * (s + 1)) for n in range(6)]

    def order(self, s):
        items = self.items(s)
        yield "c", None, 0, 1.4

        def scores(k):
            for c, tiles in enumerate(items[k][1]):
                yield "q", k, c, 0.22 * tiles

        yield from scores(0)
        for k, (_, pieces) in enumerate(items):
            ahead = list(scores(k + 1)) if k + 1 < len(items) else []
            if k == 1:
                yield from ahead
                yield "ct", None, 0, 0.7
                yield "cv", None, 0, 0.7
                ahead = []
            for c, tiles in enumerate(pieces):
                yield "t", k, c, 0.12 * tiles
                if ahead:
                    yield ahead.pop(0)
                if c:
                    yield "v", k, c - 1, 0.12 * pieces[c - 1]
            yield from ahead
            yield "v", k, len(pieces) - 1, 0.12 * pieces[-1]
        yield "end", None, 0, 0.4

    def places(self, s):
        total = sum(e[3] for e in self.order(s))
        at, out = 0.0, {}
        for what, k, c, cost in self.order(s):
            out[what, k, c] = (at / total, cost / total)
            at += cost
        return out

    def names(self, s):
        items = self.items(s)
        pe, act, dve = [], ["ce"], ["c0", "c1", "cx"]
        for what, k, c, _ in self.order(s):
            if what == "c":
                pe += ["c0", "c1"]
            elif what == "ct":
                pe += ["ct0", "ct1"]
                act += ["ct0", "ct1"]
            elif what == "cv":
                pe += ["co"]
                dve += ["ocoef", "oc"]
            elif what == "end":
                pe += ["ot"]
                act += ["ot"]
            else:
                name = f"{items[k][0]}{what}{c}"
                pe += [name]
                if what == "t":
                    act += [name]
                if what == "q":
                    dve += [name]
                    if c == len(items[k][1]) - 1:
                        dve += [items[k][0] + "x"]
                        act += [items[k][0] + "e"]
                        if k == 0:
                            dve += ["cr"]
                        if k == 1:
                            dve += "imp1 imp2 sc1 sc2 sc3 top left ne el selb".split()
                        if k == 8:
                            dve += "rw cw ow aw".split()
        dve += "rs cs os as".split()
        return {"pe": " ".join(pe), "act": " ".join(act), "dve": " ".join(dve), "pool": "qz wm pc1 pc2 hs1 hs2 lm1 lm2"}

    def ring(self, s, name, kind):
        if kind == "bank":
            names = [n for n in self.spans[s]["pe"].names if n != "co" and "v" not in n]
            size = self.RING
        else:
            names = [n for n in self.spans[s]["pe"].names if "t" in n and n != "ot"]
            size = self.PT_RING
        n = names.index(name)
        if n >= size:
            return n % size, names[n - size], False
        return n, names[max(m for m in range(len(names)) if m % size == n)], True

    def bank_of(self, s, name):
        return self.bank[self.ring(s, name, "bank")[0]]

    def pt_of(self, s, name):
        return self.pt[:, self.ring(s, name, "pt")[0], :]

    def wait_bank(self, pe, s, name, t):
        _, old, earlier = self.ring(s, name, "bank")
        who = self.spans[s]["dve" if old in self.spans[s]["dve"].names else "act"]
        pe.wait_ge(who.sem, (who.before if earlier else who.after)(old, t))

    def load(self, sp):
        for dst, name in ((self.seen, "cmp_seen"), (self.cbias, "cmp_bias"), (self.elig, "blk_elig"), (self.add, "blk_add"),
                          (self.causal, "causal"), (self.band, "band"), (self.before_start, "before_start")):
            sp.dma_start(dst[:, :], self.consts[name]).then_inc(self.c_in, 16)

    def start(self, pool):
        pool.memset(self.q[:, :, :], 0.0).then_inc(self.zeroed, 1)
        pool.memset(self.psum_heads[:, :, :], 0.0).then_inc(self.zeroed, 1)
        pool.wait_ge(self.zeroed, 2)
        for n, sem in self.sems.items():
            pool.sem_inc(sem, self.credit[n])

    def join(self, eng, s):
        for who in self.spans[s].values():
            eng.wait_ge(who.sem, who.base)

    def sync(self, sp, s, t):
        pool = self.spans[s]["pool"]
        sp.wait_ge(pool.sem, pool.before("qz", t))
        sp.dma_start(self.q_raw[:, :, :], self.proj[T_NQ:T_NQ + 3, :, bass.ds(t * P + s * 4 * P, P)]
                     .rearrange("m p t -> p m t")).then_inc(self.q_in, 16)

    def send(self, sp, s, t):
        act = self.spans[s]["act"]
        sp.wait_ge(act.sem, act.after("ot", t))
        sp.dma_start(self.mixed[:, 5:8, bass.ds(t * P + s * 4 * P, P)], self.mix[:, :, :]).then_inc(self.sent, 16)

    def tensor(self, pe, s, t):
        span = self.spans[s]
        me, v, a, p = span["pe"], span["dve"], span["act"], span["pool"]
        items = self.items(s)
        places = self.places(s)
        for what, k, c, _ in self.order(s):
            yield places[what, k, c][0]
            if k is not None:
                item, pieces = items[k]
                tiles = pieces[c]
                name = f"{item}{what}{c}"
                hh, g = HEADS[k % 6]
                h = g * HPG + hh
            if what == "c":
                pe.wait_ge(p.sem, p.after("qz", t))
                for n in range(2):
                    self.wait_bank(pe, s, f"c{n}", t)
                    for m in range(3):
                        last = pe.matmul(self.bank_of(s, f"c{n}")[:, m * P:(m + 1) * P], self.q[:, 3 * n + m, :],
                                         self.kc[:, :], start=True, stop=True)
                    last.then_inc(me.step(f"c{n}"), 1)
            elif what == "q":
                self.wait_bank(pe, s, name, t)
                if k < 6:
                    keys = self.kw[:, bass.ds(t * P + (s * 4 * P + c * NB), tiles * P)]
                else:
                    keys = self.ks[:, c * NB:c * NB + tiles * P]
                pe.matmul(self.bank_of(s, name)[:, 0:tiles * P], self.q[:, k % 6, :], keys,
                          start=True, stop=True).then_inc(me.step(name), 1)
            elif what == "ct":
                pe.wait_ge(p.sem, p.after("pc2", t))
                for n in range(2):
                    self.wait_bank(pe, s, f"ct{n}", t)
                    for m in range(3):
                        last = pe.transpose(self.bank_of(s, f"ct{n}")[:, m * P:(m + 1) * P], self.cp[:, 3 * n + m, :],
                                            self.ident[:, :])
                    last.then_inc(me.step(f"ct{n}"), 1)
            elif what == "cv":
                pe.wait_ge(v.sem, v.before("os", t))
                for n in range(6):
                    hh, g = HEADS[n]
                    if n % 3 == 0:
                        pe.wait_ge(a.sem, a.after(f"ct{n // 3}", t))
                    h = g * HPG + hh
                    last = pe.matmul(self.out_bank[0][:, h * DH:(h + 1) * DH],
                                     self.pt_of(s, f"ct{n // 3}")[:, (n % 3) * P:(n % 3 + 1) * P],
                                     self.vc[:, g * DH:(g + 1) * DH], start=True, stop=True)
                last.then_inc(me.step("co"), 1)
            elif what == "t":
                if c == 0:
                    pe.wait_ge(a.sem, a.after(item + "e", t))
                self.wait_bank(pe, s, name, t)
                for m in range(tiles):
                    at = c * NB + m * P
                    last = pe.transpose(self.bank_of(s, name)[:, m * P:(m + 1) * P], self.sx[:, k % 2, at:at + P],
                                        self.ident[:, :])
                last.then_inc(me.step(name), 1)
            elif what == "v":
                if k == 0 and c == 0:
                    pe.wait_ge(v.sem, v.before("ow", t))
                if k == 6 and c == 0:
                    pe.wait_ge(v.sem, v.after("oc", t))
                pe.wait_ge(a.sem, a.after(f"{item}t{c}", t))
                for m in range(tiles):
                    kt = 4 * c + m
                    if k < 6:
                        vals = self.vw[:, bass.ds(t + (4 * s + kt), 1), g * DH:(g + 1) * DH].rearrange("p a d -> p (a d)")
                    else:
                        vals = self.vs[:, kt, g * DH:(g + 1) * DH]
                    last = pe.matmul(self.out_bank[1 if k < 6 else 0][:, h * DH:(h + 1) * DH],
                                     self.pt_of(s, f"{item}t{c}")[:, m * P:(m + 1) * P], vals,
                                     start=kt == 0, stop=kt == sum(pieces) - 1)
                last.then_inc(me.step(name), 1)
            else:
                pe.wait_ge(v.sem, v.after("as", t))
                self.wait_bank(pe, s, "ot", t)
                for m in range(3):
                    last = pe.transpose(self.bank_of(s, "ot")[:, m * P:(m + 1) * P],
                                        self.acc[:, 2 * m:2 * m + 2, :].rearrange("p h d -> p (h d)"), self.ident[:, :])
                last.then_inc(me.step("ot"), 1)

    def scalar(self, act, s, t):
        span = self.spans[s]
        me, v, pe, p = span["act"], span["dve"], span["pe"], span["pool"]
        items = self.items(s)

        def take(name):
            _, old, earlier = self.ring(s, name, "pt")
            old = "co" if old[0] == "c" else old.replace("t", "v")
            act.wait_ge(pe.sem, (pe.before if earlier else pe.after)(old, t))
            act.wait_ge(pe.sem, pe.after(name, t))
            tiles = 3 if name[0] == "c" else 1 if name[0] == "w" and name[-1] == "1" else 4
            act.activation(self.pt_of(s, name)[:, 0:tiles * P], self.bank_of(s, name)[:, 0:tiles * P],
                           ACT.Copy).then_inc(me.step(name), 1)

        places = self.places(s)

        def place(what, k, c, into):
            at, cost = places[what, k, c]
            return at + into * cost

        yield place("c", None, 0, 0.7)
        act.wait_ge(v.sem, v.after("cx", t))
        for n in range(6):
            hh, g = HEADS[n]
            last = act.activation(self.cp[:, n, :], self.cp[:, n, :], ACT.Exp, bias=self.cmx[:, n:n + 1],
                                  accum_out=self.rsum[:, 0, g * HPG + hh:g * HPG + hh + 1])
        last.then_inc(me.step("ce"), 1)
        for what, k, c, _ in self.order(s):
            if what == "q" and c == len(items[k][1]) - 1:
                yield place(what, k, c, 0.7)
                item, pieces = items[k]
                hh, g = HEADS[k % 6]
                h = g * HPG + hh
                width = sum(pieces) * P
                act.wait_ge(v.sem, v.after(item + "x", t))
                if k == 0:
                    act.wait_ge(v.sem, v.before("rw", t))
                if k == 6:
                    act.wait_ge(v.sem, v.before("rs", t))
                act.activation(self.sx[:, k % 2, 0:width], self.sx[:, k % 2, 0:width], ACT.Exp,
                               bias=self.nm[:, k % 2:k % 2 + 1],
                               accum_out=self.rsum[:, 1 if k < 6 else 2, h:h + 1]).then_inc(me.step(item + "e"), 1)
            elif what == "ct":
                yield place(what, k, c, 0.5)
                take("ct0")
                take("ct1")
            elif what == "t":
                yield place(what, k, c, 0.5)
                take(f"{items[k][0]}t{c}")
            elif what == "end":
                yield place(what, k, c, 0.9)
                act.wait_ge(pe.sem, pe.after("ot", t))
                act.wait_ge(self.sent, t * 16 + s * 64)
                act.activation(self.mix[:, :, :], self.bank_of(s, "ot")[:, 0:3 * P].rearrange("p (m t) -> p m t", m=3),
                               ACT.Copy).then_inc(me.step("ot"), 1)

    def gpsimd(self, pool, s, t):
        span = self.spans[s]
        me, v, pe, a = span["pool"], span["dve"], span["pe"], span["act"]
        places = self.places(s)
        yield 0.0
        pool.wait_ge(self.q_in, t * 16 + (64 * s + 16))
        pool.wait_ge(pe.sem, pe.before(f"s5q{s}", t))
        for g in range(2):
            at = slice(g * DH, (g + 1) * DH)
            if g:
                pool.wait_ge(me.sem, me.before("lm2", t))
            alone(pool, self.stood)
            last = pool.tensor_scalar(self.q[at, g:6:2, :], self.q_raw[at, :, :], DH ** -0.5, 1.0, ALU.mult, ALU.mult)
            if g == 0:
                last.then_inc(self.zeroed, 1)
                pool.wait_ge(self.zeroed, t + (4 * s + 3))
        last.then_inc(me.step("qz"), 1)
        pool.wait_ge(me.sem, me.after("qz", t))
        pool.wait_ge(v.sem, v.before("w5q1", t))
        pool.tensor_tensor(self.win_mask[:, :], self.band[:, :], self.before_start[:, bass.ds(t * P + s * 4 * P, WINDOW + P)],
                           ALU.add).then_inc(me.step("wm"), 1)
        at, cost = places["q", 0, 1]
        yield at + 0.7 * cost
        pool.wait_ge(v.sem, v.after("cr", t))
        rinv = self.coef[:, 0, :].rearrange("p (g m) -> p m g", g=2)[:, :, :, None].to_broadcast([P, HPG, 2, P])
        cp = self.cp[:, :, :].rearrange("p (m g) n -> p m g n", g=2)
        pool.tensor_tensor(cp, cp, rinv, ALU.mult).then_inc(me.step("pc1"), 1)
        pool.wait_ge(me.sem, me.after("pc1", t))
        seen = self.seen[:, bass.ds(t * -8 + (P - 8 - 32 * s), P)]
        pool.tensor_tensor(self.cp[:, :, :], self.cp[:, :, :], seen[:, None, :].to_broadcast([P, 6, P]),
                           ALU.mult).then_inc(me.step("pc2"), 1)
        pool.wait_ge(me.sem, me.after("pc2", t))
        pool.wait_ge(v.sem, v.before("imp2", t))
        pool.tensor_tensor(self.psum_heads[:, :, 1:1 + P], self.cp[:, 0:2, :], self.cp[:, 2:4, :],
                           ALU.add).then_inc(me.step("hs1"), 1)
        pool.wait_ge(me.sem, me.after("hs1", t))
        pool.tensor_tensor(self.psum_heads[:, :, 1:1 + P], self.psum_heads[:, :, 1:1 + P], self.cp[:, 4:6, :],
                           ALU.add).then_inc(me.step("hs2"), 1)
        at, cost = places["q", 1, 1]
        yield at + 0.7 * cost
        pool.wait_ge(v.sem, v.after("selb", t))
        blocks = self.selb[:, :, 8 * s:8 * s + 8]
        pool.wait_ge(v.sem, v.before(f"s5q{s}", t))
        alone(pool, self.stood)
        pool.tensor_copy(self.last_mask[:, :, :].rearrange("p g (b k) -> p g b k", k=SEL_BLOCK),
                         blocks[:, :, :, None].to_broadcast([P, 2, 8, SEL_BLOCK])).then_inc(me.step("lm1"), 1)
        pool.wait_ge(me.sem, me.after("lm1", t))
        diag = self.last_mask[:, :, bass.ds(t * P, P)]
        pool.tensor_tensor(diag, diag, self.causal[:, None, :].to_broadcast([P, 2, P]), ALU.add).then_inc(me.step("lm2"), 1)

    def vector(self, dve, s, t):
        span = self.spans[s]
        me, pe, a, p = span["dve"], span["pe"], span["act"], span["pool"]
        items = self.items(s)
        places = self.places(s)

        def place(what, k, c, into):
            at, cost = places[what, k, c]
            return at + into * cost

        yield place("c", None, 0, 0.5)
        cbias = self.cbias[:, bass.ds(t * -8 + (P - 8 - 32 * s), P)]
        dve.wait_ge(pe.sem, pe.before("ct1", t))
        for n in range(2):
            dve.wait_ge(pe.sem, pe.after(f"c{n}", t))
            dve.tensor_tensor(self.cp[:, 3 * n:3 * n + 3, :],
                              self.bank_of(s, f"c{n}")[:, 0:3 * P].rearrange("p (h n) -> p h n", h=3),
                              cbias[:, None, :].to_broadcast([P, 3, P]), ALU.add).then_inc(me.step(f"c{n}"), 1)
        dve.wait_ge(me.sem, me.after("c1", t))
        dve.tensor_reduce(self.cmx[:, :], self.cp[:, :, :], AX.X, ALU.max, negate=True).then_inc(me.step("cx"), 1)

        def masked(k):
            yield place("q", k, 0, 0.5)
            item, pieces = items[k]
            g = HEADS[k % 6][1]
            if k < 2:
                dve.wait_ge(pe.sem, pe.before(f"s{k + 4}t{s}", t))
            else:
                old = items[k - 2]
                dve.wait_ge(pe.sem, pe.after(f"{old[0]}t{len(old[1]) - 1}", t))
            if k == 0:
                dve.wait_ge(p.sem, p.after("wm", t))
            if k == 6:
                dve.wait_ge(p.sem, p.after("lm2", t))
            for c, tiles in enumerate(pieces):
                if c:
                    yield place("q", k, c, 0.5)
                w = tiles * P
                dve.wait_ge(pe.sem, pe.after(f"{item}q{c}", t))
                out, src = self.sx[:, k % 2, c * NB:c * NB + w], self.bank_of(s, f"{item}q{c}")[:, 0:w]
                if k < 6:
                    mask = self.win_mask[:, c * NB:c * NB + w]
                elif c == s:
                    mask = self.last_mask[:, g, :]
                else:
                    out, src = (x.rearrange("p (b k) -> p b k", k=SEL_BLOCK) for x in (out, src))
                    mask = self.selb[:, g, 8 * c:8 * c + 8][:, :, None].to_broadcast([P, 8, SEL_BLOCK])
                alone(dve, self.stood)
                dve.tensor_tensor_reduce(out, src, mask, 1.0, LOW, ALU.add, ALU.max,
                                         self.mx[:, k % 2, c:c + 1]).then_inc(me.step(f"{item}q{c}"), 1)
            dve.wait_ge(me.sem, me.after(f"{item}q{len(pieces) - 1}", t))
            if k < 2:
                dve.wait_ge(a.sem, a.before(f"s{k + 4}e", t))
            else:
                dve.wait_ge(a.sem, a.after(items[k - 2][0] + "e", t))
            dve.tensor_reduce(self.nm[:, k % 2:k % 2 + 1], self.mx[:, k % 2, 0:len(pieces)], AX.X, ALU.max,
                              negate=True).then_inc(me.step(item + "x"), 1)

        def gated(branch, names, bank):
            recip, mul, out, add = names
            at = 12 + 6 * (3 - branch)
            gate = self.gates[:, bass.ds(t + 4 * s, 1), at:at + 6].rearrange("p a h -> p (a h)")
            dve.reciprocal(self.coef[:, branch, :], self.rsum[:, branch, :]).then_inc(me.step(recip), 1)
            dve.wait_ge(me.sem, me.after(recip, t))
            dve.tensor_tensor(self.coef[:, branch, :], self.coef[:, branch, :], gate, ALU.mult).then_inc(me.step(mul), 1)
            dve.wait_ge(me.sem, me.after(mul, t))
            dve.tensor_tensor(self.part[:, :, :], bank[:, 0:6 * DH].rearrange("p (h d) -> p h d", h=6),
                              self.coef[:, branch, :, None].to_broadcast([P, 6, DH]), ALU.mult).then_inc(me.step(out), 1)
            dve.wait_ge(me.sem, me.after(out, t))
            dve.tensor_tensor(self.acc[:, :, :], self.acc[:, :, :], self.part[:, :, :], ALU.add).then_inc(me.step(add), 1)

        def compressed_out():
            yield place("cv", None, 0, 0.9)
            gate = self.gates[:, bass.ds(t + 4 * s, 1), 12:18].rearrange("p a h -> p (a h)")
            dve.tensor_copy(self.cmx[:, :], gate).then_inc(me.step("ocoef"), 1)
            dve.wait_ge(me.sem, me.after("ocoef", t))
            dve.wait_ge(pe.sem, pe.after("co", t))
            dve.wait_ge(pe.sem, pe.before("ot", t))
            dve.tensor_tensor(self.acc[:, :, :], self.out_bank[0][:, 0:6 * DH].rearrange("p (h d) -> p h d", h=6),
                              self.cmx[:, :, None].to_broadcast([P, 6, DH]), ALU.mult).then_inc(me.step("oc"), 1)

        for k in range(12):
            yield from masked(k)
            if k == 0:
                dve.wait_ge(a.sem, a.after("ce", t))
                dve.reciprocal(self.coef[:, 0, :], self.rsum[:, 0, :]).then_inc(me.step("cr"), 1)
            if k == 1:
                yield place("q", 1, 1, 0.7)
                dve.wait_ge(p.sem, p.after("hs2", t))
                four = self.psum_heads[:, :, 0:P].rearrange("p g (b i) -> p g b i", i=4)
                dve.tensor_reduce(self.imp[:, :, :], four, AX.X, ALU.add).then_inc(me.step("imp1"), 1)
                dve.wait_ge(me.sem, me.after("imp1", t))
                fifth = self.psum_heads[:, :, 4:P + 4].rearrange("p g (b i) -> p g b i", i=4)[:, :, :, 0]
                dve.tensor_tensor(self.imp[:, :, :], self.imp[:, :, :], fifth, ALU.add).then_inc(me.step("imp2"), 1)
                both = [P, 2, N_BLK]
                elig = self.elig[:, bass.ds(t * -2 + (N_BLK - 2 - 8 * s), N_BLK)][:, None, :].to_broadcast(both)
                add = self.add[:, bass.ds(t * -2 + (N_BLK - 2 - 8 * s), N_BLK)][:, None, :].to_broadcast(both)
                dve.wait_ge(me.sem, me.after("imp2", t))
                dve.tensor_tensor(self.score[:, :, :], self.imp[:, :, :], elig, ALU.mult).then_inc(me.step("sc1"), 1)
                dve.wait_ge(me.sem, me.after("sc1", t))
                dve.tensor_tensor(self.score[:, :, :], self.score[:, :, :], add, ALU.add).then_inc(me.step("sc2"), 1)
                dve.wait_ge(me.sem, me.after("sc2", t))
                dve.tensor_scalar(self.score[:, :, 0:1], self.score[:, :, 0:1], SEL_BIG, None, ALU.add).then_inc(me.step("sc3"), 1)
                dve.wait_ge(me.sem, me.after("sc3", t))
                alone(dve, self.stood)
                for g in range(2):
                    last = dve.max(self.top[:, g, :], self.score[:, g, :])
                last.then_inc(me.step("top"), 1)
                dve.wait_ge(me.sem, me.after("top", t))
                alone(dve, self.stood)
                for g in range(2):
                    last = dve.match_replace(self.left[:, g, :], self.top[:, g, :], self.score[:, g, :], LOW)
                last.then_inc(me.step("left"), 1)
                dve.wait_ge(me.sem, me.after("left", t))
                dve.tensor_tensor(self.left[:, :, :], self.left[:, :, :], self.score[:, :, :],
                                  ALU.not_equal).then_inc(me.step("ne"), 1)
                dve.wait_ge(me.sem, me.after("ne", t))
                dve.tensor_tensor(self.left[:, :, :], self.left[:, :, :], elig, ALU.mult).then_inc(me.step("el"), 1)
                dve.wait_ge(me.sem, me.after("el", t))
                dve.wait_ge(p.sem, p.before("lm1", t))
                dve.tensor_scalar(self.selb[:, :, :], self.left[:, :, :], -NEG, NEG, ALU.mult, ALU.add).then_inc(me.step("selb"), 1)
            if k == 2:
                yield from compressed_out()
            if k == 8:
                yield place("q", 8, s, 0.6)
                dve.wait_ge(pe.sem, pe.after("w5v1", t))
                gated(1, ("rw", "cw", "ow", "aw"), self.out_bank[1])
        yield place("v", 11, s, 0.9)
        dve.wait_ge(pe.sem, pe.after(f"s5v{s}", t))
        gated(2, ("rs", "cs", "os", "as"), self.out_bank[0])


class SpanSteps(Steps):

    def __init__(self, sem, names, base):
        super().__init__(sem, names)
        self.base = base

    def after(self, name, t):
        return t * self.count + (self.base + self.names.index(name) + 1)

    def before(self, name, t):
        return t * self.count + (self.base - self.count + self.names.index(name) + 1)


def weave(parts):
    heads = [[next(g) / size, n, g, size] for n, (g, size) in enumerate(parts)]
    while heads:
        head = min(heads, key=lambda h: h[:2])
        at = next(head[2], None)
        if at is None:
            heads.remove(head)
        else:
            assert at / head[3] >= head[0] - 1e-9, (at, head)
            head[0] = at / head[3]


def mix_tokens(nc, consts, prm, proj, rows, gates, kv, mixed, ident):
    with ExitStack() as ctx:
        sc = Scope(nc, ctx, "mixer")
        banks = [sc.ps(f"bank{n}", [P, NB]) for n in range(8)]
        dn = DeltaNet(Scope(nc, ctx, "dn"), banks[0:3], consts, prm, proj, rows, gates, mixed, ident)
        nsa = Nsa(Scope(nc, ctx, "nsa"), banks[3:6], banks[6:8], consts, proj, gates, *kv, mixed, ident)
        block = ctx.enter_context(nc.Block())

        def tiles(eng, dn_part, nsa_part):
            for s in range(4):
                nsa.join(eng, s)
                with eng.Fori(0, 4) as t:
                    weave([(dn_part(eng, t + 4 * s), DeltaNet.PLACES), (nsa_part(eng, s, t), 1)])

        @block.sync
        def _(sp):
            dn.start(sp, None)
            nsa.load(sp)
            sp.wait_ge(dn.ready, 2)
            for s in range(4):
                nsa.join(sp, s)
                with sp.Fori(0, 4) as t:
                    dn.sync(sp, t + 4 * s)
                    nsa.sync(sp, s, t)
                    dn.send(sp, t + 4 * s)
                    nsa.send(sp, s, t)
            sp.wait_ge(dn.sent, 16 * NT)
            sp.wait_ge(nsa.sent, 16 * NT)

        @block.gpsimd
        def _(pool):
            dn.start(None, pool)
            nsa.start(pool)
            pool.wait_ge(dn.c_in, 64)
            pool.wait_ge(nsa.c_in, 16 * 7)
            tiles(pool, dn.gpsimd, nsa.gpsimd)

        @block.scalar
        def _(act):
            act.preload_act_table_set(LOG_EXP)
            act.wait_ge(dn.ready, 2)
            tiles(act, dn.scalar, nsa.scalar)

        @block.vector
        def _(dve):
            dve.wait_ge(dn.c_in, 64)
            dve.wait_ge(nsa.c_in, 16 * 7)
            tiles(dve, dn.vector, nsa.vector)

        @block.tensor
        def _(pe):
            pe.wait_ge(dn.c_in, 64)
            tiles(pe, dn.tensor, nsa.tensor)


FP = FT // 2


def mix_out(nc, prm, x, mixed, x_mid, h_mid, ident):
    with ExitStack() as ctx:
        sc = Scope(nc, ctx, "out")
        w_raw = sc.sb("w_raw", [P, 2, D_MODEL])
        w_hi, w_lo = sc.sb("w_hi", [P, KT, D_MODEL], F32R), sc.sb("w_lo", [P, KT, D_MODEL], F32R)
        m_raw, xt = sc.sb("m_raw", [P, 2, D_MODEL]), sc.sb("xt", [P, 2, D_MODEL])
        m_hi, m_lo = sc.sb("m_hi", [P, 2, D_MODEL], F32R), sc.sb("m_lo", [P, 2, D_MODEL], F32R)
        sq = sc.sb("sq", [P, D_MODEL])
        y, hn, turned = sc.sb("y", [P, 2, D_MODEL]), sc.sb("hn", [P, 2, D_MODEL]), sc.sb("turned", [P, 2, D_MODEL])
        w_post, w_pre = sc.sb("w_post", [P, D_MODEL]), sc.sb("w_pre", [P, D_MODEL])
        eps = sc.sb("eps", [P, 1])
        ssq, rstd = sc.sb("ssq", [P, 2, 4]), sc.sb("rstd", [P, 2, 2])
        acc = [[sc.ps(f"acc{b}{g}", [P, NB]) for g in range(2)] for b in range(2)]
        tp = [[sc.ps(f"tp{b}{g}", [P, NB]) for g in range(2)] for b in range(2)]
        w_in = [sc.sem(f"w_in{b}") for b in range(2)]
        m_in, x_in, y_sent, h_sent = ([sc.sem(f"{n}{b}") for b in range(2)] for n in ("m_in", "x_in", "y_sent", "h_sent"))
        (c_in, ready, whi, wlo, m_split_hi, m_split_lo, summed, squared, ssum, rooted, scaled, added, squared2, rooted2,
         normed, turn_done, taken) = (sc.sem(n) for n in (
             "c_in ready whi wlo m_split_hi m_split_lo summed squared ssum rooted scaled added squared2 rooted2 normed "
             "turn_done taken").split())
        block = ctx.enter_context(nc.Block())
        PAIRS = NT // 2
        m3 = "p (k t) -> p k t"

        @block.sync
        def _(sp):
            sp.dma_start(w_post[:, :], prm["w_post_mix"].partition_broadcast(P)).then_inc(c_in, 16)
            sp.dma_start(w_pre[:, :], prm["w_pre_ffn"].partition_broadcast(P)).then_inc(c_in, 16)
            for b in range(2):
                sp.dma_start(m_raw[:, b, :].rearrange(m3, k=KT), mixed[:, :, b * P:(b + 1) * P]).then_inc(m_in[b], 16)
                sp.dma_start(xt[:, b, :], x[b * P:(b + 1) * P, :]).then_inc(x_in[b], 16)
            for k in range(KT):
                if k >= 2:
                    sp.wait_ge(wlo, k - 1)
                sp.dma_start(w_raw[:, k % 2, :], prm["w_out"][k * P:(k + 1) * P, :]).then_inc(w_in[k % 2], 16)
            with sp.Fori(1, PAIRS) as i:
                for b in range(2):
                    sp.wait_ge(m_split_lo, i * 2 + (b - 1))
                    sp.dma_start(m_raw[:, b, :].rearrange(m3, k=KT),
                                 mixed[:, :, bass.ds(i * (2 * P) + b * P, P)]).then_inc(m_in[b], 16)
                for b in range(2):
                    sp.wait_ge(added, i * 4 + (2 * b - 2))
                    sp.dma_start(xt[:, b, :], x[bass.ds(i * (2 * P) + b * P, P), :]).then_inc(x_in[b], 16)

        @block.gpsimd
        def _(pool):
            pool.memset(eps[:, :], EPS).then_inc(ready, 1)
            for k in range(KT):
                pool.wait_ge(whi, k + 1)
                pool.tensor_tensor(w_lo[:, k, :], w_raw[:, k % 2, :], w_hi[:, k, :].bitcast(F32), ALU.subtract).then_inc(wlo, 1)
            with pool.Fori(0, PAIRS) as i:
                for b in range(2):
                    pool.wait_ge(added, i * 4 + (2 * b + 2))
                    pool.dma_start(x_mid[bass.ds(i * (2 * P) + b * P, P), :], y[:, b, :]).then_inc(y_sent[b], 16)
                    pool.wait_ge(taken, i * 4 + (2 * b + 2))
                    pool.dma_start(h_mid[:, :, bass.ds(i * (2 * P) + b * P, P)],
                                   turned[:, b, :].rearrange(m3, k=KT)).then_inc(h_sent[b], 16)
            for b in range(2):
                pool.wait_ge(y_sent[b], 16 * PAIRS)
                pool.wait_ge(h_sent[b], 16 * PAIRS)

        def rsqrt(eng, dst, src, sem, n):
            eng.activation(dst, src, ACT.Ln, bias=eps[:, :], scale=1.0 / D_MODEL).then_inc(sem, 1)
            eng.wait_ge(sem, n + 1)
            eng.activation(dst, dst, ACT.Exp, scale=-0.5).then_inc(sem, 1)

        @block.scalar
        def _(act):
            act.preload_act_table_set(LOG_EXP)
            for k in range(KT):
                act.wait_ge(w_in[k % 2], 16 * (k // 2 + 1))
                act.activation(w_hi[:, k, :], w_raw[:, k % 2, :], ACT.Copy).then_inc(whi, 1)
            act.wait_ge(ready, 1)

            def split(i, b, first=False):
                act.wait_ge(m_in[b], i * 16 + 16)
                if not first:
                    act.wait_ge(summed, i * 4 + (2 * b - 2))
                act.activation(m_hi[:, b, :], m_raw[:, b, :], ACT.Copy).then_inc(m_split_hi, 1)

            def norms(i, b, last=False):
                for g in range(2):
                    act.wait_ge(summed, i * 4 + (2 * b + g + 1))
                    if g == 0:
                        act.wait_ge(squared2, i * 2 + b)
                    act.activation(sq[:, g * NB:(g + 1) * NB], acc[b][g][:, :], ACT.Square,
                                   accum_out=ssq[:, b, g:g + 1]).then_inc(squared, 1)
                act.wait_ge(ssum, i * 2 + b + 1)
                rsqrt(act, rstd[:, b, 0:1], ssq[:, b, 2:3], rooted, i * 4 + 2 * b)
                if not last:
                    split(i + 1, b)
                act.wait_ge(added, i * 4 + (2 * b + 2))
                act.activation(sq[:, :], y[:, b, :], ACT.Square, accum_out=ssq[:, b, 3:4]).then_inc(squared2, 1)
                act.wait_ge(squared2, i * 2 + b + 1)
                rsqrt(act, rstd[:, b, 1:2], ssq[:, b, 3:4], rooted2, i * 4 + 2 * b)

            def take(i, b):
                for g in range(2):
                    act.wait_ge(turn_done, i * 4 + (2 * b + g + 1))
                    if g == 0:
                        act.wait_ge(h_sent[b], i * 16)
                    act.activation(turned[:, b, g * NB:(g + 1) * NB], tp[b][g][:, :], ACT.Copy).then_inc(taken, 1)

            split(0, 0, True)
            split(0, 1, True)
            norms(0, 0)
            norms(0, 1)
            take(0, 0)
            with act.Fori(1, PAIRS - 1) as i:
                norms(i, 0)
                take(i - 1, 1)
                norms(i, 1)
                take(i, 0)
            norms(PAIRS - 1, 0, last=True)
            take(PAIRS - 2, 1)
            norms(PAIRS - 1, 1, last=True)
            take(PAIRS - 1, 0)
            take(PAIRS - 1, 1)

        @block.vector
        def _(dve):
            dve.wait_ge(c_in, 32)

            def split(i, b, first=False):
                dve.wait_ge(m_split_hi, i * 2 + b + 1)
                if not first:
                    dve.wait_ge(summed, i * 4 + (2 * b - 2))
                dve.tensor_tensor(m_lo[:, b, :], m_raw[:, b, :], m_hi[:, b, :].bitcast(F32), ALU.subtract).then_inc(m_split_lo, 1)

            def norms(i, b, last=False):
                dve.wait_ge(squared, i * 4 + (2 * b + 2))
                dve.tensor_tensor(ssq[:, b, 2:3], ssq[:, b, 0:1], ssq[:, b, 1:2], ALU.add).then_inc(ssum, 1)
                dve.wait_ge(rooted, i * 4 + (2 * b + 2))
                dve.wait_ge(y_sent[b], i * 16)
                for g in range(2):
                    at = slice(g * NB, (g + 1) * NB)
                    dve.scalar_tensor_tensor(y[:, b, at], acc[b][g][:, :], rstd[:, b, 0:1], w_post[:, at],
                                             ALU.mult, ALU.mult).then_inc(scaled, 1)
                dve.wait_ge(x_in[b], i * 16 + 16)
                for g in range(2):
                    at = slice(g * NB, (g + 1) * NB)
                    dve.wait_ge(scaled, i * 4 + (2 * b + g + 1))
                    dve.tensor_tensor(y[:, b, at], y[:, b, at], xt[:, b, at], ALU.add).then_inc(added, 1)
                if not last:
                    split(i + 1, b)
                dve.wait_ge(rooted2, i * 4 + (2 * b + 2))
                if not isinstance(i, int) or i:
                    dve.wait_ge(turn_done, i * 4 + (2 * b - 2))
                dve.scalar_tensor_tensor(hn[:, b, :], y[:, b, :], rstd[:, b, 1:2], w_pre[:, :],
                                         ALU.mult, ALU.mult).then_inc(normed, 1)

            split(0, 0, True)
            split(0, 1, True)
            for b in range(2):
                norms(0, b)
            with dve.Fori(1, PAIRS - 1) as i:
                for b in range(2):
                    norms(i, b)
            for b in range(2):
                norms(PAIRS - 1, b, last=True)

        @block.tensor
        def _(pe):
            pe.wait_ge(wlo, KT)

            def products(i, b, first=False):
                pe.wait_ge(m_split_lo, i * 2 + b + 1)
                if not first:
                    pe.wait_ge(scaled, i * 4 + (2 * b - 2))
                for g in range(2):
                    for k in range(KT):
                        at = slice(k * P, (k + 1) * P)
                        last = mm3(pe, acc[b][g][:, :], m_hi[:, b, at], m_lo[:, b, at], w_hi[:, k, g * NB:(g + 1) * NB],
                                   w_lo[:, k, g * NB:(g + 1) * NB], k == 0, k == KT - 1)
                    last.then_inc(summed, 1)

            def turns(i, b, first=False):
                pe.wait_ge(normed, i * 2 + b + 1)
                for g in range(2):
                    if not first:
                        pe.wait_ge(taken, i * 4 + (2 * b + g - 3))
                    for k in range(4):
                        last = pe.transpose(tp[b][g][:, k * P:(k + 1) * P], hn[:, b, (4 * g + k) * P:(4 * g + k + 1) * P],
                                            ident[:, :])
                    last.then_inc(turn_done, 1)

            products(0, 0, True)
            products(0, 1, True)
            products(1, 0)
            turns(0, 0, True)
            products(1, 1)
            turns(0, 1, True)
            with pe.Fori(2, PAIRS) as i:
                for b in range(2):
                    products(i, b)
                    turns(i - 1, b)
            for b in range(2):
                turns(PAIRS - 1, b)


def feed_forward(nc, prm, x_mid, h_mid, out):
    with ExitStack() as ctx:
        sc = Scope(nc, ctx, "ffn")
        gu_raw = sc.sb("gu_raw", [P, 2, KT * 2 * P])
        gu_hi, gu_lo = sc.sb("gu_hi", [P, 2, KT * 2 * P], F32R), sc.sb("gu_lo", [P, 2, KT * 2 * P], F32R)
        d_raw = sc.sb("d_raw", [P, 2, D_MODEL])
        d_hi, d_lo = sc.sb("d_hi", [P, 2, D_MODEL], F32R), sc.sb("d_lo", [P, 2, D_MODEL], F32R)
        h_raw = sc.sb("h_raw", [P, 2, 2, NB])
        h_hi, h_lo = sc.sb("h_hi", [P, KT, NB], F32R), sc.sb("h_lo", [P, KT, NB], F32R)
        sg = sc.sb("sg", [P, 2, NB])
        a = sc.sb("a", [P, FT, NB])
        a_hi, a_lo = sc.sb("a_hi", [P, 2, NB], F32R), sc.sb("a_lo", [P, 2, NB], F32R)
        f = sc.sb("f", [P, 4, D_MODEL])
        xm = sc.sb("xm", [P, 2, D_MODEL])
        sq = sc.sb("sq", [P, D_MODEL])
        w_post = sc.sb("w_post", [P, D_MODEL])
        eps, ssq, rstd = sc.sb("eps", [P, 1]), sc.sb("ssq", [P, 4]), sc.sb("rstd", [P, 4])
        bank = [sc.ps(f"bank{n}", [P, NB]) for n in range(8)]
        gu_in, d_in, h_in, x_in, out_sent = ([sc.sem(f"{n}{b}") for b in range(2)] for n in
                                             ("gu_in", "d_in", "h_in", "x_in", "out_sent"))
        (c_in, ready, gu_hi_d, gu_lo_d, h_hi_d, h_lo_d, gate_up, silu_d, a_d, d_hi_d, d_lo_d, a_hi_d, a_lo_d, down,
         drained, f_v, f_s, sq_d, rooted, scaled, added, stood) = (sc.sem(n) for n in (
             "c_in ready gu_hi_d gu_lo_d h_hi_d h_lo_d gate_up silu_d a_d d_hi_d d_lo_d a_hi_d a_lo_d down "
             "drained f_v f_s sq_d rooted scaled added stood").split())
        block = ctx.enter_context(nc.Block())
        blk = "p (k t) -> p k t"

        @block.sync
        def _(sp):
            sp.dma_start(w_post[:, :], prm["w_post_ffn"].partition_broadcast(P)).then_inc(c_in, 16)

            def load_h(i, n):
                if not (isinstance(i, int) and n < 2):
                    sp.wait_ge(h_lo_d, i * 4 + (n - 1))
                sp.dma_start(h_raw[:, n % 2, :, :], h_mid[:, 2 * n:2 * n + 2, bass.ds((i % TB) * NB, NB)]).then_inc(h_in[n % 2], 16)

            def load_gu(j, i, b, first=False):
                if not first:
                    sp.wait_ge(gu_lo_d, i * FT + j * 2 + (b - 1))
                sp.dma_start(gu_raw[:, b, :], prm["w_gate_up"][j * 2 + b]).then_inc(gu_in[b], 16)

            def load_d(j, i, b):
                sp.wait_ge(d_lo_d, i * FT + j * 2 + (b + 1))
                sp.dma_start(d_raw[:, b, :], prm["w_down"][j * 2 + b]).then_inc(d_in[b], 16)

            load_gu(0, 0, 0, True)
            for n in range(4):
                load_h(0, n)
                if n == 1:
                    load_gu(0, 0, 1, True)
            with sp.Fori(0, TB) as i:
                with sp.Fori(1, FP) as j:
                    for b in range(2):
                        load_gu(j, i, b)
                for b in range(2):
                    load_d(0, i, b)
                for n in range(4):
                    sp.wait_ge(h_lo_d, i * 4 + (n + 3))
                    sp.dma_start(h_raw[:, n % 2, :, :],
                                 h_mid[:, 2 * n:2 * n + 2, bass.ds((i + 1) % TB * NB, NB)]).then_inc(h_in[n % 2], 16)
                with sp.Fori(1, FP) as j:
                    for b in range(2):
                        load_d(j, i, b)
                for b in range(2):
                    sp.wait_ge(gu_lo_d, i * FT + (FT + b - 1))
                    sp.dma_start(gu_raw[:, b, :], prm["w_gate_up"][b]).then_inc(gu_in[b], 16)
                for n in range(4):
                    b = n % 2
                    sp.wait_ge(added, i * 4 + (n + 1))
                    sp.dma_start(xm[:, b, :], x_mid[bass.ds(i * NB + n * P, P), :]).then_inc(x_in[b], 16)
                for n in range(4):
                    sp.wait_ge(added, i * 4 + (n + 3))
                    sp.dma_start(out[bass.ds(i * NB + n * P, P), :], f[:, n, :]).then_inc(out_sent[0], 16)
            for b in range(2):
                sp.wait_ge(gu_in[b], 16 * (TB * FP + 1))
                sp.wait_ge(h_in[b], 16 * (2 * TB + 2))
            sp.wait_ge(out_sent[0], 16 * 4 * TB)

        @block.gpsimd
        def _(pool):
            pool.memset(eps[:, :], EPS).then_inc(ready, 1)
            pool.sem_inc(d_lo_d, 2)
            pool.sem_inc(added, 2)
            with pool.Fori(0, TB) as i:
                with pool.Fori(0, FP) as j:
                    for b in range(2):
                        pool.wait_ge(gu_hi_d, i * FT + j * 2 + (b + 1))
                        pool.tensor_tensor(gu_lo[:, b, :], gu_raw[:, b, :], gu_hi[:, b, :].bitcast(F32),
                                           ALU.subtract).then_inc(gu_lo_d, 1)
                with pool.Fori(0, FP) as j:
                    for b in range(2):
                        pool.wait_ge(d_hi_d, i * FT + j * 2 + (b + 1))
                        pool.tensor_tensor(d_lo[:, b, :], d_raw[:, b, :], d_hi[:, b, :].bitcast(F32),
                                           ALU.subtract).then_inc(d_lo_d, 1)

        @block.scalar
        def _(act):
            def split_h(i, n, first=False):
                act.wait_ge(h_in[n % 2], i * 32 + (n // 2 * 16 + 16))
                act.activation(h_hi[:, 2 * n:2 * n + 2, :], h_raw[:, n % 2, :, :], ACT.Copy).then_inc(h_hi_d, 1)

            def split_gu(i, j, b, first=False):
                act.wait_ge(gu_in[b], i * (16 * FP) + j * 16 + 16)
                if not first:
                    act.wait_ge(gate_up, i * FT + j * 2 + (b - 1))
                act.activation(gu_hi[:, b, :], gu_raw[:, b, :], ACT.Copy).then_inc(gu_hi_d, 1)

            def split_d(i, j, b, first=False):
                act.wait_ge(d_in[b], i * (16 * FP) + j * 16 + 16)
                act.wait_ge(down, i * FT + j * 2 + (b + 1))
                act.activation(d_hi[:, b, :], d_raw[:, b, :], ACT.Copy).then_inc(d_hi_d, 1)

            def silu(i, j, b):
                act.wait_ge(gate_up, i * FT + j * 2 + (b + 1))
                act.wait_ge(a_d, i * FT + j * 2 + (b + 1))
                act.activation(sg[:, b, :], bank[2 * b][:, :], ACT.Silu).then_inc(silu_d, 1)

            act.wait_ge(ready, 1)
            split_gu(0, 0, 0, True)
            for n in range(4):
                split_h(0, n, True)
            split_gu(0, 0, 1, True)
            with act.Fori(0, TB) as i:
                with act.Fori(0, FP - 1) as j:
                    for b in range(2):
                        silu(i, j, b)
                        split_gu(i, j + 1, b)
                for b in range(2):
                    split_d(i, 0, b)
                    silu(i, FP - 1, b)
                for n in range(4):
                    split_h(i + 1, n)
                with act.Fori(1, FP) as j:
                    for b in range(2):
                        split_d(i, j, b)
                for b in range(2):
                    split_gu(i + 1, 0, b)
                for n in range(4):
                    act.wait_ge(down, i * FT + (FT + 2))
                    act.activation(f[:, n, NB:2 * NB], bank[2 * n + 1][:, :], ACT.Copy).then_inc(f_s, 1)
                for n in range(4):
                    act.wait_ge(f_v, i * 4 + (n + 1))
                    act.wait_ge(f_s, i * 4 + (n + 1))
                    act.wait_ge(sq_d, i * 4 + n)
                    act.activation(sq[:, :], f[:, n, :], ACT.Square, accum_out=ssq[:, n:n + 1]).then_inc(sq_d, 1)
                act.preload_act_table_set(LOG_EXP)
                act.wait_ge(sq_d, i * 4 + 4)
                act.activation(rstd[:, :], ssq[:, :], ACT.Ln, bias=eps[:, :], scale=1.0 / D_MODEL).then_inc(rooted, 1)
                act.wait_ge(rooted, i * 2 + 1)
                act.activation(rstd[:, :], rstd[:, :], ACT.Exp, scale=-0.5).then_inc(rooted, 1)

        @block.vector
        def _(dve):
            def split_h(i, n):
                dve.wait_ge(h_hi_d, i * 4 + (n + 1))
                dve.tensor_tensor(h_lo[:, 2 * n:2 * n + 2, :], h_raw[:, n % 2, :, :], h_hi[:, 2 * n:2 * n + 2, :].bitcast(F32),
                                  ALU.subtract).then_inc(h_lo_d, 1)

            def split_a(i, j, b):
                act_tile = a[:, bass.ds(j * 2 + b, 1), :].rearrange("p a t -> p (a t)")
                dve.wait_ge(down, i * FT + j * 2 + (b + 1))
                dve.tensor_copy(a_hi[:, b, :], act_tile).then_inc(a_hi_d, 1)
                dve.wait_ge(a_hi_d, i * FT + j * 2 + (b + 1))
                dve.tensor_tensor(a_lo[:, b, :], act_tile, a_hi[:, b, :].bitcast(F32), ALU.subtract).then_inc(a_lo_d, 1)

            dve.wait_ge(c_in, 16)
            for n in range(4):
                split_h(0, n)
            with dve.Fori(0, TB) as i:
                with dve.Fori(0, FP) as j:
                    for b in range(2):
                        dve.wait_ge(silu_d, i * FT + j * 2 + (b + 1))
                        dve.tensor_tensor(a[:, bass.ds(j * 2 + b, 1), :].rearrange("p a t -> p (a t)"), sg[:, b, :],
                                          bank[2 * b + 1][:, :], ALU.mult).then_inc(a_d, 1)
                dve.wait_ge(a_d, i * FT + (FT + 2))
                for b in range(2):
                    split_a(i, 0, b)
                for n in range(4):
                    split_h(i + 1, n)
                with dve.Fori(1, FP) as j:
                    for b in range(2):
                        split_a(i, j, b)
                for n in range(4):
                    if n == 0:
                        dve.wait_ge(down, i * FT + (FT + 2))
                        dve.wait_ge(out_sent[0], i * 64)
                    dve.tensor_copy(f[:, n, 0:NB], bank[2 * n][:, :]).then_inc(f_v, 1)
                dve.wait_ge(rooted, i * 2 + 2)
                for n in range(4):
                    b = n % 2
                    dve.scalar_tensor_tensor(f[:, n, :], f[:, n, :], rstd[:, n:n + 1], w_post[:, :],
                                             ALU.mult, ALU.mult).then_inc(scaled, 1)
                    dve.wait_ge(scaled, i * 4 + (n + 1))
                    dve.wait_ge(x_in[b], i * 32 + (n // 2 * 16 + 16))
                    dve.tensor_tensor(f[:, n, :], f[:, n, :], xm[:, b, :], ALU.add).then_inc(added, 1)

        @block.tensor
        def _(pe):
            def hidden(i, j, b):
                pe.wait_ge(gu_lo_d, i * FT + j * 2 + (b + 1))
                pe.wait_ge(a_d, i * FT + j * 2 + (b + 1))
                for u in range(2):
                    for k in range(KT):
                        at = slice((2 * k + u) * P, (2 * k + u + 1) * P)
                        last = mm3(pe, bank[2 * b + u][:, :], gu_hi[:, b, at], gu_lo[:, b, at], h_hi[:, k, :], h_lo[:, k, :],
                                   k == 0, k == KT - 1)
                last.then_inc(gate_up, 1)

            def project(i, j, b, start, stop):
                pe.wait_ge(d_lo_d, i * FT + j * 2 + (b + 3))
                pe.wait_ge(a_lo_d, i * FT + j * 2 + (b + 1))
                for n in range(4):
                    for g in range(2):
                        at = slice(g * NB, (g + 1) * NB)
                        tok = slice(n * P, (n + 1) * P)
                        last = mm3(pe, bank[2 * n + g][:, :], a_hi[:, b, tok], a_lo[:, b, tok], d_hi[:, b, at],
                                   d_lo[:, b, at], start, stop)
                last.then_inc(down, 1)

            pe.sem_inc(a_d, 2)
            pe.sem_inc(down, 2)
            with pe.Fori(0, TB) as i:
                pe.wait_ge(h_lo_d, i * 4 + 4)
                pe.wait_ge(f_v, i * 4)
                pe.wait_ge(f_s, i * 4)
                alone(pe, stood)
                with pe.Fori(0, FP) as j:
                    for b in range(2):
                        hidden(i, j, b)
                pe.wait_ge(a_d, i * FT + (FT + 2))
                project(i, 0, 0, True, False)
                project(i, 0, 1, False, False)
                with pe.Fori(1, FP - 1) as j:
                    for b in range(2):
                        project(i, j, b, False, False)
                project(i, FP - 1, 0, False, False)
                project(i, FP - 1, 1, False, True)


def decoder_layer(nc, arrays, out):
    consts = {n[2:]: a for n, a in arrays.items() if n.startswith("c_")}
    prm = {n: a for n, a in arrays.items() if not n.startswith("c_")}
    dram = {n: nc.dram_tensor(n, shape, F32, kind="Internal").ap() for n, shape in (
        ("proj", (MT, P, SEQ)), ("rows", (2, NT * DN_HEADS * P)), ("mixed", (P, KT, SEQ)),
        ("x_mid", (SEQ, D_MODEL)), ("h_mid", (P, KT, SEQ)))}
    with ExitStack() as ctx:
        sc = Scope(nc, ctx, "layer")
        ident = sc.sb("ident", [P, P])
        build_constants(nc, ident)
        with ExitStack() as ctx_cf:
            cf_conv = Scope(nc, ctx_cf, "layer").sb("cf_conv", [P, 2, SEQ])
            with ExitStack() as ctx_h:
                sc_h = Scope(nc, ctx_h, "layer")
                h_hi, h_lo = sc_h.sb("h_hi", [P, KT, SEQ], F32R), sc_h.sb("h_lo", [P, KT, SEQ], F32R)
                norm_and_turn(nc, prm["x"], prm["w_pre_mix"], ident, h_hi, h_lo)
                project_in(nc, prm["w_in"], prm["cf_taps"], prm["cf_bias"], prm["dn_taps"], h_hi, h_lo, cf_conv, dram["proj"])
            with ExitStack() as ctx_kv:
                sc_kv = Scope(nc, ctx_kv, "layer")
                gates = sc_kv.sb("gates", [P, NT, 51])
                kv = [sc_kv.sb(n, shape) for n, shape in (
                    ("kc", [P, P]), ("vc", [P, P]), ("vs", [P, NT, P]), ("ks", [P, SEQ]), ("vw", [P, NT + WINDOW // P, P]),
                    ("kw", [P, WINDOW + SEQ]))]
                prepare(nc, consts, prm, cf_conv, dram["proj"], dram["mixed"], dram["rows"], gates, *kv)
                mix_tokens(nc, consts, prm, dram["proj"], dram["rows"], gates, kv, dram["mixed"], ident)
        mix_out(nc, prm, prm["x"], dram["mixed"], dram["x_mid"], dram["h_mid"], ident)
        feed_forward(nc, prm, dram["x_mid"], dram["h_mid"], out)


def layout(inputs):
    i = {n: np.asarray(a) for n, a in inputs.items()}
    one = {n: a[0] for n, a in i.items()}
    dn = DN_HEADS * DH
    heads = np.array(HX)
    o = 4 * dn
    beta, decay = o + heads, o + DN_HEADS + heads
    value = np.arange(CF_CH) + o + 2 * DN_HEADS
    gate = value + CF_CH
    o += 2 * DN_HEADS + 2 * CF_CH
    queries = (o + np.arange(2 * HPG * DH)).reshape(2, HPG, DH).transpose(1, 0, 2).reshape(-1)
    rest = np.arange(o + 2 * HPG * DH, one["w_in"].shape[1])
    kv, nsa_gates = rest[:6 * P], rest[6 * P:]
    first = np.concatenate([gate[:P], value[:P], gate[P:], value[P:], queries, kv, beta, decay, nsa_gates])
    last = np.concatenate([np.arange(3 * dn, 4 * dn), np.arange(3 * dn)])
    w_in = np.zeros((D_MODEL, MT * P), one["w_in"].dtype)
    w_in[:, :len(first)] = one["w_in"][:, first]
    w_in[:, T_DZ * P:] = one["w_in"][:, last]
    gate_up = np.stack([one["ffn_w_gate"], one["ffn_w_up"]]).reshape(2, KT, P, FT, P)
    arrays = {
        "x": one["x"],
        "w_pre_mix": one["norm_w"][0], "w_post_mix": one["norm_w"][1],
        "w_pre_ffn": one["norm_w"][2], "w_post_ffn": one["norm_w"][3],
        "w_in": w_in.reshape(KT, P, MT, P).transpose(2, 1, 0, 3).reshape(MT, P, D_MODEL),
        "cf_taps": one["cf_dw_w"].T.reshape(2, P, CF_TAPS).transpose(1, 0, 2),
        "cf_bias": one["cf_dw_b"].reshape(2, P).T,
        "dn_taps": one["dn_conv_w"].T.reshape(9, P, DN_TAPS).transpose(1, 0, 2),
        "cf_ln_w": one["cf_ln_w"].reshape(2, P).T, "cf_ln_b": one["cf_ln_b"].reshape(2, P).T,
        "dn_dt_bias": one["dn_dt_bias"][heads], "dn_a_log": one["dn_a_log"][heads],
        "dn_norm_w": np.tile(one["dn_norm_w"], 2)[:, None],
        "w_out": one["w_out"],
        "w_gate_up": gate_up.transpose(3, 2, 1, 0, 4).reshape(FT, P, 2 * D_MODEL),
        "w_down": one["ffn_w_down"].reshape(FT, P, D_MODEL),
    }
    for n in "kv":
        arrays[f"nsa_{n}_w1"] = one[f"nsa_{n}_w1"].reshape(CMP_LEN, DH, P).transpose(1, 0, 2)
        arrays[f"nsa_{n}_w2"] = one[f"nsa_{n}_w2"]
        arrays[f"nsa_{n}_pos"] = one[f"nsa_{n}_pos"].T
    return arrays


def kernel(**inputs):
    import concourse.bacc as _bacc
    from concourse.bass_utils import run_bass_kernel_spmd as _run

    arrays = layout(inputs)
    arrays |= {"c_" + n: a for n, a in shape_constants().items()}
    arrays = {n: np.ascontiguousarray(a) for n, a in arrays.items()}
    nc = _bacc.Bacc("TRN2", target_bir_lowering=False, num_devices=1)
    ins = {n: nc.dram_tensor(f"in_{n}", a.shape, F32, kind="ExternalInput").ap() for n, a in arrays.items()}
    out = nc.dram_tensor("out", (SEQ, D_MODEL), F32, kind="ExternalOutput").ap()
    decoder_layer(nc, ins, out)
    r = _run(nc, [{f"in_{n}": a for n, a in arrays.items()}], core_ids=[0])
    return r.results[0]["out"].reshape(1, SEQ, D_MODEL)
```

```python
from contextlib import ExitStack

import numpy as np
import concourse.bass as bass
from concourse import mybir

F32 = mybir.dt.float32
F32R = mybir.dt.float32r
ALU = mybir.AluOpType
ACT = mybir.ActivationFunctionType
AX = mybir.AxisListType

LOG_EXP = "natural_log_exp_and_others"

P = 128
D_MODEL = 1024
SEQ = 2048
KT = D_MODEL // P
NT = SEQ // P
NB = 512
TB = SEQ // NB
EPS = 1e-6
NEG = -1e30
SEL_BIG = 1e4

DN_HEADS = 6
DH = 64
DN_PAIRS = DN_HEADS // 2
DN_TAPS = 4
CF_CH = 256
CF_TAPS = 31
HPG = 3
CMP_LEN = 32
CMP_STRIDE = 16
N_CMP = (SEQ - CMP_LEN) // CMP_STRIDE + 1
SEL_BLOCK = 64
N_BLK = SEQ // SEL_BLOCK
WINDOW = 512
D_FF = 2816
FT = D_FF // P

T_CF = 0
T_NQ = 4
T_KC, T_VC, T_KS, T_VS, T_KW, T_VW, T_SM = 7, 8, 9, 10, 11, 12, 13
T_DZ, T_DQ, T_DK, T_DV = 14, 17, 20, 23
MT = 26
PAD = 32
N_SMALL = 2 * DN_HEADS + 3 * 2 * HPG


def mm3(pe, out, w_hi, w_lo, a_hi, a_lo, start, stop):
    pe.matmul(out, w_hi, a_hi, start=start, stop=False)
    pe.matmul(out, w_hi, a_lo, start=False, stop=False)
    return pe.matmul(out, w_lo, a_hi, start=False, stop=stop)


def alone(eng, stood):
    eng.sem_inc(stood, 1)


class Scope:

    def __init__(self, nc, ctx, tag):
        self.nc, self.ctx, self.tag = nc, ctx, tag

    def sb(self, name, shape, dt=F32):
        return self.ctx.enter_context(self.nc.sbuf_tensor(f"{self.tag}_{name}", shape, dt))

    def ps(self, name, shape, dt=F32):
        return self.ctx.enter_context(self.nc.psum_tensor(f"{self.tag}_{name}", shape, dt))

    def sem(self, name):
        return self.nc.alloc_semaphore(f"{self.tag}_{name}")


def build_constants(nc, ident):
    with ExitStack() as ctx:
        sc = Scope(nc, ctx, "const")
        made = sc.sem("made")
        block = ctx.enter_context(nc.Block())

        @block.gpsimd
        def _(pool):
            pool.memset(ident[:, :], 0.0).then_inc(made, 1)
            pool.wait_ge(made, 1)
            pool.affine_select(out=ident[:, :], in_=ident[:, :], compare_op=ALU.not_equal, fill=1.0, base=0,
                               pattern=[[-1, P]], channel_multiplier=1).then_inc(made, 1)
            pool.wait_ge(made, 2)


def norm_and_turn(nc, x, w_pre, ident, h_hi, h_lo):
    with ExitStack() as ctx:
        sc = Scope(nc, ctx, "turn")
        xt = sc.sb("xt", [P, 2, D_MODEL])
        xn = sc.sb("xn", [P, 2, D_MODEL])
        sq = sc.sb("sq", [P, D_MODEL])
        wb = sc.sb("wb", [P, D_MODEL])
        eps = sc.sb("eps", [P, 1])
        ssq = sc.sb("ssq", [P, NT])
        rms = sc.sb("rms", [P, NT])
        rstd = sc.sb("rstd", [P, NT])
        turned = [[sc.ps(f"turned{b}{g}", [P, NB]) for g in range(2)] for b in range(2)]
        x_in = [sc.sem(f"x_in{b}") for b in range(2)]
        w_in, eps_set, squared, rooted, inverted, normed = (
            sc.sem(n) for n in ("w_in", "eps_set", "squared", "rooted", "inverted", "normed"))
        turn_done, hi_done, lo_done = sc.sem("turn_done"), sc.sem("hi_done"), sc.sem("lo_done")
        block = ctx.enter_context(nc.Block())

        @block.sync
        def _(sp):
            sp.dma_start(wb[:, :], w_pre.partition_broadcast(P)).then_inc(w_in, 16)
            for b in range(2):
                sp.dma_start(xt[:, b, :], x[b * P:(b + 1) * P, :]).then_inc(x_in[b], 16)
            with sp.Fori(1, NT // 2) as i:
                for b in range(2):
                    sp.wait_ge(normed, i * 2 + (b - 1))
                    sp.dma_start(xt[:, b, :], x[bass.ds((i * 2 + b) * P, P), :]).then_inc(x_in[b], 16)

        @block.scalar
        def _(act):
            act.preload_act_table_set("sqrt_and_others")
            act.wait_ge(eps_set, 1)
            with act.Fori(0, NT // 2) as i:
                for b in range(2):
                    act.wait_ge(x_in[b], i * 16 + 16)
                    act.wait_ge(rooted, i * 2 + b) if b else None
                    act.activation(sq[:, :], xt[:, b, :], ACT.Square,
                                   accum_out=ssq[:, bass.ds(i * 2 + b, 1)]).then_inc(squared, 1)
                    act.wait_ge(squared, i * 2 + b + 1)
                    act.activation(rms[:, bass.ds(i * 2 + b, 1)], ssq[:, bass.ds(i * 2 + b, 1)], ACT.Sqrt,
                                   bias=eps[:, :], scale=1.0 / D_MODEL).then_inc(rooted, 1)
                for b in range(2):
                    for g in range(2):
                        act.wait_ge(turn_done, i * 4 + 2 * b + g + 1)
                        act.activation(h_hi[:, 4 * g:4 * g + 4, bass.ds((i * 2 + b) * P, P)],
                                       turned[b][g][:, :].rearrange("p (k t) -> p k t", k=4),
                                       ACT.Copy).then_inc(hi_done, 1)

        @block.vector
        def _(dve):
            dve.memset(eps[:, :], EPS).then_inc(eps_set, 1)
            dve.wait_ge(w_in, 16)
            with dve.Fori(0, NT // 2) as i:
                for b in range(2):
                    dve.wait_ge(rooted, i * 2 + b + 1)
                    dve.reciprocal(rstd[:, bass.ds(i * 2 + b, 1)], rms[:, bass.ds(i * 2 + b, 1)]).then_inc(inverted, 1)
                    dve.wait_ge(inverted, i * 2 + b + 1)
                    dve.scalar_tensor_tensor(xn[:, b, :], xt[:, b, :], rstd[:, bass.ds(i * 2 + b, 1)], wb[:, :],
                                             ALU.mult, ALU.mult).then_inc(normed, 1)
                for b in range(2):
                    for g in range(2):
                        dve.wait_ge(hi_done, i * 4 + 2 * b + g + 1)
                        part = (slice(None), slice(4 * g, 4 * g + 4), bass.ds((i * 2 + b) * P, P))
                        dve.tensor_tensor(h_lo[part], turned[b][g][:, :].rearrange("p (k t) -> p k t", k=4),
                                          h_hi[part].bitcast(F32), ALU.subtract).then_inc(lo_done, 1)

        @block.tensor
        def _(pe):
            def tile(i, b, first):
                pe.wait_ge(normed, i * 2 + b + 1)
                for g in range(2):
                    if not first:
                        pe.wait_ge(lo_done, i * 4 + (2 * b + g - 3))
                    for k in range(4):
                        last = pe.transpose(turned[b][g][:, k * P:(k + 1) * P],
                                            xn[:, b, (4 * g + k) * P:(4 * g + k + 1) * P], ident[:, :])
                    last.then_inc(turn_done, 1)

            for b in range(2):
                tile(0, b, True)
            with pe.Fori(1, NT // 2) as i:
                for b in range(2):
                    tile(i, b, False)


def project_in(nc, w_cols, cf_w, cf_b, dn_w, h_hi, h_lo, cf_conv, proj):
    with ExitStack() as ctx:
        sc = Scope(nc, ctx, "proj")
        w_raw = sc.sb("w_raw", [P, 2, D_MODEL])
        w_hi = sc.sb("w_hi", [P, 2, D_MODEL], F32R)
        w_lo = sc.sb("w_lo", [P, 2, D_MODEL], F32R)
        row = sc.sb("row", [P, 2, PAD + SEQ])
        work = sc.sb("work", [P, 2, PAD + SEQ])
        taps_cf = sc.sb("taps_cf", [P, 2, CF_TAPS])
        bias_cf = sc.sb("bias_cf", [P, 2])
        taps_dn = sc.sb("taps_dn", [P, 9, DN_TAPS])
        acc = [sc.ps(f"acc{n}", [P, NB]) for n in range(8)]
        raw_in = [sc.sem(f"raw_in{b}") for b in range(2)]
        row_sent = [sc.sem(f"row_sent{b}") for b in range(2)]
        conv_sent = [sc.sem(f"conv_sent{b}") for b in range(2)]
        taps_in, zeroed, hi_done, lo_done, summed, taken = (
            sc.sem(n) for n in ("taps_in", "zeroed", "hi_done", "lo_done", "summed", "taken"))
        gated, cf_step, dn_step, silu_done = (sc.sem(n) for n in ("gated", "cf_step", "dn_step", "silu_done"))
        block = ctx.enter_context(nc.Block())
        PLAIN, CONV = T_NQ, T_DQ
        tok = slice(PAD, PAD + SEQ)

        @block.sync
        def _(sp):
            for b in range(2):
                sp.dma_start(w_raw[:, b, :], w_cols[b]).then_inc(raw_in[b], 16)
            sp.dma_start(taps_cf[:, :, :], cf_w).then_inc(taps_in, 16)
            sp.dma_start(bias_cf[:, :], cf_b).then_inc(taps_in, 16)
            sp.dma_start(taps_dn[:, :, :], dn_w).then_inc(taps_in, 16)
            with sp.Fori(1, MT // 2) as i:
                for b in range(2):
                    sp.wait_ge(lo_done, i * 2 + (b - 1))
                    sp.dma_start(w_raw[:, b, :], w_cols[i * 2 + b]).then_inc(raw_in[b], 16)

        @block.gpsimd
        def _(pool):
            pool.memset(row[:, :, 0:PAD], 0.0).then_inc(zeroed, 1)
            pool.memset(work[:, :, 0:PAD], 0.0).then_inc(zeroed, 1)
            with pool.Fori(0, MT // 2) as i:
                for b in range(2):
                    pool.wait_ge(hi_done, i * 2 + b + 1)
                    if b == 0:
                        pool.wait_ge(lo_done, i * 2)
                    pool.tensor_tensor(w_lo[:, b, :], w_raw[:, b, :], w_hi[:, b, :].bitcast(F32),
                                       ALU.subtract).then_inc(lo_done, 1)

        @block.scalar
        def _(act):
            def split(r, b, first=False):
                act.wait_ge(raw_in[b], (r - b) * 8 + 16)
                if not first:
                    act.wait_ge(summed, r * 4 - 4)
                act.activation(w_hi[:, b, :], w_raw[:, b, :], ACT.Copy).then_inc(hi_done, 1)

            def evacuate(r, b, dst, func=ACT.Copy):
                for t in range(4):
                    act.wait_ge(summed, r * 4 + (t + 1))
                    act.activation(dst[:, b, PAD + t * NB:PAD + (t + 1) * NB], acc[4 * b + t][:, :],
                                   func).then_inc(taken, 1)

            def send_row(r, b):
                act.wait_ge(taken, r * 4 + 4)
                act.dma_start(proj[r], row[:, b, tok]).then_inc(row_sent[b], 16)

            def silu_row(n, b):
                act.wait_ge(dn_step, n * DN_TAPS + DN_TAPS)
                act.activation(work[:, b, tok], work[:, b, tok], ACT.Silu).then_inc(silu_done, 1)
                act.wait_ge(silu_done, n + 1)
                act.dma_start(proj[n + CONV], work[:, b, tok]).then_inc(conv_sent[b], 16)

            split(0, 0, True)
            split(1, 1, True)
            for c in range(2):
                for t in range(4):
                    act.wait_ge(summed, 8 * c + t + 1)
                    act.activation(work[:, c, PAD + t * NB:PAD + (t + 1) * NB], acc[t][:, :],
                                   ACT.Sigmoid).then_inc(taken, 1)
                split(2 * c + 2, 0)
                if c:
                    act.wait_ge(gated, 1)
                evacuate(2 * c + 1, 1, row)
                split(2 * c + 3, 1)
            def plain(r, b, sent, func=ACT.Copy):
                if sent is not None:
                    act.wait_ge(row_sent[b], sent)
                evacuate(r, b, row, func)
                send_row(r, b)
                split(r + 2, b)

            plain(PLAIN, 0, None)
            act.wait_ge(gated, 2)
            plain(PLAIN + 1, 1, None)
            with act.Fori(1, 5) as i:
                for b in range(2):
                    plain(i * 2 + (PLAIN + b), b, i * 16)
            for r in range(T_DZ, T_DQ):
                plain(r, r % 2, (r - PLAIN) // 2 * 16, ACT.Silu)

            def convolved(r, b, n, first):
                if first:
                    act.wait_ge(row_sent[b], (7 - b) * 16)
                else:
                    act.wait_ge(dn_step, n * DN_TAPS - DN_TAPS)
                evacuate(r, b, row)

            convolved(CONV, 1, 0, True)
            split(CONV + 2, 1)
            convolved(CONV + 1, 0, 1, True)
            split(CONV + 3, 0)
            silu_row(0, 0)
            with act.Fori(1, 3) as i:
                convolved(i * 2 + CONV, 1, i * 2, False)
                split(i * 2 + (CONV + 2), 1)
                silu_row(i * 2 - 1, 1)
                convolved(i * 2 + (CONV + 1), 0, i * 2 + 1, False)
                split(i * 2 + (CONV + 3), 0)
                silu_row(i * 2, 0)
            convolved(CONV + 6, 1, 6, False)
            split(CONV + 8, 1)
            silu_row(5, 1)
            convolved(CONV + 7, 0, 7, False)
            silu_row(6, 0)
            convolved(CONV + 8, 1, 8, False)
            silu_row(7, 1)
            silu_row(8, 0)
            for b in range(2):
                act.wait_ge(row_sent[b], (7 - b) * 16)
                act.wait_ge(conv_sent[b], (5 - b) * 16)

        @block.vector
        def _(dve):
            dve.wait_ge(taps_in, 48)
            dve.wait_ge(zeroed, 2)
            n = 0
            for c in range(2):
                dve.wait_ge(taken, 8 * c + 8)
                dve.tensor_tensor(work[:, c, tok], work[:, c, tok], row[:, 1, tok], ALU.mult).then_inc(gated, 1)
                dve.wait_ge(gated, c + 1)
                for k in range(CF_TAPS):
                    at = work[:, c, PAD - CF_TAPS + 1 + k:PAD - CF_TAPS + 1 + k + SEQ]
                    if k == 0:
                        dve.tensor_scalar(cf_conv[:, c, :], at, taps_cf[:, c, k:k + 1], bias_cf[:, c:c + 1],
                                          ALU.mult, ALU.add).then_inc(cf_step, 1)
                    else:
                        dve.wait_ge(cf_step, n)
                        dve.scalar_tensor_tensor(cf_conv[:, c, :], at, taps_cf[:, c, k:k + 1], cf_conv[:, c, :],
                                                 ALU.mult, ALU.add).then_inc(cf_step, 1)
                    n += 1

            def convolve(n, b, sent):
                dve.wait_ge(taken, n * 4 + (CONV * 4 + 4))
                if sent is not None:
                    dve.wait_ge(conv_sent[b], sent)
                for k in range(DN_TAPS):
                    at = row[:, 1 - b, PAD - DN_TAPS + 1 + k:PAD - DN_TAPS + 1 + k + SEQ]
                    tap = taps_dn[:, bass.ds(n, 1), k]
                    if k == 0:
                        dve.wait_ge(cf_step, 2 * CF_TAPS)
                        dve.tensor_scalar(work[:, b, tok], at, tap, None, ALU.mult).then_inc(dn_step, 1)
                    else:
                        dve.wait_ge(dn_step, n * DN_TAPS + k)
                        dve.scalar_tensor_tensor(work[:, b, tok], at, tap, work[:, b, tok],
                                                 ALU.mult, ALU.add).then_inc(dn_step, 1)

            convolve(0, 0, None)
            convolve(1, 1, None)
            with dve.Fori(1, 4) as i:
                convolve(i * 2, 0, i * 16)
                convolve(i * 2 + 1, 1, i * 16)
            convolve(8, 0, 4 * 16)

        @block.tensor
        def _(pe):
            def project(r, b, first):
                pe.wait_ge(lo_done, r + 1)
                for t in range(4):
                    if not first:
                        pe.wait_ge(taken, r * 4 + (t - 7))
                    for k in range(KT):
                        last = mm3(pe, acc[4 * b + t][:, :], w_hi[:, b, k * P:(k + 1) * P],
                                   w_lo[:, b, k * P:(k + 1) * P], h_hi[:, k, t * NB:(t + 1) * NB],
                                   h_lo[:, k, t * NB:(t + 1) * NB], k == 0, k == KT - 1)
                    last.then_inc(summed, 1)

            for b in range(2):
                project(b, b, True)
            with pe.Fori(1, MT // 2) as i:
                for b in range(2):
                    project(i * 2 + b, b, False)


def shape_constants():
    f = np.float32
    i, j = np.arange(P)[:, None], np.arange(P)[None, :]
    c = {"ident": (i == j), "upper": (i <= j), "halves": (i // DH == j // DH),
         "mean_cf": np.full((P, P), 1.0 / CF_CH)}
    steps = [2 ** n for n in range(7)]
    c["joins"] = np.concatenate([(i // (2 * s) == j // (2 * s)) & (j // s % 2 == 1) & (i // s % 2 == 0)
                                 for s in steps], axis=1)
    c["falls"] = np.concatenate([(i // (2 * s) == j // (2 * s)) & (j // s % 2 == 0) & (i // s % 2 == 1)
                                 for s in steps[1:]], axis=1)
    c["same"] = np.concatenate([i // (2 * s) == j // (2 * s) for s in steps[:-2]], axis=1)
    s = np.array(steps)[None, :]
    c["sides"] = np.concatenate([i // s % 2 == 0, i // s % 2 == 1], axis=1)
    m = np.arange(2 * P - 8)[None, :] - (P - 8)
    seen = CMP_STRIDE * m + CMP_LEN - 1 <= i
    c["cmp_seen"], c["cmp_bias"] = seen, np.where(seen, 0.0, NEG)
    m = np.arange(2 * N_BLK - 2)[None, :] - (N_BLK - 2)
    cur = i // SEL_BLOCK
    elig = m <= cur
    c["blk_elig"] = elig
    c["blk_add"] = np.where(elig, np.where(m >= cur - 1, SEL_BIG, 0.0), -SEL_BIG)
    c["causal"] = np.where(j <= i, 0.0, NEG)
    k = np.arange(WINDOW + P)[None, :]
    c["band"] = np.where((k > i) & (k <= i + WINDOW), 0.0, NEG)
    return {n: np.ascontiguousarray(np.broadcast_to(a, (P, a.shape[1])).astype(f)) for n, a in c.items()}


def prepare(nc, consts, prm, cf_conv, proj, mixed, rows, gates, kc, vc, vs, ks, vw, kw):
    with ExitStack() as ctx:
        sc = Scope(nc, ctx, "prep")
        ident, upper, mean_w = sc.sb("ident", [P, P]), sc.sb("upper", [P, P]), sc.sb("mean_w", [P, P])
        ones = sc.sb("ones", [P, P])
        total = sc.sb("total", [P, NT * DN_HEADS])
        to_last = sc.sb("to_last", [P, NT * DN_HEADS])
        ln_w, ln_b = sc.sb("ln_w", [P, 2]), sc.sb("ln_b", [P, 2])
        eps = sc.sb("eps", [P, 1])
        dt_b, a_log = sc.sb("dt_b", [P, DN_HEADS]), sc.sb("a_log", [P, DN_HEADS])
        small = sc.sb("small", [N_SMALL, SEQ])
        tok_small = sc.sb("tok_small", [P, NT, 32])
        sp_t = [sc.sb(f"sp{n}", [P, NT * DN_HEADS]) for n in range(4)]
        neg_rate = sc.sb("neg_rate", [P, DN_HEADS])
        row_sb = sc.sb("row_sb", [NT * DN_HEADS, 2, P])
        sq = sc.sb("sq", [P, 2, SEQ])
        std = sc.sb("std", [P, SEQ])
        pairs = {(n, g): sc.sb(f"pairs_{n}{g}", [P, SEQ]) for n in "kv" for g in range(2)}
        feat = {n: sc.sb(f"f_{n}", [P, SEQ]) for n in ("vs", "vw")}
        w1 = {n: sc.sb(f"w1_{n}", [P, CMP_LEN // 2, P]) for n in "kv"}
        w2 = {n: sc.sb(f"w2_{n}", [P, DH]) for n in "kv"}
        pos = {n: sc.sb(f"pos_{n}", [P, CMP_LEN // 2]) for n in "kv"}
        pos_b = sc.sb("pos_b", [P, 2])
        hid = sc.sb("hid", [P, 4, P])
        bank = [sc.ps(f"bank{n}", [P, NB]) for n in range(8)]
        names = ("c_in c_small in_v in_wk in_wv in_k in_small zeroed m_sum m_sub sq_done v_sum v_std v_inv v_mul cf_done cf_sent "
                 "sm_turn sm_copy sg step pe_gam gam_copy pe_rows rows_copy rows_sent pe_pos pos_copy pe_hid hid_done pe_cmp "
                 "cmp_copy pe_v v_copy")
        (c_in, c_small, in_v, in_wk, in_wv, in_k, in_small, zeroed, m_sum, m_sub, sq_done, v_sum, v_std, v_inv, v_mul, cf_done, cf_sent,
         sm_turn, sm_copy, sg, step, pe_gam, gam_copy, pe_rows, rows_copy, rows_sent, pe_pos, pos_copy, pe_hid, hid_done, pe_cmp,
         cmp_copy, pe_v, v_copy) = (sc.sem(n) for n in names.split())
        block = ctx.enter_context(nc.Block())
        NH = NT * DN_HEADS
        hid_bank = [bank[7], bank[0]]
        beta, gam, nsa_gate = gates[:, :, 0:6], gates[:, :, 6:12], gates[:, :, 12:30]

        @block.sync
        def _(sp):
            sp.dma_start(mean_w[:, :], consts["mean_cf"]).then_inc(c_in, 16)
            sp.dma_start(ident[:, :], consts["ident"]).then_inc(c_in, 16)
            sp.dma_start(upper[:, :], consts["upper"]).then_inc(c_in, 16)
            sp.dma_start(small[:, :], proj[T_SM][0:N_SMALL, :]).then_inc(in_small, 16)
            sp.dma_start(ln_w[:, :], prm["cf_ln_w"]).then_inc(c_small, 16)
            sp.dma_start(ln_b[:, :], prm["cf_ln_b"]).then_inc(c_small, 16)
            sp.dma_start(dt_b[:, :], prm["dn_dt_bias"].partition_broadcast(P)).then_inc(c_small, 16)
            sp.dma_start(a_log[:, :], prm["dn_a_log"].partition_broadcast(P)).then_inc(c_small, 16)
            for n, t, loaded in (("k", T_KC, in_wk), ("v", T_VC, in_wv)):
                sp.dma_start(w1[n][:, :, :], prm[f"nsa_{n}_w1"]).then_inc(loaded, 16)
                sp.dma_start(w2[n][:, :], prm[f"nsa_{n}_w2"]).then_inc(loaded, 16)
                sp.dma_start(pos[n][:, :], prm[f"nsa_{n}_pos"]).then_inc(loaded, 16)
                for g in range(2):
                    at = slice(g * DH, (g + 1) * DH)
                    sp.dma_start(pairs[n, g][0:DH, :], proj[t][at, :]).then_inc(loaded, 16)
                    sp.dma_start(pairs[n, g][DH:P, 0:SEQ - 1], proj[t][at, 1:SEQ]).then_inc(loaded, 16)
            for n, t in (("vs", T_VS), ("vw", T_VW)):
                sp.dma_start(feat[n][:, :], proj[t]).then_inc(in_v, 16)
            sp.dma_start(ks[:, :], proj[T_KS]).then_inc(in_k, 16)
            sp.dma_start(kw[:, WINDOW:WINDOW + SEQ], proj[T_KW]).then_inc(in_k, 16)
            for c in range(2):
                sp.wait_ge(cf_done, c + 1)
                sp.dma_start(mixed[:, 3 + c, :], sq[:, c, :]).then_inc(cf_sent, 16)
            sp.wait_ge(rows_copy, 2)
            sp.dma_start(rows.rearrange("r (h t) -> h r t", t=P), row_sb[:, :, :]).then_inc(rows_sent, 16)
            sp.wait_ge(in_k, 32)
            sp.wait_ge(cf_sent, 32)
            sp.wait_ge(rows_sent, 16)

        @block.gpsimd
        def _(pool):
            pool.memset(vw[:, 0:4, :], 0.0).then_inc(zeroed, 1)
            pool.memset(kw[:, 0:WINDOW], 0.0).then_inc(zeroed, 1)
            pool.memset(kc[:, :], 0.0).then_inc(zeroed, 1)
            pool.memset(vc[:, :], 0.0).then_inc(zeroed, 1)
            pool.memset(eps[:, :], EPS).then_inc(zeroed, 1)
            pool.memset(ones[:, :], 1.0).then_inc(zeroed, 1)
            pool.wait_ge(zeroed, 6)

        @block.tensor
        def _(pe):
            pe.wait_ge(c_in, 48)
            for t in range(TB):
                for c in range(2):
                    last = pe.matmul(bank[t][:, :], mean_w[:, :], cf_conv[:, c, t * NB:(t + 1) * NB],
                                     start=c == 0, stop=c == 1)
                last.then_inc(m_sum, 1)
            pe.wait_ge(in_small, 16)
            for t in range(NT):
                last = pe.transpose(bank[4][:, t * 32:t * 32 + N_SMALL], small[:, t * P:(t + 1) * P],
                                    ident[0:N_SMALL, 0:N_SMALL])
            last.then_inc(sm_turn, 1)
            for t in range(TB):
                pe.wait_ge(sq_done, 2 * t + 2)
                for c in range(2):
                    last = pe.matmul(bank[t][:, :], mean_w[:, :], sq[:, c, t * NB:(t + 1) * NB],
                                     start=c == 0, stop=c == 1)
                last.then_inc(v_sum, 1)
            pe.wait_ge(v_std, 1)
            for n, x in enumerate("kv"):
                pe.wait_ge(in_wv if n else in_wk, 16 * 7)
                for l in range(CMP_LEN // 2):
                    last = pe.matmul(bank[6][:, n:n + 1], w1[x][:, l, :], pos[x][:, l:l + 1],
                                     start=l == 0, stop=l == CMP_LEN // 2 - 1)
                last.then_inc(pe_pos, 1)
                for l in range(CMP_LEN // 2):
                    for g in range(2):
                        last = pe.matmul(hid_bank[g][:, n * P:n * P + N_CMP], w1[x][:, l, :],
                                         pairs[x, g][:, 2 * l:2 * l + CMP_STRIDE * (N_CMP - 1) + 1:CMP_STRIDE],
                                         start=l == 0, stop=l == CMP_LEN // 2 - 1)
                        if l == CMP_LEN // 2 - 1 and n:
                            last.then_inc(pe_hid, 1)
            pe.wait_ge(gam_copy, 1)
            pe.matmul(bank[5][:, 0:NH], upper[:, :], sp_t[3][:, :], start=True, stop=True)
            pe.wait_ge(zeroed, 6)
            pe.matmul(bank[5][:, 3 * P:3 * P + NH], ones[:, :], sp_t[3][:, :], start=True, stop=True).then_inc(pe_gam, 1)
            pe.wait_ge(in_v, 32)
            n = 0
            for x, dst in (("vs", vs), ("vw", vw)):
                for q in range(4):
                    b = bank[6] if n % 2 else bank[4]
                    if n == 0:
                        pe.wait_ge(sm_copy, 1)
                    elif n == 1:
                        pe.wait_ge(pos_copy, 1)
                    else:
                        pe.wait_ge(v_copy, n - 1)
                    for k in range(4):
                        last = pe.transpose(b[:, k * P:(k + 1) * P], feat[x][:, (4 * q + k) * P:(4 * q + k + 1) * P],
                                            ident[:, :])
                    last.then_inc(pe_v, 1)
                    n += 1
            pe.wait_ge(gam_copy, 2)
            pe.transpose(bank[5][0:NH, P:2 * P], sp_t[0][:, :], ident[:, :]).then_inc(pe_rows, 1)
            pe.transpose(bank[5][0:NH, 2 * P:3 * P], sp_t[1][:, :], ident[:, :]).then_inc(pe_rows, 1)
            pe.wait_ge(hid_done, 4)
            pe.wait_ge(v_copy, 8)
            for g in range(2):
                pe.matmul(bank[6][g * DH:(g + 1) * DH, 0:N_CMP], w2["k"][:, :], hid[:, g, 0:N_CMP],
                          start=True, stop=True)
            for g in range(2):
                last = pe.matmul(bank[6][0:N_CMP, P + g * DH:P + (g + 1) * DH], hid[:, 2 + g, 0:N_CMP], w2["v"][:, :],
                                 start=True, stop=True)
            last.then_inc(pe_cmp, 1)

        @block.scalar
        def _(act):
            for t in range(TB):
                for c in range(2):
                    act.wait_ge(m_sub, 2 * t + c + 1)
                    act.activation(sq[:, c, t * NB:(t + 1) * NB], cf_conv[:, c, t * NB:(t + 1) * NB],
                                   ACT.Square).then_inc(sq_done, 1)
            act.wait_ge(zeroed, 6)
            act.wait_ge(sm_copy, 1)
            act.activation(beta, tok_small[:, :, 0:6], ACT.Sigmoid).then_inc(sg, 1)
            act.activation(nsa_gate, tok_small[:, :, 12:30], ACT.Sigmoid).then_inc(sg, 1)
            for t in range(TB):
                act.wait_ge(v_sum, t + 1)
                act.activation(std[:, t * NB:(t + 1) * NB], bank[t][:, :], ACT.Sqrt, bias=eps[:, :]).then_inc(v_std, 1)
            for c in range(2):
                act.wait_ge(c_small, 64)
                act.wait_ge(v_mul, c + 1)
                act.activation(sq[:, c, :], cf_conv[:, c, :], ACT.Silu, scale=ln_w[:, c:c + 1],
                               bias=ln_b[:, c:c + 1]).then_inc(cf_done, 1)
            act.wait_ge(step, 2)
            act.activation(sp_t[1][:, :], sp_t[0][:, :], ACT.Abs).then_inc(sg, 1)
            act.wait_ge(sg, 3)
            act.activation(sp_t[2][:, :], sp_t[1][:, :], ACT.Exp, scale=-1.0).then_inc(sg, 1)
            act.wait_ge(c_small, 64)
            act.activation(neg_rate[:, :], a_log[:, :], ACT.Exp).then_inc(sg, 1)
            act.wait_ge(sg, 4)
            act.activation(sp_t[1][:, :], sp_t[2][:, :], ACT.Ln, bias=1.0).then_inc(sg, 1)
            act.wait_ge(step, 7)
            for at, src in ((30, sp_t[0]), (42, to_last)):
                act.activation(gates[:, :, at:at + 6], src[:, :].rearrange("p (t h) -> p t h", h=DN_HEADS),
                               ACT.Exp).then_inc(sg, 1)
            for r in range(2):
                part = slice(r * DH, (r + 1) * DH)
                act.activation(gates[part, :, 48:51],
                               total[part, :].rearrange("p (t h) -> p t h", h=DN_HEADS)[:, :, 3 * r:3 * r + 3],
                               ACT.Exp).then_inc(sg, 1)
            for n in range(4):
                act.wait_ge(pe_hid, 2)
                act.wait_ge(pos_copy, 1)
                act.activation(hid[:, n, 0:N_CMP], hid_bank[n % 2][:, (n // 2) * P:(n // 2) * P + N_CMP], ACT.Silu,
                               bias=pos_b[:, n // 2:n // 2 + 1]).then_inc(hid_done, 1)

        @block.vector
        def _(dve):
            for t in range(TB):
                dve.wait_ge(m_sum, t + 1)
                for c in range(2):
                    part = cf_conv[:, c, t * NB:(t + 1) * NB]
                    dve.tensor_tensor(part, part, bank[t][:, :], ALU.subtract).then_inc(m_sub, 1)
            dve.wait_ge(sm_turn, 1)
            dve.tensor_copy(tok_small[:, :, 0:N_SMALL],
                            bank[4][:, :].rearrange("p (t n) -> p t n", n=32)[:, :, 0:N_SMALL]).then_inc(sm_copy, 1)
            for t in range(TB):
                dve.wait_ge(v_std, t + 1)
                part = std[:, t * NB:(t + 1) * NB]
                dve.reciprocal(part, part).then_inc(v_inv, 1)
            dve.wait_ge(v_inv, TB)
            dve.wait_ge(sq_done, 2 * TB)
            for c in range(2):
                dve.tensor_tensor(cf_conv[:, c, :], cf_conv[:, c, :], std[:, :], ALU.mult).then_inc(v_mul, 1)
            dve.wait_ge(pe_pos, 2)
            dve.tensor_copy(pos_b[:, :], bank[6][:, 0:2]).then_inc(pos_copy, 1)
            dve.wait_ge(sm_copy, 1)
            dve.wait_ge(c_small, 64)
            heads = [P, NT, DN_HEADS]
            x0 = sp_t[0][:, :].rearrange("p (t h) -> p t h", h=DN_HEADS)
            dve.tensor_tensor(x0, tok_small[:, :, 6:12], dt_b[:, None, :].to_broadcast(heads), ALU.add).then_inc(step, 1)
            dve.wait_ge(step, 1)
            dve.tensor_scalar(sp_t[3][:, :], sp_t[0][:, :], 0.0, None, ALU.max).then_inc(step, 1)
            dve.wait_ge(sg, 6)
            dve.wait_ge(step, 2)
            dve.tensor_tensor(sp_t[3][:, :], sp_t[3][:, :], sp_t[1][:, :], ALU.add).then_inc(step, 1)
            dve.wait_ge(step, 3)
            x3 = sp_t[3][:, :].rearrange("p (t h) -> p t h", h=DN_HEADS)
            dve.scalar_tensor_tensor(x3, x3, -1.0, neg_rate[:, None, :].to_broadcast(heads),
                                     ALU.mult, ALU.mult).then_inc(gam_copy, 1)
            dve.tensor_copy(sp_t[1][:, :].rearrange("p (t h) -> p t h", h=DN_HEADS), beta).then_inc(step, 1)
            dve.wait_ge(pe_gam, 1)
            dve.tensor_copy(gam, bank[5][:, 0:NH].rearrange("p (t h) -> p t h", h=DN_HEADS)).then_inc(step, 1)
            dve.wait_ge(step, 4)
            dve.tensor_copy(sp_t[0][:, :], bank[5][:, 0:NH]).then_inc(gam_copy, 1)
            dve.tensor_copy(total[:, :], bank[5][:, 3 * P:3 * P + NH]).then_inc(step, 1)
            dve.wait_ge(step, 6)
            dve.wait_ge(gam_copy, 2)
            dve.tensor_tensor(to_last[:, :], total[:, :], sp_t[0][:, :], ALU.subtract).then_inc(step, 1)
            dve.wait_ge(sg, 10)
            dve.tensor_tensor(gates[:, :, 36:42], beta, gates[:, :, 30:36], ALU.mult).then_inc(step, 1)
            for n in range(8):
                dve.wait_ge(pe_v, n + 1)
                dst = vs[:, 4 * n:4 * n + 4, :] if n < 4 else vw[:, 4 * (n - 3):4 * (n - 3) + 4, :]
                b = bank[6] if n % 2 else bank[4]
                dve.tensor_copy(dst, b[:, :].rearrange("p (k t) -> p k t", k=4)).then_inc(v_copy, 1)
            dve.wait_ge(pe_rows, 2)
            for r in range(2):
                dve.tensor_copy(row_sb[:, r, :], bank[5][0:NH, (1 + r) * P:(2 + r) * P]).then_inc(rows_copy, 1)
            dve.wait_ge(zeroed, 6)
            dve.wait_ge(pe_cmp, 1)
            dve.tensor_copy(kc[:, 0:N_CMP], bank[6][:, 0:N_CMP]).then_inc(cmp_copy, 1)
            dve.tensor_copy(vc[0:N_CMP, :], bank[6][0:N_CMP, P:2 * P]).then_inc(cmp_copy, 1)
            dve.wait_ge(cmp_copy, 2)


LEVELS = [2, 4, 8, 16, 32, 64]
HX = [0, 2, 4, 1, 3, 5]


class Steps:

    def __init__(self, sem, names):
        self.sem, self.names, self.at = sem, names.split(), 0
        self.count = len(self.names)

    def step(self, name):
        assert self.names[self.at] == name, (self.names[self.at], name)
        self.at = (self.at + 1) % self.count
        return self.sem

    def after(self, name, t):
        return t * self.count + (self.count + self.names.index(name) + 1)

    def before(self, name, t):
        return t * self.count + (self.names.index(name) + 1)


class DeltaNet:

    RING = 2
    JOIN_COLS = DH
    PLACES = 22.8
    CUT = 5

    def __init__(self, sc, banks, consts, prm, proj, rows, gates, mixed, ident):
        self.proj, self.rows, self.gates, self.mixed, self.ident, self.prm, self.consts = (
            proj, rows, gates, mixed, ident, prm, consts)
        self.bank = banks
        sb = sc.sb
        self.qkv = sb("qkv", [P, 9, P])
        self.z = sb("z", [P, 3, P])
        self.bc = sb("bc", [P, 2, DN_HEADS, P])
        self.sq = sb("sq", [P, 2, 3 * P])
        self.rs = sb("rs", [P, 2, 3 * P])
        self.qn, self.kn = sb("qn", [P, 3, P]), sb("kn", [P, 3, P])
        self.E, self.EB = sb("E", [P, DN_HEADS, P]), sb("EB", [P, DN_HEADS, P])
        self.AT, self.QK = sb("AT", [P, DN_HEADS, P]), sb("QK", [P, DN_HEADS, P])
        self.L = sb("L", [P, 7, DN_HEADS, P])
        self.x_pack, self.xt_pack = sb("x_pack", [P, 2, DN_HEADS * DH]), sb("xt_pack", [P, 2, DN_HEADS * DH])
        self.y_pack = sb("y_pack", [P, DN_HEADS * DH])
        self.XT, self.Y = sb("XT", [P, DN_HEADS, P]), sb("Y", [P, DN_HEADS, P])
        self.first = sb("first", [P, DN_HEADS])
        self.bv, self.kb, self.kd = sb("bv", [P, 3, P]), sb("kb", [P, 3, P]), sb("kd", [P, 3, P])
        self.U, self.WT, self.vn, self.o = sb("U", [P, 3, P]), sb("WT", [P, 3, P]), sb("vn", [P, 3, P]), sb("o", [P, 3, P])
        self.S, self.Sg = sb("S", [P, 3, P]), sb("Sg", [P, 3, P])
        self.osq, self.ssq, self.ors = sb("osq", [P, 3, P]), sb("ssq", [P, DN_HEADS]), sb("ors", [P, DN_HEADS])
        self.mix = sb("mix", [P, 3, P])
        self.halves, self.upper, self.joins = sb("halves", [P, P]), sb("upper", [P, P]), sb("joins", [P, 7, P])
        self.falls, self.same, self.sides = sb("falls", [P, 6, P]), sb("same", [P, 5, P]), sb("sides", [P, 2, 7])
        self.one = sb("one", [P, DH])
        self.nw, self.eps = sb("nw", [P, 1]), sb("eps", [P, 1])
        self.c_in, self.ready, self.stood = sc.sem("c_in"), sc.sem("ready"), sc.sem("stood")
        self.qkv_in, self.z_in, self.bc_in, self.sent = (sc.sem(n) for n in ("qkv_in", "z_in", "bc_in", "sent"))
        lev = " ".join(f"y{s} x{s}" for s in LEVELS)
        self.pe = Steps(sc.sem("pe"), f"l2q l2k kt vt kkA kkB qkA qkB y1 {lev} u wt ws o1 o2 sn ot")
        lev = " ".join(f"f{s} x{s}" + (f" e{s}" if s < 32 else "") for s in LEVELS)
        self.v = Steps(sc.sem("dve"), f"qn kn diff kb kd bv atA atB l1 r1 l2 qkA qkB x1 e1 {lev} vn o1 o2 sn ssq mix")
        lev = " ".join(f"y{s}" for s in LEVELS)
        self.a = Steps(sc.sem("act"), f"lnq rsq lnk rsk e {lev} u wt lno rso")
        self.p = Steps(sc.sem("pool"), "sq em eb l4 l8 l16 l32 l64 sg osq on")
        self.taker = {n: (self.v, n) for n in self.pe.names if n in self.v.names}
        self.taker |= {n: (self.a, n) for n in self.pe.names if n in self.a.names}
        self.taker |= {"l2q": (self.a, "lnq"), "l2k": (self.a, "lnk"), "kt": (self.v, "kd"), "vt": (self.v, "bv"),
                       "kkA": (self.v, "atA"), "kkB": (self.v, "atB"), "ws": (self.v, "vn"), "y1": (self.v, "x1"), "ot": (self.v, "mix")}
        assert set(self.taker) == set(self.pe.names)

    def bank_of(self, name):
        return self.bank[self.pe.names.index(name) % self.RING]

    def wait_bank(self, pe, name, t):
        n = self.pe.names.index(name)
        if n >= self.RING:
            who, what = self.taker[self.pe.names[n - self.RING]]
            pe.wait_ge(who.sem, who.after(what, t))
        else:
            last = max(m for m in range(self.pe.count) if m % self.RING == n % self.RING)
            who, what = self.taker[self.pe.names[last]]
            pe.wait_ge(who.sem, who.before(what, t))

    def start(self, sp, pool):
        if sp is not None:
            sp.dma_start(self.halves[:, :], self.consts["halves"]).then_inc(self.c_in, 16)
            sp.dma_start(self.upper[:, :], self.consts["upper"]).then_inc(self.c_in, 16)
            sp.dma_start(self.joins[:, :, :], self.consts["joins"].rearrange("p (s t) -> p s t", s=7)).then_inc(self.c_in, 16)
            sp.dma_start(self.falls[:, :, :], self.consts["falls"].rearrange("p (s t) -> p s t", s=6)).then_inc(self.c_in, 16)
            sp.dma_start(self.same[:, :, :], self.consts["same"].rearrange("p (s t) -> p s t", s=5)).then_inc(self.c_in, 16)
            sp.dma_start(self.sides[:, :, :], self.consts["sides"].rearrange("p (s t) -> p s t", s=2)).then_inc(self.c_in, 16)
            sp.dma_start(self.nw[:, :], self.prm["dn_norm_w"]).then_inc(self.c_in, 16)
        if pool is not None:
            pool.memset(self.eps[:, :], EPS).then_inc(self.ready, 1)
            pool.memset(self.one[:, :], 1.0).then_inc(self.ready, 1)
            pool.memset(self.x_pack[:, :, :], 0.0).then_inc(self.ready, 1)
            pool.memset(self.xt_pack[:, :, :], 0.0).then_inc(self.ready, 1)
            pool.memset(self.y_pack[:, :], 0.0).then_inc(self.ready, 1)
            pool.memset(self.S[:, :, :], 0.0).then_inc(self.ready, 1)
            pool.wait_ge(self.ready, 6)
            for who in (self.pe, self.v, self.a, self.p):
                pool.sem_inc(who.sem, who.count)

    def sync(self, sp, t):
        at = bass.ds(t * P, P)
        sp.wait_ge(self.v.sem, self.v.before("kn", t))
        sp.wait_ge(self.pe.sem, self.pe.before("vt", t))
        sp.dma_start(self.qkv[:, :, :], self.proj[T_DQ:T_DQ + 9, :, at].rearrange("m p t -> p m t")).then_inc(self.qkv_in, 16)
        sp.wait_ge(self.v.sem, self.v.before("diff", t))
        sp.wait_ge(self.p.sem, self.p.before("eb", t))
        alone(sp, self.stood)
        sp.dma_start(self.bc[:, :, :, :], self.rows[:, bass.ds(t * (DN_HEADS * P), DN_HEADS * P)]
                     .rearrange("r (h t) -> r h t", t=P).partition_broadcast(P)).then_inc(self.bc_in, 16)
        sp.wait_ge(self.v.sem, self.v.before("mix", t))
        alone(sp, self.stood)
        sp.dma_start(self.z[:, :, :], self.proj[T_DZ:T_DZ + 3, :, at].rearrange("m p t -> p m t")).then_inc(self.z_in, 16)

    def send(self, sp, t):
        sp.wait_ge(self.v.sem, self.v.after("mix", t))
        alone(sp, self.stood)
        sp.dma_start(self.mixed[:, 0:3, bass.ds(t * P, P)], self.mix[:, :, :]).then_inc(self.sent, 16)

    def tensor_first(self, pe, t):
        v, a, p = self.v, self.a, self.p
        me = self.pe
        q, k, val = self.qkv[:, 0:3, :], self.qkv[:, 3:6, :], self.qkv[:, 6:9, :]

        yield 0
        pe.wait_ge(p.sem, p.after("sq", t))
        for n, name in enumerate(("l2q", "l2k")):
            self.wait_bank(pe, name, t)
            pe.matmul(self.bank_of(name)[:, 0:3 * P], self.halves[:, :], self.sq[:, n, :],
                      start=True, stop=True).then_inc(me.step(name), 1)
        yield 1
        pe.wait_ge(v.sem, v.after("kn", t))
        self.wait_bank(pe, "kt", t)
        for m in range(3):
            last = pe.transpose(self.bank_of("kt")[:, m * P:(m + 1) * P], self.kn[:, m, :], self.ident[:, :])
        last.then_inc(me.step("kt"), 1)
        self.wait_bank(pe, "vt", t)
        for m in range(3):
            last = pe.transpose(self.bank_of("vt")[:, m * P:(m + 1) * P], val[:, m, :], self.ident[:, :])
        last.then_inc(me.step("vt"), 1)
        yield 2
        for what, other in (("kk", self.kn), ("qk", self.qn)):
            for g, name in enumerate((what + "A", what + "B")):
                self.wait_bank(pe, name, t)
                rows = slice(g * DH, (g + 1) * DH)
                for m in range(3):
                    last = pe.matmul(self.bank_of(name)[:, m * P:(m + 1) * P], self.kn[rows, m, :], other[rows, m, :],
                                     start=True, stop=True)
                last.then_inc(me.step(name), 1)
            yield 3 if what == "kk" else 4

    def tensor_then(self, pe, t):
        v, a, p = self.v, self.a, self.p
        me = self.pe
        cols, half = self.JOIN_COLS, self.JOIN_COLS // 2
        flat = "p m t -> p (m t)"
        yield 5
        pe.wait_ge(v.sem, v.after("l1", t))
        self.wait_bank(pe, "y1", t)
        for h in range(DN_HEADS):
            last = pe.matmul(self.bank_of("y1")[:, h * DH:(h + 1) * DH], self.L[:, 0, h, :], self.one[:, :], start=True, stop=True)
        last.then_inc(me.step("y1"), 1)
        prev = 1
        for n, s in enumerate(LEVELS):
            yield 6 + 2 * n
            name = f"y{s}"
            self.wait_bank(pe, name, t)
            if s > 2:
                pe.wait_ge(p.sem, p.after(f"l{s}", t))
            pe.wait_ge(v.sem, v.after(f"x{prev}", t))
            for h in range(DN_HEADS):
                last = pe.matmul(self.bank_of(name)[:, h * cols:(h + 1) * cols], self.L[:, n + 1, h, :],
                                 self.x_pack[:, n % 2, h * s:h * s + cols],
                                 start=True, stop=True)
            last.then_inc(me.step(name), 1)
            yield 6.7 + 2 * n
            name = f"x{s}"
            self.wait_bank(pe, name, t)
            pe.wait_ge(a.sem, a.after(f"y{s}", t))
            if s < 64:
                pe.wait_ge(v.sem, v.after(f"e{prev}", t))
                for h in range(DN_HEADS):
                    pe.matmul(self.bank_of(name)[:, h * half:(h + 1) * half], self.XT[:, h, :], self.y_pack[:, h * s:h * s + half],
                              start=True, stop=True)
            yield 7.3 + 2 * n
            pe.wait_ge(v.sem, v.after(f"f{s}", t))
            for h in range(DN_HEADS):
                w = max(s, half)
                to = (DN_HEADS + h) * half if s < 64 else h * s
                last = pe.matmul(self.bank_of(name)[:, to:to + w], self.Y[:, h, :], self.xt_pack[:, n % 2, h * s:h * s + w],
                                 start=True, stop=True)
            last.then_inc(me.step(name), 1)
            prev = s
        yield 18
        pe.wait_ge(v.sem, v.after("x64", t))
        self.wait_bank(pe, "u", t)
        for h in range(DN_HEADS):
            at = slice(h * DH, (h + 1) * DH)
            last = pe.matmul(self.bank_of("u")[:, at], self.XT[:, HX.index(h), :],
                             self.bv[:, :, :].rearrange(flat)[:, at], start=True, stop=True)
        last.then_inc(me.step("u"), 1)
        self.wait_bank(pe, "wt", t)
        for h in range(DN_HEADS):
            r = h % 2
            last = pe.matmul(self.bank_of("wt")[r * DH:(r + 1) * DH, (h // 2) * P:(h // 2 + 1) * P],
                             self.kb[:, h // 2, r * DH:(r + 1) * DH], self.XT[:, HX.index(h), :], start=True, stop=True)
        last.then_inc(me.step("wt"), 1)
        yield 19
        pe.wait_ge(v.sem, v.before("sn", t))
        pe.wait_ge(a.sem, a.after("wt", t))
        for name, lhs in (("ws", self.WT), ("o1", self.qn)):
            self.wait_bank(pe, name, t)
            for m in range(3):
                last = pe.matmul(self.bank_of(name)[:, m * P:(m + 1) * P], lhs[:, m, :], self.S[:, m, :],
                                 start=True, stop=True)
            last.then_inc(me.step(name), 1)
        yield 20
        pe.wait_ge(v.sem, v.after("vn", t))
        self.wait_bank(pe, "o2", t)
        for h in range(DN_HEADS):
            at = slice(h * DH, (h + 1) * DH)
            last = pe.matmul(self.bank_of("o2")[:, at], self.QK[:, HX.index(h), :],
                             self.vn[:, :, :].rearrange(flat)[:, at], start=True, stop=True)
        last.then_inc(me.step("o2"), 1)
        self.wait_bank(pe, "sn", t)
        for m in range(3):
            last = pe.matmul(self.bank_of("sn")[:, m * P:(m + 1) * P], self.kd[:, m, :], self.vn[:, m, :],
                             start=True, stop=True)
        last.then_inc(me.step("sn"), 1)
        yield 22.0
        pe.wait_ge(p.sem, p.after("on", t))
        self.wait_bank(pe, "ot", t)
        for m in range(3):
            last = pe.transpose(self.bank_of("ot")[:, m * P:(m + 1) * P], self.o[:, m, :], self.ident[:, :])
        last.then_inc(me.step("ot"), 1)

    def scalar_first(self, act, t):
        me, pe, v, p = self.a, self.pe, self.v, self.p
        yield 0.3
        for n, x in enumerate("qk"):
            act.wait_ge(pe.sem, pe.after("l2" + x, t))
            act.wait_ge(v.sem, v.before(x + "n", t))
            act.activation(self.rs[:, n, :], self.bank_of("l2" + x)[:, 0:3 * P], ACT.Ln,
                           bias=self.eps[:, :]).then_inc(me.step("ln" + x), 1)
            act.wait_ge(me.sem, me.after("ln" + x, t))
            act.activation(self.rs[:, n, :], self.rs[:, n, :], ACT.Exp, scale=-0.5).then_inc(me.step("rs" + x), 1)
        yield 0.7
        act.wait_ge(v.sem, v.after("diff", t))
        act.activation(self.E[:, :, :], self.E[:, :, :], ACT.Exp).then_inc(me.step("e"), 1)

    def scalar_then(self, act, t):
        me, pe, v = self.a, self.pe, self.v
        for n, s in enumerate(LEVELS):
            yield 6.3 + 2 * n
            act.wait_ge(pe.sem, pe.after(f"y{s}", t))
            act.activation(self.y_pack[:, 0:DN_HEADS * s].rearrange("p (h c) -> p h c", c=s),
                           self.bank_of(f"y{s}")[:, 0:DN_HEADS * self.JOIN_COLS].rearrange("p (h c) -> p h c", c=self.JOIN_COLS)[:, :, 0:s],
                           ACT.Copy).then_inc(me.step(f"y{s}"), 1)
        yield 18.3
        for name, dst in (("u", self.U), ("wt", self.WT)):
            act.wait_ge(pe.sem, pe.after(name, t))
            act.activation(dst[:, :, :], self.bank_of(name)[:, 0:3 * P].rearrange("p (h t) -> p h t", h=3),
                           ACT.Copy).then_inc(me.step(name), 1)
        yield 21.4
        act.wait_ge(v.sem, v.after("ssq", t))
        act.activation(self.ors[:, :], self.ssq[:, :], ACT.Ln, bias=self.eps[:, :], scale=1.0 / DH).then_inc(me.step("lno"), 1)
        act.wait_ge(me.sem, me.after("lno", t))
        act.activation(self.ors[:, :], self.ors[:, :], ACT.Exp, scale=-0.5).then_inc(me.step("rso"), 1)

    def joined(self, pool, n, t):
        pool.wait_ge(self.pe.sem, self.pe.before(f"y{2 ** n}", t))
        pool.tensor_tensor(self.L[:, n, :, :], self.AT[:, :, :], self.joins[:, n:n + 1, :].to_broadcast([P, DN_HEADS, P]),
                           ALU.mult).then_inc(self.p.step(f"l{2 ** n}"), 1)

    def gpsimd_first(self, pool, t):
        me, v, a, pe = self.p, self.v, self.a, self.pe

        yield 0
        pool.wait_ge(self.qkv_in, t * 16 + 16)
        pool.wait_ge(pe.sem, pe.before("l2k", t))
        pool.tensor_tensor(self.sq[:, :, :], self.qkv[:, 0:6, :].rearrange("p (a m) t -> p a (m t)", a=2),
                           self.qkv[:, 0:6, :].rearrange("p (a m) t -> p a (m t)", a=2), ALU.mult).then_inc(me.step("sq"), 1)
        yield 0.8
        pool.wait_ge(a.sem, a.after("e", t))
        pool.tensor_tensor(self.E[:, :, :], self.E[:, :, :], self.upper[:, None, :].to_broadcast([P, DN_HEADS, P]),
                           ALU.mult).then_inc(me.step("em"), 1)
        pool.wait_ge(me.sem, me.after("em", t))
        pool.wait_ge(v.sem, v.before("atB", t))
        pool.tensor_tensor(self.EB[:, :, :], self.E[:, :, :], self.bc[:, 1, :, :], ALU.mult).then_inc(me.step("eb"), 1)
        yield 2.7
        pool.wait_ge(v.sem, v.after("atB", t))
        self.joined(pool, 2, t)
        self.joined(pool, 3, t)

    def gpsimd_then(self, pool, t):
        me, pe, v, a = self.p, self.pe, self.v, self.a
        for n in range(4, 7):
            yield 2 * n - 2.4
            self.joined(pool, n, t)
        yield 14
        pool.wait_ge(v.sem, v.before("sn", t))
        pool.tensor_tensor(self.Sg[:, :, :], self.S[:, :, :],
                           self.gates[:, bass.ds(t, 1), 48:51].rearrange("p a h -> p (a h)")[:, :, None]
                           .to_broadcast([P, 3, P]), ALU.mult).then_inc(me.step("sg"), 1)
        yield 20.9
        pool.wait_ge(v.sem, v.after("o2", t))
        pool.tensor_tensor(self.osq[:, :, :], self.o[:, :, :], self.o[:, :, :], ALU.mult).then_inc(me.step("osq"), 1)
        yield 21.7
        pool.wait_ge(a.sem, a.after("rso", t))
        o = self.o[:, :, :].rearrange("p m (r d) -> p (m r) d", r=2)
        pool.tensor_tensor(o, o, self.ors[:, :, None].to_broadcast([P, DN_HEADS, DH]), ALU.mult).then_inc(me.step("on"), 1)

    def by_head(self, t, at):
        return (self.gates[:, bass.ds(t, 1), at:at + 6].rearrange("p a (r m) -> p (a m) r", r=2)[:, :, :, None]
                .to_broadcast([P, 3, 2, DH]))

    def vector_first(self, dve, t):
        me, pe, a, p = self.v, self.pe, self.a, self.p
        four = "p (m r d) -> p m r d"
        q, k = self.qkv[:, 0:3, :], self.qkv[:, 3:6, :]
        rs = [self.rs[:, n, :].rearrange("p (m t) -> p m t", m=3) for n in range(2)]
        yield 0.5
        dve.wait_ge(a.sem, a.after("rsq", t))
        dve.wait_ge(pe.sem, pe.before("o1", t))
        dve.scalar_tensor_tensor(self.qn[:, :, :], q, DH ** -0.5, rs[0], ALU.mult, ALU.mult).then_inc(me.step("qn"), 1)
        dve.wait_ge(a.sem, a.after("rsk", t))
        dve.tensor_tensor(self.kn[:, :, :], k, rs[1], ALU.mult).then_inc(me.step("kn"), 1)
        dve.wait_ge(self.bc_in, t * 16 + 16)
        dve.wait_ge(p.sem, p.before("eb", t))
        for h in range(DN_HEADS):
            last = dve.tensor_scalar(self.E[:, h, :], self.bc[:, 0, h, :],
                                     self.gates[:, bass.ds(t, 1), 6 + h], 0.0, ALU.subtract, ALU.min)
        last.then_inc(me.step("diff"), 1)
        yield 1.5
        dve.wait_ge(pe.sem, pe.after("kt", t))
        kt = self.bank_of("kt")[:, 0:3 * P].rearrange(four, m=3, r=2)
        dve.tensor_tensor(self.kb[:, :, :].rearrange("p m (r d) -> p m r d", r=2), kt, self.by_head(t, 36),
                          ALU.mult).then_inc(me.step("kb"), 1)
        dve.tensor_tensor(self.kd[:, :, :].rearrange("p m (r d) -> p m r d", r=2), kt, self.by_head(t, 42),
                          ALU.mult).then_inc(me.step("kd"), 1)
        dve.wait_ge(pe.sem, pe.after("vt", t))
        dve.tensor_tensor(self.bv[:, :, :].rearrange("p m (r d) -> p m r d", r=2),
                          self.bank_of("vt")[:, 0:3 * P].rearrange(four, m=3, r=2), self.by_head(t, 0),
                          ALU.mult).then_inc(me.step("bv"), 1)
        yield 2.5
        dve.wait_ge(p.sem, p.after("eb", t))
        for name, src, dec, dst in (("at", "kk", self.EB, self.AT), ("qk", "qk", self.E, self.QK)):
            for g, G in enumerate("AB"):
                dve.wait_ge(pe.sem, pe.after(src + G, t))
                at = slice(3 * g, 3 * g + 3)
                dve.tensor_tensor(dst[:, at, :], self.bank_of(src + G)[:, 0:3 * P].rearrange("p (h t) -> p h t", h=3),
                                  dec[:, at, :], ALU.mult).then_inc(me.step(name + G), 1)
            if name == "at":
                dve.wait_ge(me.sem, me.after("atB", t))
                for n in range(2):
                    dve.wait_ge(pe.sem, pe.before(f"y{2 ** n}", t))
                    dve.tensor_tensor(self.L[:, n, :, :], self.AT[:, :, :],
                                      self.joins[:, n:n + 1, :].to_broadcast([P, DN_HEADS, P]),
                                      ALU.mult).then_inc(me.step(f"l{2 ** n}"), 1)
                    if n == 0:
                        dve.wait_ge(me.sem, me.after("l1", t))
                        dve.tensor_reduce(self.first[:, :], self.L[:, 0, :, :], AX.X, ALU.add).then_inc(me.step("r1"), 1)
                yield 3.5

    def vector_then(self, dve, t):
        me, pe, a, p = self.v, self.pe, self.a, self.p
        four = "p (m r d) -> p m r d"
        half = self.JOIN_COLS // 2
        yield 5.5
        up, low = self.sides[:, 0, :], self.sides[:, 1, :]
        x, xt = (pack[:, 0, 0:2 * DN_HEADS].rearrange("p (h c) -> p h c", c=2) for pack in (self.x_pack, self.xt_pack))
        heads = [P, DN_HEADS]
        dve.wait_ge(me.sem, me.after("r1", t))
        dve.wait_ge(pe.sem, pe.after("y1", t))
        dve.tensor_tensor(x[:, :, 0], up[:, 0:1].to_broadcast(heads), self.bank_of("y1")[:, 0:DN_HEADS * DH:DH], ALU.subtract)
        dve.tensor_copy(x[:, :, 1], low[:, 0:1].to_broadcast(heads))
        dve.tensor_copy(xt[:, :, 0], up[:, 0:1].to_broadcast(heads))
        dve.tensor_tensor(xt[:, :, 1], low[:, 0:1].to_broadcast(heads), self.first[:, :],
                          ALU.subtract).then_inc(me.step("x1"), 1)

        def spread(n):
            w = 2 ** (n + 1)
            blocks = [P, DN_HEADS, P // w, w]
            src = self.xt_pack[:, n % 2, 0:DN_HEADS * w].rearrange("p (h c) -> p h c", c=w)
            dve.wait_ge(me.sem, me.after(f"x{w // 2}", t))
            if n == 0:
                dve.wait_ge(pe.sem, pe.before("wt", t))
            dve.tensor_tensor(self.XT[:, :, :].rearrange("p h (b c) -> p h b c", c=w),
                              src[:, :, None, :].to_broadcast(blocks),
                              self.same[:, n, :].rearrange("p (b c) -> p b c", c=w)[:, None, :, :].to_broadcast(blocks),
                              ALU.mult).then_inc(me.step(f"e{w // 2}"), 1)

        spread(0)
        for n, s in enumerate(LEVELS):
            yield 6.6 + 2 * n
            blocks = [P, DN_HEADS, P // s, s]
            dve.wait_ge(a.sem, a.after(f"y{s}", t))
            dve.tensor_tensor(self.Y[:, :, :].rearrange("p h (b c) -> p h b c", c=s),
                              self.y_pack[:, 0:DN_HEADS * s].rearrange("p (h c) -> p h c", c=s)[:, :, None, :].to_broadcast(blocks),
                              self.falls[:, n, :].rearrange("p (b c) -> p b c", c=s)[:, None, :, :].to_broadcast(blocks),
                              ALU.mult).then_inc(me.step(f"f{s}"), 1)
            yield 7.5 + 2 * n
            def packed(pack, width):
                return pack[:, 0:DN_HEADS * width].rearrange("p (h c) -> p h c", c=width)

            bank = self.bank_of(f"x{s}")
            xt_old = packed(self.xt_pack[:, n % 2, :], s)
            if s < 64:
                x_old, x_new = packed(self.x_pack[:, n % 2, :], s), packed(self.x_pack[:, 1 - n % 2, :], 2 * s)
                xt_new = packed(self.xt_pack[:, 1 - n % 2, :], 2 * s)
                dve.wait_ge(pe.sem, pe.after(f"x{s}", t))
                dve.scalar_tensor_tensor(x_new[:, :, 0:s], x_old, up[:, n + 1:n + 2], packed(bank, half)[:, :, 0:s], ALU.mult, ALU.subtract)
                dve.tensor_scalar(x_new[:, :, s:2 * s], x_old, low[:, n + 1:n + 2], None, ALU.mult)
                product = packed(bank[:, DN_HEADS * half:2 * DN_HEADS * half], half)[:, :, 0:s]
            else:
                xt_new = self.XT[:, :, :]
                dve.wait_ge(pe.sem, pe.after(f"x{s}", t))
                product = packed(bank, s)
            dve.tensor_scalar(xt_new[:, :, 0:s], xt_old, up[:, n + 1:n + 2], None, ALU.mult)
            dve.scalar_tensor_tensor(xt_new[:, :, s:2 * s], xt_old, low[:, n + 1:n + 2], product,
                                     ALU.mult, ALU.subtract).then_inc(me.step(f"x{s}"), 1)
            if s < 32:
                spread(n + 1)
        yield 19.5
        m3 = "p (m t) -> p m t"
        dve.wait_ge(pe.sem, pe.after("ws", t))
        dve.wait_ge(a.sem, a.after("u", t))
        dve.tensor_tensor(self.vn[:, :, :], self.U[:, :, :], self.bank_of("ws")[:, 0:3 * P].rearrange(m3, m=3),
                          ALU.subtract).then_inc(me.step("vn"), 1)
        dve.wait_ge(pe.sem, pe.after("o1", t))
        dve.tensor_tensor(self.o[:, :, :].rearrange("p m (r d) -> p m r d", r=2),
                          self.bank_of("o1")[:, 0:3 * P].rearrange(four, m=3, r=2), self.by_head(t, 30),
                          ALU.mult).then_inc(me.step("o1"), 1)
        yield 20.5
        dve.wait_ge(pe.sem, pe.after("o2", t))
        dve.wait_ge(me.sem, me.after("o1", t))
        dve.tensor_tensor(self.o[:, :, :], self.o[:, :, :], self.bank_of("o2")[:, 0:3 * P].rearrange(m3, m=3),
                          ALU.add).then_inc(me.step("o2"), 1)
        dve.wait_ge(pe.sem, pe.after("sn", t))
        dve.wait_ge(p.sem, p.after("sg", t))
        for r in range(2):
            at = slice(r * DH, (r + 1) * DH)
            last = dve.tensor_tensor(self.S[at, :, at], self.Sg[at, :, at],
                                     self.bank_of("sn")[at, 0:3 * P].rearrange(m3, m=3)[:, :, at], ALU.add)
        last.then_inc(me.step("sn"), 1)
        yield 21.15
        dve.wait_ge(p.sem, p.after("osq", t))
        dve.tensor_reduce(self.ssq[:, :], self.osq[:, :, :].rearrange("p m (r d) -> p (m r) d", r=2), AX.X,
                          ALU.add).then_inc(me.step("ssq"), 1)
        yield 22.7
        dve.wait_ge(pe.sem, pe.after("ot", t))
        dve.wait_ge(self.z_in, t * 16 + 16)
        if not isinstance(t, int) or t:
            dve.wait_ge(self.sent, t * 16)
        dve.scalar_tensor_tensor(self.mix[:, :, :], self.bank_of("ot")[:, 0:3 * P].rearrange(m3, m=3), self.nw[:, :],
                                 self.z[:, :, :], ALU.mult, ALU.mult).then_inc(me.step("mix"), 1)


HEADS = [(hh, g) for hh in range(HPG) for g in range(2)]
WK = (WINDOW + P) // P
LOW = -3.0e38


class Nsa:

    RING = 4
    PT_RING = 4
    AHEAD = 2
    S_RING = AHEAD + 1

    def __init__(self, sc, banks, outs, consts, proj, gates, kc, vc, vs, ks, vw, kw, spare, mixed, ident):
        self.consts, self.proj, self.gates, self.mixed, self.ident = consts, proj, gates, mixed, ident
        self.kc, self.vc, self.vs, self.ks, self.vw, self.kw = kc, vc, vs, ks, vw, kw
        self.bank, self.out_bank = banks, outs
        sb = sc.sb
        self.q_raw, self.q = sb("q_raw", [P, HPG, P]), sb("q", [P, 6, P])
        self.cp = sb("cp", [P, 6, P])
        self.psum_heads = sb("psum_heads", [P, 2, P + 4])
        self.imp, self.score, self.left, self.selb = (sb(n, [P, 2, N_BLK]) for n in ("imp", "score", "left", "selb"))
        self.top = sb("top", [P, 2, 8])
        self.last_mask = sb("last_mask", [P, 2, NB])
        self.win_mask = sb("win_mask", [P, WINDOW + P])
        self.sx = sb("sx", [P, self.S_RING, SEQ])
        self.mx = sb("mx", [P, self.S_RING, 4])
        self.nm = sb("nm", [P, self.S_RING])
        self.cmx = sb("cmx", [P, 6])
        self.rsum, self.coef = sb("rsum", [P, 3, 6]), sb("coef", [P, 3, 6])
        self.pt = sb("pt", [P, self.PT_RING, NB])
        self.acc, self.part = sb("acc", [P, 6, DH]), sb("part", [P, 6, DH])
        self.mix = sb("mix", [P, 3, P])
        self.seen, self.cbias = sb("seen", [P, 2 * P - 8]), sb("cbias", [P, 2 * P - 8])
        self.elig, self.add = sb("elig", [P, 2 * N_BLK - 2]), sb("add", [P, 2 * N_BLK - 2])
        self.causal = sb("causal", [P, P])
        spare = spare[:, :, :].rearrange("p c t -> p (c t)")
        self.before_start = spare[:, 0:WINDOW + SEQ]
        self.band = spare[:, WINDOW + SEQ:2 * WINDOW + SEQ + P]
        self.c_in, self.q_in, self.sent, self.zeroed = (sc.sem(n) for n in ("c_in", "q_in", "sent", "zeroed"))
        self.stood = sc.sem("stood")
        self.sems = {n: sc.sem(n) for n in ("pe", "dve", "act", "pool")}
        self.spans = []
        base = None
        for s in range(4):
            lists = self.names(s)
            if base is None:
                self.credit = {n: max(len(self.names(z)[n].split()) for z in range(4)) for n in lists}
                base = dict(self.credit)
            span = {n: SpanSteps(self.sems[n], lists[n], base[n]) for n in lists}
            self.spans.append(span)
            base = {n: base[n] + 4 * span[n].count for n in lists}

    def items(self, s):
        win = [(f"w{n}", [4, 1]) for n in range(6)]
        return win + [(f"s{n}", [4] * (s + 1)) for n in range(6)]

    def order(self, s):
        items = self.items(s)
        yield "c", None, 0, 1.4

        def scores(k):
            for c, tiles in enumerate(items[k][1]):
                yield "q", k, c, 0.22 * tiles

        for k in range(self.AHEAD):
            yield from scores(k)
        for k, (_, pieces) in enumerate(items):
            ahead = list(scores(k + self.AHEAD)) if k + self.AHEAD < len(items) else []
            if k == 1:
                yield from ahead
                yield "ct", None, 0, 0.7
                ahead = []
            if k == 2:
                yield from ahead
                yield "cv", None, 0, 0.7
                ahead = []
            for c, tiles in enumerate(pieces):
                yield "t", k, c, 0.21 * tiles
                if ahead:
                    yield ahead.pop(0)
                if c:
                    yield "v", k, c - 1, 0.21 * pieces[c - 1]
            yield from ahead
            yield "v", k, len(pieces) - 1, 0.21 * pieces[-1]
        yield "end", None, 0, 0.4

    def places(self, s):
        total = sum(e[3] for e in self.order(s))
        at, out = 0.0, {}
        for what, k, c, cost in self.order(s):
            out[what, k, c] = (at / total, cost / total)
            at += cost
        return out

    def names(self, s):
        items = self.items(s)
        pe, act, dve = [], ["ce"], ["c0", "c1", "cx"]
        for what, k, c, _ in self.order(s):
            if what == "c":
                pe += ["c0", "c1"]
            elif what == "ct":
                pe += ["ct0", "ct1"]
                act += ["ct0", "ct1"]
            elif what == "cv":
                pe += ["co"]
                dve += ["ocoef", "oc"]
            elif what == "end":
                pe += ["ot"]
                act += ["ot"]
            else:
                name = f"{items[k][0]}{what}{c}"
                pe += [name]
                if what == "t":
                    act += [name]
                if what == "q":
                    dve += [name]
                    if c == len(items[k][1]) - 1:
                        dve += [items[k][0] + "x"]
                        act += [items[k][0] + "e"]
                        if k == 1:
                            dve += ["cr"]
                        if k == 3:
                            dve += "imp1 imp2 sc1 sc2 sc3 top left ne el selb".split()
                        if k == 8:
                            dve += "rw cw ow aw".split()
        dve += "rs cs os as".split()
        return {"pe": " ".join(pe), "act": " ".join(act), "dve": " ".join(dve), "pool": "qz wm pc1 pc2 hs1 hs2 lm1 lm2"}

    def ring(self, s, name, kind):
        if kind == "bank":
            names = [n for n in self.spans[s]["pe"].names if n != "co" and "v" not in n]
            size = self.RING
        else:
            names = [n for n in self.spans[s]["pe"].names if "t" in n and n != "ot"]
            size = self.PT_RING
        n = names.index(name)
        if n >= size:
            return n % size, names[n - size], False
        return n, names[max(m for m in range(len(names)) if m % size == n)], True

    def bank_of(self, s, name):
        return self.bank[self.ring(s, name, "bank")[0]]

    def pt_of(self, s, name):
        return self.pt[:, self.ring(s, name, "pt")[0], :]

    def wait_bank(self, pe, s, name, t):
        _, old, earlier = self.ring(s, name, "bank")
        who = self.spans[s]["dve" if old in self.spans[s]["dve"].names else "act"]
        pe.wait_ge(who.sem, (who.before if earlier else who.after)(old, t))

    def load(self, sp):
        for dst, name in ((self.seen, "cmp_seen"), (self.cbias, "cmp_bias"), (self.elig, "blk_elig"), (self.add, "blk_add"),
                          (self.causal, "causal"), (self.band, "band")):
            sp.dma_start(dst[:, :], self.consts[name]).then_inc(self.c_in, 16)

    def start(self, pool):
        pool.memset(self.q[:, :, :], 0.0).then_inc(self.zeroed, 1)
        pool.memset(self.psum_heads[:, :, :], 0.0).then_inc(self.zeroed, 1)
        pool.wait_ge(self.zeroed, 2)
        for n, sem in self.sems.items():
            pool.sem_inc(sem, self.credit[n])
        pool.memset(self.before_start[:, 0:WINDOW], NEG).then_inc(self.zeroed, 1)
        pool.memset(self.before_start[:, WINDOW:WINDOW + SEQ], 0.0).then_inc(self.zeroed, 1)
        pool.wait_ge(self.zeroed, 4)

    def join(self, eng, s):
        for who in self.spans[s].values():
            eng.wait_ge(who.sem, who.base)

    def sync(self, sp, s, t):
        pool = self.spans[s]["pool"]
        sp.wait_ge(pool.sem, pool.before("qz", t))
        sp.dma_start(self.q_raw[:, :, :], self.proj[T_NQ:T_NQ + 3, :, bass.ds(t * P + s * 4 * P, P)]
                     .rearrange("m p t -> p m t")).then_inc(self.q_in, 16)

    def send(self, sp, s, t):
        act = self.spans[s]["act"]
        sp.wait_ge(act.sem, act.after("ot", t))
        sp.dma_start(self.mixed[:, 5:8, bass.ds(t * P + s * 4 * P, P)], self.mix[:, :, :]).then_inc(self.sent, 16)

    def tensor(self, pe, s, t):
        span = self.spans[s]
        me, v, a, p = span["pe"], span["dve"], span["act"], span["pool"]
        items = self.items(s)
        places = self.places(s)
        for what, k, c, _ in self.order(s):
            yield places[what, k, c][0]
            if k is not None:
                item, pieces = items[k]
                tiles = pieces[c]
                name = f"{item}{what}{c}"
                hh, g = HEADS[k % 6]
                h = g * HPG + hh
            if what == "c":
                pe.wait_ge(p.sem, p.after("qz", t))
                for n in range(2):
                    self.wait_bank(pe, s, f"c{n}", t)
                    for m in range(3):
                        last = pe.matmul(self.bank_of(s, f"c{n}")[:, m * P:(m + 1) * P], self.q[:, 3 * n + m, :],
                                         self.kc[:, :], start=True, stop=True)
                    last.then_inc(me.step(f"c{n}"), 1)
            elif what == "q":
                self.wait_bank(pe, s, name, t)
                if k < 6:
                    keys = self.kw[:, bass.ds(t * P + (s * 4 * P + c * NB), tiles * P)]
                else:
                    keys = self.ks[:, c * NB:c * NB + tiles * P]
                pe.matmul(self.bank_of(s, name)[:, 0:tiles * P], self.q[:, k % 6, :], keys,
                          start=True, stop=True).then_inc(me.step(name), 1)
            elif what == "ct":
                pe.wait_ge(p.sem, p.after("pc2", t))
                for n in range(2):
                    self.wait_bank(pe, s, f"ct{n}", t)
                    for m in range(3):
                        last = pe.transpose(self.bank_of(s, f"ct{n}")[:, m * P:(m + 1) * P], self.cp[:, 3 * n + m, :],
                                            self.ident[:, :])
                    last.then_inc(me.step(f"ct{n}"), 1)
            elif what == "cv":
                pe.wait_ge(v.sem, v.before("os", t))
                for n in range(6):
                    hh, g = HEADS[n]
                    if n % 3 == 0:
                        pe.wait_ge(a.sem, a.after(f"ct{n // 3}", t))
                    h = g * HPG + hh
                    last = pe.matmul(self.out_bank[0][:, h * DH:(h + 1) * DH],
                                     self.pt_of(s, f"ct{n // 3}")[:, (n % 3) * P:(n % 3 + 1) * P],
                                     self.vc[:, g * DH:(g + 1) * DH], start=True, stop=True)
                last.then_inc(me.step("co"), 1)
            elif what == "t":
                if c == 0:
                    pe.wait_ge(a.sem, a.after(item + "e", t))
                self.wait_bank(pe, s, name, t)
                for m in range(tiles):
                    at = c * NB + m * P
                    last = pe.transpose(self.bank_of(s, name)[:, m * P:(m + 1) * P], self.sx[:, k % self.S_RING, at:at + P],
                                        self.ident[:, :])
                last.then_inc(me.step(name), 1)
            elif what == "v":
                if k == 0 and c == 0:
                    pe.wait_ge(v.sem, v.before("ow", t))
                if k == 6 and c == 0:
                    pe.wait_ge(v.sem, v.after("oc", t))
                pe.wait_ge(a.sem, a.after(f"{item}t{c}", t))
                for m in range(tiles):
                    kt = 4 * c + m
                    if k < 6:
                        vals = self.vw[:, bass.ds(t + (4 * s + kt), 1), g * DH:(g + 1) * DH].rearrange("p a d -> p (a d)")
                    else:
                        vals = self.vs[:, kt, g * DH:(g + 1) * DH]
                    last = pe.matmul(self.out_bank[1 if k < 6 else 0][:, h * DH:(h + 1) * DH],
                                     self.pt_of(s, f"{item}t{c}")[:, m * P:(m + 1) * P], vals,
                                     start=kt == 0, stop=kt == sum(pieces) - 1)
                last.then_inc(me.step(name), 1)
            else:
                pe.wait_ge(v.sem, v.after("as", t))
                self.wait_bank(pe, s, "ot", t)
                for m in range(3):
                    last = pe.transpose(self.bank_of(s, "ot")[:, m * P:(m + 1) * P],
                                        self.acc[:, 2 * m:2 * m + 2, :].rearrange("p h d -> p (h d)"), self.ident[:, :])
                last.then_inc(me.step("ot"), 1)

    def scalar(self, act, s, t):
        span = self.spans[s]
        me, v, pe, p = span["act"], span["dve"], span["pe"], span["pool"]
        items = self.items(s)

        def take(name):
            _, old, earlier = self.ring(s, name, "pt")
            old = "co" if old[0] == "c" else old.replace("t", "v")
            act.wait_ge(pe.sem, (pe.before if earlier else pe.after)(old, t))
            act.wait_ge(pe.sem, pe.after(name, t))
            tiles = 3 if name[0] == "c" else 1 if name[0] == "w" and name[-1] == "1" else 4
            act.activation(self.pt_of(s, name)[:, 0:tiles * P], self.bank_of(s, name)[:, 0:tiles * P],
                           ACT.Copy).then_inc(me.step(name), 1)

        places = self.places(s)

        def place(what, k, c, into):
            at, cost = places[what, k, c]
            return at + into * cost

        yield place("c", None, 0, 0.7)
        act.wait_ge(v.sem, v.after("cx", t))
        for n in range(6):
            hh, g = HEADS[n]
            last = act.activation(self.cp[:, n, :], self.cp[:, n, :], ACT.Exp, bias=self.cmx[:, n:n + 1],
                                  accum_out=self.rsum[:, 0, g * HPG + hh:g * HPG + hh + 1])
        last.then_inc(me.step("ce"), 1)
        for what, k, c, _ in self.order(s):
            if what == "q" and c == len(items[k][1]) - 1:
                yield place(what, k, c, 0.7)
                item, pieces = items[k]
                hh, g = HEADS[k % 6]
                h = g * HPG + hh
                width = sum(pieces) * P
                act.wait_ge(v.sem, v.after(item + "x", t))
                if k == 0:
                    act.wait_ge(v.sem, v.before("rw", t))
                if k == 6:
                    act.wait_ge(v.sem, v.before("rs", t))
                act.activation(self.sx[:, k % self.S_RING, 0:width], self.sx[:, k % self.S_RING, 0:width], ACT.Exp,
                               bias=self.nm[:, k % self.S_RING:k % self.S_RING + 1],
                               accum_out=self.rsum[:, 1 if k < 6 else 2, h:h + 1]).then_inc(me.step(item + "e"), 1)
            elif what == "ct":
                yield place(what, k, c, 0.5)
                take("ct0")
                take("ct1")
            elif what == "t":
                yield place(what, k, c, 0.5)
                take(f"{items[k][0]}t{c}")
            elif what == "end":
                yield place(what, k, c, 0.9)
                act.wait_ge(pe.sem, pe.after("ot", t))
                act.wait_ge(self.sent, t * 16 + s * 64)
                act.activation(self.mix[:, :, :], self.bank_of(s, "ot")[:, 0:3 * P].rearrange("p (m t) -> p m t", m=3),
                               ACT.Copy).then_inc(me.step("ot"), 1)

    def gpsimd(self, pool, s, t):
        span = self.spans[s]
        me, v, pe, a = span["pool"], span["dve"], span["pe"], span["act"]
        places = self.places(s)
        yield 0.0
        pool.wait_ge(self.q_in, t * 16 + (64 * s + 16))
        pool.wait_ge(pe.sem, pe.before(f"s5q{s}", t))
        for g in range(2):
            at = slice(g * DH, (g + 1) * DH)
            if g:
                pool.wait_ge(me.sem, me.before("lm2", t))
            alone(pool, self.stood)
            last = pool.tensor_scalar(self.q[at, g:6:2, :], self.q_raw[at, :, :], DH ** -0.5, 1.0, ALU.mult, ALU.mult)
            if g == 0:
                last.then_inc(self.zeroed, 1)
                pool.wait_ge(self.zeroed, t + (4 * s + 5))
        last.then_inc(me.step("qz"), 1)
        pool.wait_ge(me.sem, me.after("qz", t))
        pool.wait_ge(v.sem, v.before("w5q1", t))
        pool.tensor_tensor(self.win_mask[:, :], self.band[:, :], self.before_start[:, bass.ds(t * P + s * 4 * P, WINDOW + P)],
                           ALU.add).then_inc(me.step("wm"), 1)
        at, cost = places["q", 1, 1]
        yield at + 0.7 * cost
        pool.wait_ge(v.sem, v.after("cr", t))
        rinv = self.coef[:, 0, :].rearrange("p (g m) -> p m g", g=2)[:, :, :, None].to_broadcast([P, HPG, 2, P])
        cp = self.cp[:, :, :].rearrange("p (m g) n -> p m g n", g=2)
        pool.tensor_tensor(cp, cp, rinv, ALU.mult).then_inc(me.step("pc1"), 1)
        pool.wait_ge(me.sem, me.after("pc1", t))
        seen = self.seen[:, bass.ds(t * -8 + (P - 8 - 32 * s), P)]
        pool.tensor_tensor(self.cp[:, :, :], self.cp[:, :, :], seen[:, None, :].to_broadcast([P, 6, P]),
                           ALU.mult).then_inc(me.step("pc2"), 1)
        pool.wait_ge(me.sem, me.after("pc2", t))
        pool.wait_ge(v.sem, v.before("imp2", t))
        pool.tensor_tensor(self.psum_heads[:, :, 1:1 + P], self.cp[:, 0:2, :], self.cp[:, 2:4, :],
                           ALU.add).then_inc(me.step("hs1"), 1)
        pool.wait_ge(me.sem, me.after("hs1", t))
        pool.tensor_tensor(self.psum_heads[:, :, 1:1 + P], self.psum_heads[:, :, 1:1 + P], self.cp[:, 4:6, :],
                           ALU.add).then_inc(me.step("hs2"), 1)
        at, cost = places["q", 3, 1]
        yield at + 0.7 * cost
        pool.wait_ge(v.sem, v.after("selb", t))
        blocks = self.selb[:, :, 8 * s:8 * s + 8]
        pool.wait_ge(v.sem, v.before(f"s5q{s}", t))
        alone(pool, self.stood)
        pool.tensor_copy(self.last_mask[:, :, :].rearrange("p g (b k) -> p g b k", k=SEL_BLOCK),
                         blocks[:, :, :, None].to_broadcast([P, 2, 8, SEL_BLOCK])).then_inc(me.step("lm1"), 1)
        pool.wait_ge(me.sem, me.after("lm1", t))
        diag = self.last_mask[:, :, bass.ds(t * P, P)]
        pool.tensor_tensor(diag, diag, self.causal[:, None, :].to_broadcast([P, 2, P]), ALU.add).then_inc(me.step("lm2"), 1)

    def vector(self, dve, s, t):
        span = self.spans[s]
        me, pe, a, p = span["dve"], span["pe"], span["act"], span["pool"]
        items = self.items(s)
        places = self.places(s)

        def place(what, k, c, into):
            at, cost = places[what, k, c]
            return at + into * cost

        yield place("c", None, 0, 0.5)
        cbias = self.cbias[:, bass.ds(t * -8 + (P - 8 - 32 * s), P)]
        dve.wait_ge(pe.sem, pe.before("ct1", t))
        for n in range(2):
            dve.wait_ge(pe.sem, pe.after(f"c{n}", t))
            dve.tensor_tensor(self.cp[:, 3 * n:3 * n + 3, :],
                              self.bank_of(s, f"c{n}")[:, 0:3 * P].rearrange("p (h n) -> p h n", h=3),
                              cbias[:, None, :].to_broadcast([P, 3, P]), ALU.add).then_inc(me.step(f"c{n}"), 1)
        dve.wait_ge(me.sem, me.after("c1", t))
        dve.tensor_reduce(self.cmx[:, :], self.cp[:, :, :], AX.X, ALU.max, negate=True).then_inc(me.step("cx"), 1)

        def masked(k):
            yield place("q", k, 0, 0.5)
            item, pieces = items[k]
            g = HEADS[k % 6][1]
            if k < self.S_RING:
                dve.wait_ge(pe.sem, pe.before(f"s{6 - self.S_RING + k}t{s}", t))
            else:
                old = items[k - self.S_RING]
                dve.wait_ge(pe.sem, pe.after(f"{old[0]}t{len(old[1]) - 1}", t))
            if k == 0:
                dve.wait_ge(p.sem, p.after("wm", t))
            if k == 6:
                dve.wait_ge(p.sem, p.after("lm2", t))
            for c, tiles in enumerate(pieces):
                if c:
                    yield place("q", k, c, 0.5)
                w = tiles * P
                dve.wait_ge(pe.sem, pe.after(f"{item}q{c}", t))
                out, src = self.sx[:, k % self.S_RING, c * NB:c * NB + w], self.bank_of(s, f"{item}q{c}")[:, 0:w]
                if k < 6:
                    mask = self.win_mask[:, c * NB:c * NB + w]
                elif c == s:
                    mask = self.last_mask[:, g, :]
                else:
                    out, src = (x.rearrange("p (b k) -> p b k", k=SEL_BLOCK) for x in (out, src))
                    mask = self.selb[:, g, 8 * c:8 * c + 8][:, :, None].to_broadcast([P, 8, SEL_BLOCK])
                alone(dve, self.stood)
                dve.tensor_tensor_reduce(out, src, mask, 1.0, LOW, ALU.add, ALU.max,
                                         self.mx[:, k % self.S_RING, c:c + 1]).then_inc(me.step(f"{item}q{c}"), 1)
            dve.wait_ge(me.sem, me.after(f"{item}q{len(pieces) - 1}", t))
            if k < self.S_RING:
                dve.wait_ge(a.sem, a.before(f"s{6 - self.S_RING + k}e", t))
            else:
                dve.wait_ge(a.sem, a.after(items[k - self.S_RING][0] + "e", t))
            dve.tensor_reduce(self.nm[:, k % self.S_RING:k % self.S_RING + 1], self.mx[:, k % self.S_RING, 0:len(pieces)], AX.X, ALU.max,
                              negate=True).then_inc(me.step(item + "x"), 1)

        def gated(branch, names, bank):
            recip, mul, out, add = names
            at = 12 + 6 * (3 - branch)
            gate = self.gates[:, bass.ds(t + 4 * s, 1), at:at + 6].rearrange("p a h -> p (a h)")
            dve.reciprocal(self.coef[:, branch, :], self.rsum[:, branch, :]).then_inc(me.step(recip), 1)
            dve.wait_ge(me.sem, me.after(recip, t))
            dve.tensor_tensor(self.coef[:, branch, :], self.coef[:, branch, :], gate, ALU.mult).then_inc(me.step(mul), 1)
            dve.wait_ge(me.sem, me.after(mul, t))
            dve.tensor_tensor(self.part[:, :, :], bank[:, 0:6 * DH].rearrange("p (h d) -> p h d", h=6),
                              self.coef[:, branch, :, None].to_broadcast([P, 6, DH]), ALU.mult).then_inc(me.step(out), 1)
            dve.wait_ge(me.sem, me.after(out, t))
            dve.tensor_tensor(self.acc[:, :, :], self.acc[:, :, :], self.part[:, :, :], ALU.add).then_inc(me.step(add), 1)

        def compressed_out():
            yield place("cv", None, 0, 0.9)
            gate = self.gates[:, bass.ds(t + 4 * s, 1), 12:18].rearrange("p a h -> p (a h)")
            dve.tensor_copy(self.cmx[:, :], gate).then_inc(me.step("ocoef"), 1)
            dve.wait_ge(me.sem, me.after("ocoef", t))
            dve.wait_ge(pe.sem, pe.after("co", t))
            dve.wait_ge(pe.sem, pe.before("ot", t))
            dve.tensor_tensor(self.acc[:, :, :], self.out_bank[0][:, 0:6 * DH].rearrange("p (h d) -> p h d", h=6),
                              self.cmx[:, :, None].to_broadcast([P, 6, DH]), ALU.mult).then_inc(me.step("oc"), 1)

        for k in range(12):
            yield from masked(k)
            if k == 1:
                dve.wait_ge(a.sem, a.after("ce", t))
                dve.reciprocal(self.coef[:, 0, :], self.rsum[:, 0, :]).then_inc(me.step("cr"), 1)
            if k == 3:
                yield place("q", 3, 1, 0.7)
                dve.wait_ge(p.sem, p.after("hs2", t))
                four = self.psum_heads[:, :, 0:P].rearrange("p g (b i) -> p g b i", i=4)
                dve.tensor_reduce(self.imp[:, :, :], four, AX.X, ALU.add).then_inc(me.step("imp1"), 1)
                dve.wait_ge(me.sem, me.after("imp1", t))
                fifth = self.psum_heads[:, :, 4:P + 4].rearrange("p g (b i) -> p g b i", i=4)[:, :, :, 0]
                dve.tensor_tensor(self.imp[:, :, :], self.imp[:, :, :], fifth, ALU.add).then_inc(me.step("imp2"), 1)
                both = [P, 2, N_BLK]
                elig = self.elig[:, bass.ds(t * -2 + (N_BLK - 2 - 8 * s), N_BLK)][:, None, :].to_broadcast(both)
                add = self.add[:, bass.ds(t * -2 + (N_BLK - 2 - 8 * s), N_BLK)][:, None, :].to_broadcast(both)
                dve.wait_ge(me.sem, me.after("imp2", t))
                dve.tensor_tensor(self.score[:, :, :], self.imp[:, :, :], elig, ALU.mult).then_inc(me.step("sc1"), 1)
                dve.wait_ge(me.sem, me.after("sc1", t))
                dve.tensor_tensor(self.score[:, :, :], self.score[:, :, :], add, ALU.add).then_inc(me.step("sc2"), 1)
                dve.wait_ge(me.sem, me.after("sc2", t))
                dve.tensor_scalar(self.score[:, :, 0:1], self.score[:, :, 0:1], SEL_BIG, None, ALU.add).then_inc(me.step("sc3"), 1)
                dve.wait_ge(me.sem, me.after("sc3", t))
                alone(dve, self.stood)
                for g in range(2):
                    last = dve.max(self.top[:, g, :], self.score[:, g, :])
                last.then_inc(me.step("top"), 1)
                dve.wait_ge(me.sem, me.after("top", t))
                alone(dve, self.stood)
                for g in range(2):
                    last = dve.match_replace(self.left[:, g, :], self.top[:, g, :], self.score[:, g, :], LOW)
                last.then_inc(me.step("left"), 1)
                dve.wait_ge(me.sem, me.after("left", t))
                dve.tensor_tensor(self.left[:, :, :], self.left[:, :, :], self.score[:, :, :],
                                  ALU.not_equal).then_inc(me.step("ne"), 1)
                dve.wait_ge(me.sem, me.after("ne", t))
                dve.tensor_tensor(self.left[:, :, :], self.left[:, :, :], elig, ALU.mult).then_inc(me.step("el"), 1)
                dve.wait_ge(me.sem, me.after("el", t))
                dve.wait_ge(p.sem, p.before("lm1", t))
                dve.tensor_scalar(self.selb[:, :, :], self.left[:, :, :], -NEG, NEG, ALU.mult, ALU.add).then_inc(me.step("selb"), 1)
            if k == 4:
                yield from compressed_out()
            if k == 8:
                yield place("q", 8, s, 0.6)
                dve.wait_ge(pe.sem, pe.after("w5v1", t))
                gated(1, ("rw", "cw", "ow", "aw"), self.out_bank[1])
        yield place("v", 11, s, 0.9)
        dve.wait_ge(pe.sem, pe.after(f"s5v{s}", t))
        gated(2, ("rs", "cs", "os", "as"), self.out_bank[0])


class SpanSteps(Steps):

    def __init__(self, sem, names, base):
        super().__init__(sem, names)
        self.base = base

    def after(self, name, t):
        return t * self.count + (self.base + self.names.index(name) + 1)

    def before(self, name, t):
        return t * self.count + (self.base - self.count + self.names.index(name) + 1)


def moved(part, by):
    for place in part:
        yield place + by


def weave(parts):
    heads = [[next(g) / size, n, g, size] for n, (g, size) in enumerate(parts)]
    while heads:
        head = min(heads, key=lambda h: h[:2])
        at = next(head[2], None)
        if at is None:
            heads.remove(head)
        else:
            assert at / head[3] >= head[0] - 1e-9, (at, head)
            head[0] = at / head[3]


def mix_tokens(nc, consts, prm, proj, rows, gates, kv, spare, mixed, ident):
    with ExitStack() as ctx:
        sc = Scope(nc, ctx, "mixer")
        banks = [sc.ps(f"bank{n}", [P, NB]) for n in range(8)]
        dn = DeltaNet(Scope(nc, ctx, "dn"), banks[0:2], consts, prm, proj, rows, gates, mixed, ident)
        nsa = Nsa(Scope(nc, ctx, "nsa"), banks[2:6], banks[6:8], consts, proj, gates, *kv, spare, mixed, ident)
        block = ctx.enter_context(nc.Block())

        def tile(eng, first, then, nsa_part, s, t, last=False):
            dn_tile = t + 4 * s
            parts = [(moved(then(eng, dn_tile), -dn.CUT), dn.PLACES), (nsa_part(eng, s, t), 1)]
            if not last:
                parts.append((moved(first(eng, dn_tile + 1), dn.PLACES - dn.CUT), dn.PLACES))
            weave(parts)

        def tiles(eng, first, then, nsa_part):
            for _ in first(eng, 0):
                pass
            for s in range(4):
                nsa.join(eng, s)
                with eng.Fori(0, 4 if s < 3 else 3) as t:
                    tile(eng, first, then, nsa_part, s, t)
            tile(eng, first, then, nsa_part, 3, 3, last=True)

        @block.sync
        def _(sp):

            def loads(s, t):
                nsa.sync(sp, s, t)
                dn.sync(sp, t + 4 * s)

            def sends(s, t):
                dn.send(sp, t + 4 * s)
                nsa.send(sp, s, t)

            loads(0, 0)
            nsa.load(sp)
            dn.start(sp, None)
            for s in range(4):
                with sp.Fori(0, 3) as t:
                    loads(s, t + 1)
                    sends(s, t)
                if s < 3:
                    loads(s + 1, 0)
                sends(s, 3)
            sp.wait_ge(dn.sent, 16 * NT)
            sp.wait_ge(nsa.sent, 16 * NT)

        @block.gpsimd
        def _(pool):
            dn.start(None, pool)
            nsa.start(pool)
            pool.wait_ge(dn.c_in, 16 * 7)
            pool.wait_ge(nsa.c_in, 16 * 6)
            tiles(pool, dn.gpsimd_first, dn.gpsimd_then, nsa.gpsimd)

        @block.scalar
        def _(act):
            act.preload_act_table_set(LOG_EXP)
            act.wait_ge(dn.ready, 6)
            tiles(act, dn.scalar_first, dn.scalar_then, nsa.scalar)

        @block.vector
        def _(dve):
            dve.wait_ge(dn.c_in, 16 * 7)
            dve.wait_ge(nsa.c_in, 16 * 6)
            tiles(dve, dn.vector_first, dn.vector_then, nsa.vector)

        @block.tensor
        def _(pe):
            pe.wait_ge(dn.c_in, 16 * 7)
            tiles(pe, dn.tensor_first, dn.tensor_then, nsa.tensor)


FP = FT // 2


def mix_out(nc, prm, x, mixed, x_mid, h_mid, ident):
    with ExitStack() as ctx:
        sc = Scope(nc, ctx, "out")
        w_raw = sc.sb("w_raw", [P, KT // 2, D_MODEL])
        w_hi, w_lo = sc.sb("w_hi", [P, KT, D_MODEL], F32R), sc.sb("w_lo", [P, KT, D_MODEL], F32R)
        m_raw, xt = sc.sb("m_raw", [P, 2, D_MODEL]), sc.sb("xt", [P, 2, D_MODEL])
        m_hi, m_lo = sc.sb("m_hi", [P, 2, D_MODEL], F32R), sc.sb("m_lo", [P, 2, D_MODEL], F32R)
        sq = sc.sb("sq", [P, D_MODEL])
        y, hn, turned = sc.sb("y", [P, 2, D_MODEL]), sc.sb("hn", [P, 2, D_MODEL]), sc.sb("turned", [P, 2, D_MODEL])
        w_post, w_pre = sc.sb("w_post", [P, D_MODEL]), sc.sb("w_pre", [P, D_MODEL])
        eps = sc.sb("eps", [P, 1])
        ssq, rstd = sc.sb("ssq", [P, 2, 4]), sc.sb("rstd", [P, 2, 2])
        acc = [[sc.ps(f"acc{b}{g}", [P, NB]) for g in range(2)] for b in range(2)]
        tp = [[sc.ps(f"tp{b}{g}", [P, NB]) for g in range(2)] for b in range(2)]
        w_in = [sc.sem(f"w_in{k}") for k in range(KT // 2)]
        m_in, x_in, y_sent, h_sent = ([sc.sem(f"{n}{b}") for b in range(2)] for n in ("m_in", "x_in", "y_sent", "h_sent"))
        (c_in, ready, whi, wlo, m_split_hi, m_split_lo, summed, squared, ssum, rooted, scaled, added, squared2, rooted2,
         normed, turn_done, taken) = (sc.sem(n) for n in (
             "c_in ready whi wlo m_split_hi m_split_lo summed squared ssum rooted scaled added squared2 rooted2 normed "
             "turn_done taken").split())
        block = ctx.enter_context(nc.Block())
        PAIRS = NT // 2
        m3 = "p (k t) -> p k t"

        @block.sync
        def _(sp):
            for b in range(2):
                sp.dma_start(m_raw[:, b, :].rearrange(m3, k=KT), mixed[:, :, b * P:(b + 1) * P]).then_inc(m_in[b], 16)
            for k in range(KT):
                if k >= KT // 2:
                    sp.wait_ge(wlo, k - KT // 2 + 1)
                sp.dma_start(w_raw[:, k % (KT // 2), :], prm["w_out"][k * P:(k + 1) * P, :]).then_inc(w_in[k % (KT // 2)], 16)
            sp.dma_start(w_post[:, :], prm["w_post_mix"].partition_broadcast(P)).then_inc(c_in, 16)
            sp.dma_start(w_pre[:, :], prm["w_pre_ffn"].partition_broadcast(P)).then_inc(c_in, 16)
            for b in range(2):
                sp.dma_start(xt[:, b, :], x[b * P:(b + 1) * P, :]).then_inc(x_in[b], 16)
            with sp.Fori(1, PAIRS) as i:
                for b in range(2):
                    sp.wait_ge(m_split_lo, i * 2 + (b - 1))
                    sp.dma_start(m_raw[:, b, :].rearrange(m3, k=KT),
                                 mixed[:, :, bass.ds(i * (2 * P) + b * P, P)]).then_inc(m_in[b], 16)
                for b in range(2):
                    sp.wait_ge(added, i * 4 + (2 * b - 2))
                    sp.dma_start(xt[:, b, :], x[bass.ds(i * (2 * P) + b * P, P), :]).then_inc(x_in[b], 16)

        @block.gpsimd
        def _(pool):
            pool.memset(eps[:, :], EPS).then_inc(ready, 1)
            for k in range(KT):
                pool.wait_ge(whi, k + 1)
                pool.tensor_tensor(w_lo[:, k, :], w_raw[:, k % (KT // 2), :], w_hi[:, k, :].bitcast(F32), ALU.subtract).then_inc(wlo, 1)
            with pool.Fori(0, PAIRS) as i:
                for b in range(2):
                    pool.wait_ge(added, i * 4 + (2 * b + 2))
                    pool.dma_start(x_mid[bass.ds(i * (2 * P) + b * P, P), :], y[:, b, :]).then_inc(y_sent[b], 16)
                    pool.wait_ge(taken, i * 4 + (2 * b + 2))
                    pool.dma_start(h_mid[:, :, bass.ds(i * (2 * P) + b * P, P)],
                                   turned[:, b, :].rearrange(m3, k=KT)).then_inc(h_sent[b], 16)
            for b in range(2):
                pool.wait_ge(y_sent[b], 16 * PAIRS)
                pool.wait_ge(h_sent[b], 16 * PAIRS)

        def rsqrt(eng, dst, src, sem, n):
            eng.activation(dst, src, ACT.Ln, bias=eps[:, :], scale=1.0 / D_MODEL).then_inc(sem, 1)
            eng.wait_ge(sem, n + 1)
            eng.activation(dst, dst, ACT.Exp, scale=-0.5).then_inc(sem, 1)

        @block.scalar
        def _(act):
            act.preload_act_table_set(LOG_EXP)

            def split(i, b, first=False):
                act.wait_ge(m_in[b], i * 16 + 16)
                if not first:
                    act.wait_ge(summed, i * 4 + (2 * b - 2))
                act.activation(m_hi[:, b, :], m_raw[:, b, :], ACT.Copy).then_inc(m_split_hi, 1)

            split(0, 0, True)
            split(0, 1, True)
            for k in range(KT):
                act.wait_ge(w_in[k % (KT // 2)], 16 * (k // (KT // 2) + 1))
                act.activation(w_hi[:, k, :], w_raw[:, k % (KT // 2), :], ACT.Copy).then_inc(whi, 1)
            act.wait_ge(ready, 1)

            def norms(i, b, last=False):
                for g in range(2):
                    act.wait_ge(summed, i * 4 + (2 * b + g + 1))
                    if g == 0:
                        act.wait_ge(squared2, i * 2 + b)
                    act.activation(sq[:, g * NB:(g + 1) * NB], acc[b][g][:, :], ACT.Square,
                                   accum_out=ssq[:, b, g:g + 1]).then_inc(squared, 1)
                act.wait_ge(ssum, i * 2 + b + 1)
                rsqrt(act, rstd[:, b, 0:1], ssq[:, b, 2:3], rooted, i * 4 + 2 * b)
                if not last:
                    split(i + 1, b)
                act.wait_ge(added, i * 4 + (2 * b + 2))
                act.activation(sq[:, :], y[:, b, :], ACT.Square, accum_out=ssq[:, b, 3:4]).then_inc(squared2, 1)
                act.wait_ge(squared2, i * 2 + b + 1)
                rsqrt(act, rstd[:, b, 1:2], ssq[:, b, 3:4], rooted2, i * 4 + 2 * b)

            def take(i, b):
                for g in range(2):
                    act.wait_ge(turn_done, i * 4 + (2 * b + g + 1))
                    if g == 0:
                        act.wait_ge(h_sent[b], i * 16)
                    act.activation(turned[:, b, g * NB:(g + 1) * NB], tp[b][g][:, :], ACT.Copy).then_inc(taken, 1)

            norms(0, 0)
            norms(0, 1)
            take(0, 0)
            with act.Fori(1, PAIRS - 1) as i:
                norms(i, 0)
                take(i - 1, 1)
                norms(i, 1)
                take(i, 0)
            norms(PAIRS - 1, 0, last=True)
            take(PAIRS - 2, 1)
            norms(PAIRS - 1, 1, last=True)
            take(PAIRS - 1, 0)
            take(PAIRS - 1, 1)

        @block.vector
        def _(dve):
            def split(i, b, first=False):
                dve.wait_ge(m_split_hi, i * 2 + b + 1)
                if not first:
                    dve.wait_ge(summed, i * 4 + (2 * b - 2))
                dve.tensor_tensor(m_lo[:, b, :], m_raw[:, b, :], m_hi[:, b, :].bitcast(F32), ALU.subtract).then_inc(m_split_lo, 1)

            def norms(i, b, last=False):
                dve.wait_ge(squared, i * 4 + (2 * b + 2))
                dve.tensor_tensor(ssq[:, b, 2:3], ssq[:, b, 0:1], ssq[:, b, 1:2], ALU.add).then_inc(ssum, 1)
                dve.wait_ge(rooted, i * 4 + (2 * b + 2))
                dve.wait_ge(y_sent[b], i * 16)
                for g in range(2):
                    at = slice(g * NB, (g + 1) * NB)
                    dve.scalar_tensor_tensor(y[:, b, at], acc[b][g][:, :], rstd[:, b, 0:1], w_post[:, at],
                                             ALU.mult, ALU.mult).then_inc(scaled, 1)
                dve.wait_ge(x_in[b], i * 16 + 16)
                for g in range(2):
                    at = slice(g * NB, (g + 1) * NB)
                    dve.wait_ge(scaled, i * 4 + (2 * b + g + 1))
                    dve.tensor_tensor(y[:, b, at], y[:, b, at], xt[:, b, at], ALU.add).then_inc(added, 1)
                if not last:
                    split(i + 1, b)
                dve.wait_ge(rooted2, i * 4 + (2 * b + 2))
                if not isinstance(i, int) or i:
                    dve.wait_ge(turn_done, i * 4 + (2 * b - 2))
                dve.scalar_tensor_tensor(hn[:, b, :], y[:, b, :], rstd[:, b, 1:2], w_pre[:, :],
                                         ALU.mult, ALU.mult).then_inc(normed, 1)

            split(0, 0, True)
            split(0, 1, True)
            dve.wait_ge(c_in, 32)
            for b in range(2):
                norms(0, b)
            with dve.Fori(1, PAIRS - 1) as i:
                for b in range(2):
                    norms(i, b)
            for b in range(2):
                norms(PAIRS - 1, b, last=True)

        @block.tensor
        def _(pe):
            def products(i, b, first=False):
                pe.wait_ge(m_split_lo, i * 2 + b + 1)
                if not first:
                    pe.wait_ge(scaled, i * 4 + (2 * b - 2))
                for g in range(2):
                    for k in range(KT):
                        if first and b == 0 and g == 0:
                            pe.wait_ge(wlo, k + 1)
                        at = slice(k * P, (k + 1) * P)
                        last = mm3(pe, acc[b][g][:, :], m_hi[:, b, at], m_lo[:, b, at], w_hi[:, k, g * NB:(g + 1) * NB],
                                   w_lo[:, k, g * NB:(g + 1) * NB], k == 0, k == KT - 1)
                    last.then_inc(summed, 1)

            def turns(i, b, first=False):
                pe.wait_ge(normed, i * 2 + b + 1)
                for g in range(2):
                    if not first:
                        pe.wait_ge(taken, i * 4 + (2 * b + g - 3))
                    for k in range(4):
                        last = pe.transpose(tp[b][g][:, k * P:(k + 1) * P], hn[:, b, (4 * g + k) * P:(4 * g + k + 1) * P],
                                            ident[:, :])
                    last.then_inc(turn_done, 1)

            products(0, 0, True)
            products(0, 1, True)
            products(1, 0)
            turns(0, 0, True)
            products(1, 1)
            turns(0, 1, True)
            with pe.Fori(2, PAIRS) as i:
                for b in range(2):
                    products(i, b)
                    turns(i - 1, b)
            for b in range(2):
                turns(PAIRS - 1, b)


def feed_forward(nc, prm, x_mid, h_mid, out):
    with ExitStack() as ctx:
        sc = Scope(nc, ctx, "ffn")
        gu_raw = sc.sb("gu_raw", [P, 2, KT * 2 * P])
        gu_hi, gu_lo = sc.sb("gu_hi", [P, 2, KT * 2 * P], F32R), sc.sb("gu_lo", [P, 2, KT * 2 * P], F32R)
        d_raw = sc.sb("d_raw", [P, 2, D_MODEL])
        d_hi, d_lo = sc.sb("d_hi", [P, 2, D_MODEL], F32R), sc.sb("d_lo", [P, 2, D_MODEL], F32R)
        h_raw = sc.sb("h_raw", [P, 2, 2, NB])
        h_hi, h_lo = sc.sb("h_hi", [P, KT, NB], F32R), sc.sb("h_lo", [P, KT, NB], F32R)
        sg = sc.sb("sg", [P, 2, NB])
        a = sc.sb("a", [P, FT, NB])
        a_hi, a_lo = sc.sb("a_hi", [P, 2, NB], F32R), sc.sb("a_lo", [P, 2, NB], F32R)
        f = sc.sb("f", [P, 4, D_MODEL])
        xm = sc.sb("xm", [P, 2, D_MODEL])
        sq = sc.sb("sq", [P, D_MODEL])
        w_post = sc.sb("w_post", [P, D_MODEL])
        eps, ssq, rstd = sc.sb("eps", [P, 1]), sc.sb("ssq", [P, 4]), sc.sb("rstd", [P, 4])
        bank = [sc.ps(f"bank{n}", [P, NB]) for n in range(8)]
        gu_in, d_in, h_in, x_in, out_sent = ([sc.sem(f"{n}{b}") for b in range(2)] for n in
                                             ("gu_in", "d_in", "h_in", "x_in", "out_sent"))
        (c_in, ready, gu_hi_d, gu_lo_d, h_hi_d, h_lo_d, gate_up, silu_d, a_d, d_hi_d, d_lo_d, a_hi_d, a_lo_d, down,
         drained, f_v, f_s, sq_d, rooted, scaled, added, stood) = (sc.sem(n) for n in (
             "c_in ready gu_hi_d gu_lo_d h_hi_d h_lo_d gate_up silu_d a_d d_hi_d d_lo_d a_hi_d a_lo_d down "
             "drained f_v f_s sq_d rooted scaled added stood").split())
        block = ctx.enter_context(nc.Block())
        blk = "p (k t) -> p k t"

        @block.sync
        def _(sp):
            sp.dma_start(w_post[:, :], prm["w_post_ffn"].partition_broadcast(P)).then_inc(c_in, 16)

            def load_h(i, n):
                if not (isinstance(i, int) and n < 2):
                    sp.wait_ge(h_lo_d, i * 4 + (n - 1))
                sp.dma_start(h_raw[:, n % 2, :, :], h_mid[:, 2 * n:2 * n + 2, bass.ds((i % TB) * NB, NB)]).then_inc(h_in[n % 2], 16)

            def load_gu(j, i, b, first=False):
                if not first:
                    sp.wait_ge(gu_lo_d, i * FT + j * 2 + (b - 1))
                sp.dma_start(gu_raw[:, b, :], prm["w_gate_up"][j * 2 + b]).then_inc(gu_in[b], 16)

            def load_d(j, i, b):
                sp.wait_ge(d_lo_d, i * FT + j * 2 + (b + 1))
                sp.dma_start(d_raw[:, b, :], prm["w_down"][j * 2 + b]).then_inc(d_in[b], 16)

            load_gu(0, 0, 0, True)
            for n in range(4):
                load_h(0, n)
                if n == 1:
                    load_gu(0, 0, 1, True)
            with sp.Fori(0, TB) as i:
                with sp.Fori(1, FP) as j:
                    for b in range(2):
                        load_gu(j, i, b)
                for b in range(2):
                    load_d(0, i, b)
                for n in range(4):
                    sp.wait_ge(h_lo_d, i * 4 + (n + 3))
                    sp.dma_start(h_raw[:, n % 2, :, :],
                                 h_mid[:, 2 * n:2 * n + 2, bass.ds((i + 1) % TB * NB, NB)]).then_inc(h_in[n % 2], 16)
                with sp.Fori(1, FP) as j:
                    for b in range(2):
                        load_d(j, i, b)
                for b in range(2):
                    sp.wait_ge(gu_lo_d, i * FT + (FT + b - 1))
                    sp.dma_start(gu_raw[:, b, :], prm["w_gate_up"][b]).then_inc(gu_in[b], 16)
                for n in range(4):
                    b = n % 2
                    sp.wait_ge(added, i * 4 + (n + 1))
                    sp.dma_start(xm[:, b, :], x_mid[bass.ds(i * NB + n * P, P), :]).then_inc(x_in[b], 16)
                for n in range(4):
                    sp.wait_ge(added, i * 4 + (n + 3))
                    sp.dma_start(out[bass.ds(i * NB + n * P, P), :], f[:, n, :]).then_inc(out_sent[0], 16)
            for b in range(2):
                sp.wait_ge(gu_in[b], 16 * (TB * FP + 1))
                sp.wait_ge(h_in[b], 16 * (2 * TB + 2))
            sp.wait_ge(out_sent[0], 16 * 4 * TB)

        @block.gpsimd
        def _(pool):
            pool.memset(eps[:, :], EPS).then_inc(ready, 1)
            pool.sem_inc(d_lo_d, 2)
            pool.sem_inc(added, 2)
            with pool.Fori(0, TB) as i:
                with pool.Fori(0, FP) as j:
                    for b in range(2):
                        pool.wait_ge(gu_hi_d, i * FT + j * 2 + (b + 1))
                        pool.tensor_tensor(gu_lo[:, b, :], gu_raw[:, b, :], gu_hi[:, b, :].bitcast(F32),
                                           ALU.subtract).then_inc(gu_lo_d, 1)
                with pool.Fori(0, FP) as j:
                    for b in range(2):
                        pool.wait_ge(d_hi_d, i * FT + j * 2 + (b + 1))
                        pool.tensor_tensor(d_lo[:, b, :], d_raw[:, b, :], d_hi[:, b, :].bitcast(F32),
                                           ALU.subtract).then_inc(d_lo_d, 1)

        @block.scalar
        def _(act):
            def split_h(i, n, first=False):
                act.wait_ge(h_in[n % 2], i * 32 + (n // 2 * 16 + 16))
                act.activation(h_hi[:, 2 * n:2 * n + 2, :], h_raw[:, n % 2, :, :], ACT.Copy).then_inc(h_hi_d, 1)

            def split_gu(i, j, b, first=False):
                act.wait_ge(gu_in[b], i * (16 * FP) + j * 16 + 16)
                if not first:
                    act.wait_ge(gate_up, i * FT + j * 2 + (b - 1))
                act.activation(gu_hi[:, b, :], gu_raw[:, b, :], ACT.Copy).then_inc(gu_hi_d, 1)

            def split_d(i, j, b, first=False):
                act.wait_ge(d_in[b], i * (16 * FP) + j * 16 + 16)
                act.wait_ge(down, i * FT + j * 2 + (b + 1))
                act.activation(d_hi[:, b, :], d_raw[:, b, :], ACT.Copy).then_inc(d_hi_d, 1)

            def silu(i, j, b):
                act.wait_ge(gate_up, i * FT + j * 2 + (b + 1))
                act.wait_ge(a_d, i * FT + j * 2 + (b + 1))
                act.activation(sg[:, b, :], bank[2 * b][:, :], ACT.Silu).then_inc(silu_d, 1)

            act.wait_ge(ready, 1)
            split_gu(0, 0, 0, True)
            for n in range(4):
                split_h(0, n, True)
            split_gu(0, 0, 1, True)
            with act.Fori(0, TB) as i:
                with act.Fori(0, FP - 1) as j:
                    for b in range(2):
                        silu(i, j, b)
                        split_gu(i, j + 1, b)
                for b in range(2):
                    split_d(i, 0, b)
                    silu(i, FP - 1, b)
                for n in range(4):
                    split_h(i + 1, n)
                with act.Fori(1, FP) as j:
                    for b in range(2):
                        split_d(i, j, b)
                for b in range(2):
                    split_gu(i + 1, 0, b)
                for n in range(4):
                    act.wait_ge(down, i * FT + (FT + 2))
                    act.activation(f[:, n, NB:2 * NB], bank[2 * n + 1][:, :], ACT.Copy).then_inc(f_s, 1)
                for n in range(4):
                    act.wait_ge(f_v, i * 4 + (n + 1))
                    act.wait_ge(f_s, i * 4 + (n + 1))
                    act.wait_ge(sq_d, i * 4 + n)
                    act.activation(sq[:, :], f[:, n, :], ACT.Square, accum_out=ssq[:, n:n + 1]).then_inc(sq_d, 1)
                act.preload_act_table_set(LOG_EXP)
                act.wait_ge(sq_d, i * 4 + 4)
                act.activation(rstd[:, :], ssq[:, :], ACT.Ln, bias=eps[:, :], scale=1.0 / D_MODEL).then_inc(rooted, 1)
                act.wait_ge(rooted, i * 2 + 1)
                act.activation(rstd[:, :], rstd[:, :], ACT.Exp, scale=-0.5).then_inc(rooted, 1)

        @block.vector
        def _(dve):
            def split_h(i, n):
                dve.wait_ge(h_hi_d, i * 4 + (n + 1))
                dve.tensor_tensor(h_lo[:, 2 * n:2 * n + 2, :], h_raw[:, n % 2, :, :], h_hi[:, 2 * n:2 * n + 2, :].bitcast(F32),
                                  ALU.subtract).then_inc(h_lo_d, 1)

            def split_a(i, j, b):
                act_tile = a[:, bass.ds(j * 2 + b, 1), :].rearrange("p a t -> p (a t)")
                dve.wait_ge(down, i * FT + j * 2 + (b + 1))
                dve.tensor_copy(a_hi[:, b, :], act_tile).then_inc(a_hi_d, 1)
                dve.wait_ge(a_hi_d, i * FT + j * 2 + (b + 1))
                dve.tensor_tensor(a_lo[:, b, :], act_tile, a_hi[:, b, :].bitcast(F32), ALU.subtract).then_inc(a_lo_d, 1)

            dve.wait_ge(c_in, 16)
            for n in range(4):
                split_h(0, n)
            with dve.Fori(0, TB) as i:
                with dve.Fori(0, FP) as j:
                    for b in range(2):
                        dve.wait_ge(silu_d, i * FT + j * 2 + (b + 1))
                        dve.tensor_tensor(a[:, bass.ds(j * 2 + b, 1), :].rearrange("p a t -> p (a t)"), sg[:, b, :],
                                          bank[2 * b + 1][:, :], ALU.mult).then_inc(a_d, 1)
                dve.wait_ge(a_d, i * FT + (FT + 2))
                for b in range(2):
                    split_a(i, 0, b)
                for n in range(4):
                    split_h(i + 1, n)
                with dve.Fori(1, FP) as j:
                    for b in range(2):
                        split_a(i, j, b)
                for n in range(4):
                    if n == 0:
                        dve.wait_ge(down, i * FT + (FT + 2))
                        dve.wait_ge(out_sent[0], i * 64)
                    dve.tensor_copy(f[:, n, 0:NB], bank[2 * n][:, :]).then_inc(f_v, 1)
                dve.wait_ge(rooted, i * 2 + 2)
                for n in range(4):
                    b = n % 2
                    dve.scalar_tensor_tensor(f[:, n, :], f[:, n, :], rstd[:, n:n + 1], w_post[:, :],
                                             ALU.mult, ALU.mult).then_inc(scaled, 1)
                    dve.wait_ge(scaled, i * 4 + (n + 1))
                    dve.wait_ge(x_in[b], i * 32 + (n // 2 * 16 + 16))
                    dve.tensor_tensor(f[:, n, :], f[:, n, :], xm[:, b, :], ALU.add).then_inc(added, 1)

        @block.tensor
        def _(pe):
            def hidden(i, j, b):
                pe.wait_ge(gu_lo_d, i * FT + j * 2 + (b + 1))
                pe.wait_ge(a_d, i * FT + j * 2 + (b + 1))
                for u in range(2):
                    for k in range(KT):
                        at = slice((2 * k + u) * P, (2 * k + u + 1) * P)
                        last = mm3(pe, bank[2 * b + u][:, :], gu_hi[:, b, at], gu_lo[:, b, at], h_hi[:, k, :], h_lo[:, k, :],
                                   k == 0, k == KT - 1)
                last.then_inc(gate_up, 1)

            def project(i, j, b, start, stop):
                pe.wait_ge(d_lo_d, i * FT + j * 2 + (b + 3))
                pe.wait_ge(a_lo_d, i * FT + j * 2 + (b + 1))
                for n in range(4):
                    for g in range(2):
                        at = slice(g * NB, (g + 1) * NB)
                        tok = slice(n * P, (n + 1) * P)
                        last = mm3(pe, bank[2 * n + g][:, :], a_hi[:, b, tok], a_lo[:, b, tok], d_hi[:, b, at],
                                   d_lo[:, b, at], start, stop)
                last.then_inc(down, 1)

            pe.sem_inc(a_d, 2)
            pe.sem_inc(down, 2)
            with pe.Fori(0, TB) as i:
                pe.wait_ge(h_lo_d, i * 4 + 4)
                pe.wait_ge(f_v, i * 4)
                pe.wait_ge(f_s, i * 4)
                alone(pe, stood)
                with pe.Fori(0, FP) as j:
                    for b in range(2):
                        hidden(i, j, b)
                pe.wait_ge(a_d, i * FT + (FT + 2))
                project(i, 0, 0, True, False)
                project(i, 0, 1, False, False)
                with pe.Fori(1, FP - 1) as j:
                    for b in range(2):
                        project(i, j, b, False, False)
                project(i, FP - 1, 0, False, False)
                project(i, FP - 1, 1, False, True)


def decoder_layer(nc, arrays, out):
    consts = {n[2:]: a for n, a in arrays.items() if n.startswith("c_")}
    prm = {n: a for n, a in arrays.items() if not n.startswith("c_")}
    dram = {n: nc.dram_tensor(n, shape, F32, kind="Internal").ap() for n, shape in (
        ("proj", (MT, P, SEQ)), ("rows", (2, NT * DN_HEADS * P)), ("mixed", (P, KT, SEQ)),
        ("x_mid", (SEQ, D_MODEL)), ("h_mid", (P, KT, SEQ)))}
    with ExitStack() as ctx:
        sc = Scope(nc, ctx, "layer")
        ident = sc.sb("ident", [P, P])
        build_constants(nc, ident)
        with ExitStack() as ctx_cf:
            cf_conv = Scope(nc, ctx_cf, "layer").sb("cf_conv", [P, 2, SEQ])
            with ExitStack() as ctx_h:
                sc_h = Scope(nc, ctx_h, "layer")
                h_hi, h_lo = sc_h.sb("h_hi", [P, KT, SEQ], F32R), sc_h.sb("h_lo", [P, KT, SEQ], F32R)
                norm_and_turn(nc, prm["x"], prm["w_pre_mix"], ident, h_hi, h_lo)
                project_in(nc, prm["w_in"], prm["cf_taps"], prm["cf_bias"], prm["dn_taps"], h_hi, h_lo, cf_conv, dram["proj"])
            with ExitStack() as ctx_kv:
                sc_kv = Scope(nc, ctx_kv, "layer")
                gates = sc_kv.sb("gates", [P, NT, 51])
                kv = [sc_kv.sb(n, shape) for n, shape in (
                    ("kc", [P, P]), ("vc", [P, P]), ("vs", [P, NT, P]), ("ks", [P, SEQ]), ("vw", [P, NT + WINDOW // P, P]),
                    ("kw", [P, WINDOW + SEQ]))]
                prepare(nc, consts, prm, cf_conv, dram["proj"], dram["mixed"], dram["rows"], gates, *kv)
                mix_tokens(nc, consts, prm, dram["proj"], dram["rows"], gates, kv, cf_conv, dram["mixed"], ident)
        mix_out(nc, prm, prm["x"], dram["mixed"], dram["x_mid"], dram["h_mid"], ident)
        feed_forward(nc, prm, dram["x_mid"], dram["h_mid"], out)


def layout(inputs):
    i = {n: np.asarray(a) for n, a in inputs.items()}
    one = {n: a[0] for n, a in i.items()}
    dn = DN_HEADS * DH
    heads = np.array(HX)
    o = 4 * dn
    beta, decay = o + heads, o + DN_HEADS + heads
    value = np.arange(CF_CH) + o + 2 * DN_HEADS
    gate = value + CF_CH
    o += 2 * DN_HEADS + 2 * CF_CH
    queries = (o + np.arange(2 * HPG * DH)).reshape(2, HPG, DH).transpose(1, 0, 2).reshape(-1)
    rest = np.arange(o + 2 * HPG * DH, one["w_in"].shape[1])
    kv, nsa_gates = rest[:6 * P], rest[6 * P:]
    first = np.concatenate([gate[:P], value[:P], gate[P:], value[P:], queries, kv, beta, decay, nsa_gates])
    last = np.concatenate([np.arange(3 * dn, 4 * dn), np.arange(3 * dn)])
    w_in = np.zeros((D_MODEL, MT * P), one["w_in"].dtype)
    w_in[:, :len(first)] = one["w_in"][:, first]
    w_in[:, T_DZ * P:] = one["w_in"][:, last]
    gate_up = np.stack([one["ffn_w_gate"], one["ffn_w_up"]]).reshape(2, KT, P, FT, P)
    arrays = {
        "x": one["x"],
        "w_pre_mix": one["norm_w"][0], "w_post_mix": one["norm_w"][1],
        "w_pre_ffn": one["norm_w"][2], "w_post_ffn": one["norm_w"][3],
        "w_in": w_in.reshape(KT, P, MT, P).transpose(2, 1, 0, 3).reshape(MT, P, D_MODEL),
        "cf_taps": one["cf_dw_w"].T.reshape(2, P, CF_TAPS).transpose(1, 0, 2),
        "cf_bias": one["cf_dw_b"].reshape(2, P).T,
        "dn_taps": one["dn_conv_w"].T.reshape(9, P, DN_TAPS).transpose(1, 0, 2),
        "cf_ln_w": one["cf_ln_w"].reshape(2, P).T, "cf_ln_b": one["cf_ln_b"].reshape(2, P).T,
        "dn_dt_bias": one["dn_dt_bias"][heads], "dn_a_log": one["dn_a_log"][heads],
        "dn_norm_w": np.tile(one["dn_norm_w"], 2)[:, None],
        "w_out": one["w_out"],
        "w_gate_up": gate_up.transpose(3, 2, 1, 0, 4).reshape(FT, P, 2 * D_MODEL),
        "w_down": one["ffn_w_down"].reshape(FT, P, D_MODEL),
    }
    for n in "kv":
        arrays[f"nsa_{n}_w1"] = one[f"nsa_{n}_w1"].reshape(CMP_LEN // 2, P, P).transpose(1, 0, 2)
        arrays[f"nsa_{n}_w2"] = one[f"nsa_{n}_w2"]
        arrays[f"nsa_{n}_pos"] = one[f"nsa_{n}_pos"].reshape(CMP_LEN // 2, P).T
    return arrays


def kernel(**inputs):
    import concourse.bacc as _bacc
    from concourse.bass_utils import run_bass_kernel_spmd as _run

    arrays = layout(inputs)
    arrays |= {"c_" + n: a for n, a in shape_constants().items()}
    arrays = {n: np.ascontiguousarray(a) for n, a in arrays.items()}
    nc = _bacc.Bacc("TRN2", target_bir_lowering=False, num_devices=1)
    ins = {n: nc.dram_tensor(f"in_{n}", a.shape, F32, kind="ExternalInput").ap() for n, a in arrays.items()}
    out = nc.dram_tensor("out", (SEQ, D_MODEL), F32, kind="ExternalOutput").ap()
    decoder_layer(nc, ins, out)
    r = _run(nc, [{f"in_{n}": a for n, a in arrays.items()}], core_ids=[0])
    return r.results[0]["out"].reshape(1, SEQ, D_MODEL)
```
